# Optimizing a Trainium2 kernel written in Bass

```python
import jax, jax.numpy as jnp
from jax import lax
import numpy as np

'''One trunk layer of a hybrid diffusion / flow-matching backbone, run for two request groups with shared weights.

Each layer: adaLN-modulated RMSNorm -> parallel head groups [Conformer convolution module | bidirectional RWKV-7 time mixing]
from ONE combined input projection, concatenated into ONE output projection, gated residual -> adaLN-modulated RMSNorm ->
expert-choice SwiGLU mixture of experts, gated residual. One final RMSNorm.

Inputs:
  x_prompt  (BATCH, SEQ, D_MODEL)        context tokens of new requests (group i), modulated by c_ctx
  x_sample  (DEC_BATCH, DEC_SEQ, D_MODEL) noisy latent tokens on a GRID_W-wide grid (group ii), modulated by c
  state_wkv (DEC_BATCH, DEPTH, 2, H, N, N) cached final context scan states (dir 0 = forward, dir 1 = backward)
  c         (DEC_BATCH, D_MODEL)          conditioning vectors of group ii
  c_ctx     (D_MODEL,)                    learned constant conditioning vector for context tokens
  followed by the layer weights (leading dim DEPTH) and final_norm_g (D_MODEL,).
Returns the tuple (y_prompt, y_sample, new_state_wkv):
  y_prompt      (BATCH, SEQ, D_MODEL)
  y_sample      (DEC_BATCH, DEC_SEQ, D_MODEL)
  new_state_wkv (BATCH, DEPTH, 2, H, N, N)   final context scan states of group i, same layout as state_wkv
'''

D_MODEL = 1024
BATCH = 1
SEQ = 256
DEPTH = 1
DEC_BATCH = 1
DEC_SEQ = 1024
PAST_LEN = 512

GRID_W = 64
D_MIX = D_MODEL
CONV_W = D_MIX // 2
CONV_K = 31
CONV_PAD = (CONV_K - 1) // 2
RWKV_W = D_MIX - CONV_W
HEAD_SIZE = 64
N_RWKV_HEADS = RWKV_W // HEAD_SIZE
DECAY_LORA = 64
AAA_LORA = 64
GATE_LORA = 128
N_DIR = 2
N_EXPERTS = 16
EC_CAPACITY = 2
D_FF = 2816
D_IN = 2 * CONV_W + 3 * RWKV_W + N_DIR * DECAY_LORA + N_DIR * AAA_LORA + GATE_LORA
SPLIT_IDX = (CONV_W, 2 * CONV_W, 2 * CONV_W + RWKV_W, 2 * CONV_W + 2 * RWKV_W, 2 * CONV_W + 3 * RWKV_W,
             2 * CONV_W + 3 * RWKV_W + N_DIR * DECAY_LORA,
             2 * CONV_W + 3 * RWKV_W + N_DIR * (DECAY_LORA + AAA_LORA))
RMS_EPS = 1e-6
LN_EPS = 1e-5
GN_EPS = 64e-5

kernel_name = 'hymba_conformer_rwkv7_ec_diffusion_step'

def _rmsnorm(x, g):
    xf = x.astype(jnp.float32)
    return (xf * lax.rsqrt(jnp.mean(xf * xf, -1, keepdims=True) + RMS_EPS) * g).astype(x.dtype)

def _heads(t):
    return t.reshape(*t.shape[:-1], N_RWKV_HEADS, HEAD_SIZE)

def _time_major(t):
    t = jnp.transpose(t, (1, 2, 0, 3, 4))
    return jnp.stack([t[:, 0], t[::-1, 1]], axis=1)

def _conv_group(u_val, u_gate, grid, dw, db, ln_g, ln_b):
    u = u_val * jax.nn.sigmoid(u_gate)
    B, T, C = u.shape
    seq = u.reshape(B * (T // GRID_W), GRID_W, C) if grid else u
    out = lax.conv_general_dilated(seq, dw[:, None, :].astype(u.dtype), (1,), [(CONV_PAD, CONV_PAD)],
                                   dimension_numbers=('NWC', 'WIO', 'NWC'), feature_group_count=C)
    out = out.reshape(B, T, C).astype(jnp.float32) + db
    mu = jnp.mean(out, -1, keepdims=True)
    var = jnp.mean(jnp.square(out - mu), -1, keepdims=True)
    out = (out - mu) * lax.rsqrt(var + LN_EPS) * ln_g + ln_b
    return jax.nn.silu(out).astype(u.dtype)

def _wkv_step(S, inp):
    r_t, kk_t, w_t, b_t, k_t, v_t = inp
    sa = jnp.einsum('dbhvk,dbhk->dbhv', S, kk_t)
    S = S * w_t[..., None, :] - sa[..., :, None] * b_t[..., None, :] + v_t[..., :, None] * k_t[..., None, :]
    return S, jnp.einsum('dbhvk,dbhk->dbhv', S, r_t)

def _rwkv_group(r, k, v, xw, xa, xg, S0, w0, w_up, a0, a_up, g_up, k_k, k_a, r_k, gn_g, gn_b):
    f32 = jnp.float32
    B, T, _ = r.shape
    r, k, v, xw, xa, xg = (t.astype(f32) for t in (r, k, v, xw, xa, xg))
    xw = xw.reshape(B, T, N_DIR, DECAY_LORA)
    xa = xa.reshape(B, T, N_DIR, AAA_LORA)
    wl = w0 + jnp.einsum('btdl,dlc->btdc', jnp.tanh(xw), w_up)
    decay = jnp.exp(-jnp.exp(-jax.nn.softplus(-wl) - 0.5))
    a = jax.nn.sigmoid(a0 + jnp.einsum('btdl,dlc->btdc', xa, a_up))
    g = jax.nn.sigmoid(xg) @ g_up
    kk = _heads(k * k_k)
    kk = kk * lax.rsqrt(jnp.maximum(jnp.sum(kk * kk, -1, keepdims=True), 1e-24))
    a_h = _heads(a)
    k_dir = _heads(k[:, :, None, :] * (1.0 + (a - 1.0) * k_a))
    r_h, v_h = _heads(r), _heads(v)
    shp = a_h.shape
    kk2 = jnp.broadcast_to(kk[:, :, None], shp)
    xs = (_time_major(jnp.broadcast_to(r_h[:, :, None], shp)), _time_major(kk2), _time_major(_heads(decay)),
          _time_major(kk2 * a_h), _time_major(k_dir), _time_major(jnp.broadcast_to(v_h[:, :, None], shp)))
    S_fin, ys = lax.scan(_wkv_step, S0.astype(f32), xs)
    y = jnp.transpose(ys[:, 0] + ys[::-1, 1], (1, 0, 2, 3))
    mu = jnp.mean(y, -1, keepdims=True)
    var = jnp.mean(jnp.square(y - mu), -1, keepdims=True)
    yn = (y - mu) * lax.rsqrt(var + GN_EPS) * gn_g.reshape(N_RWKV_HEADS, HEAD_SIZE) + gn_b.reshape(N_RWKV_HEADS, HEAD_SIZE)
    bonus = jnp.einsum('bthn,btdhn,hn->bth', r_h, k_dir, r_k)[..., None] * v_h
    out = (yn + bonus).reshape(B, T, RWKV_W) * g
    return out, S_fin

def _expert_choice_ffn(h, router, w1, w3, w2):
    B, T, D = h.shape
    x = h.reshape(B * T, D)
    n = B * T
    cap = min(n, max(1, EC_CAPACITY * n // N_EXPERTS))
    aff = jax.nn.softmax((x @ router).astype(jnp.float32), axis=-1)
    gate, idx = lax.top_k(aff.T, cap)
    xe = x[idx]
    hid = jax.nn.silu(jnp.einsum('ecd,edf->ecf', xe, w1)) * jnp.einsum('ecd,edf->ecf', xe, w3)
    ye = jnp.einsum('ecf,efd->ecd', hid, w2) * gate[..., None].astype(hid.dtype)
    y = jnp.zeros((n, D), ye.dtype).at[idx.reshape(-1)].add(ye.reshape(-1, D))
    return y.reshape(B, T, D).astype(h.dtype)

def _layer(x, cond, S0, grid, norm1_g, norm2_g, w_mod, b_mod, w_in, conv_dw, conv_b, conv_ln_g, conv_ln_b,
           rwkv_w0, rwkv_w_up, rwkv_a0, rwkv_a_up, rwkv_g_up, rwkv_k_k, rwkv_k_a, rwkv_r_k, rwkv_gn_g, rwkv_gn_b,
           w_out, router, exp_w1, exp_w3, exp_w2):
    mod = (jax.nn.silu(cond) @ w_mod + b_mod)[:, None, :].astype(x.dtype)
    sh1, sc1, g1, sh2, sc2, g2 = jnp.split(mod, 6, axis=-1)
    h = _rmsnorm(x, norm1_g) * (1.0 + sc1) + sh1
    proj = h @ w_in
    u_val, u_gate, r, k, v, xw, xa, xg = jnp.split(proj, SPLIT_IDX, axis=-1)
    conv_out = _conv_group(u_val, u_gate, grid, conv_dw, conv_b, conv_ln_g, conv_ln_b)
    rw_out, S_fin = _rwkv_group(r, k, v, xw, xa, xg, S0, rwkv_w0, rwkv_w_up, rwkv_a0, rwkv_a_up, rwkv_g_up,
                                rwkv_k_k, rwkv_k_a, rwkv_r_k, rwkv_gn_g, rwkv_gn_b)
    mix = jnp.concatenate([conv_out, rw_out.astype(conv_out.dtype)], axis=-1) @ w_out
    x = x + g1 * mix.astype(x.dtype)
    h = _rmsnorm(x, norm2_g) * (1.0 + sc2) + sh2
    x = x + g2 * _expert_choice_ffn(h, router, exp_w1, exp_w3, exp_w2)
    return x, S_fin

def setup_inputs(seed: int = 0) -> dict:
    key = jax.random.key(seed)
    ks = jax.random.split(key, 32)
    f32 = jnp.float32

    def nrm(k, shape, s):
        return jax.random.normal(k, shape, f32) * s

    L, D, E, F, H, N = DEPTH, D_MODEL, N_EXPERTS, D_FF, N_RWKV_HEADS, HEAD_SIZE
    return {
        'x_prompt': nrm(ks[0], (BATCH, SEQ, D), 1.0),
        'x_sample': nrm(ks[1], (DEC_BATCH, DEC_SEQ, D), 1.0),
        'state_wkv': nrm(ks[2], (DEC_BATCH, DEPTH, N_DIR, H, N, N), 0.5),
        'c': nrm(ks[3], (DEC_BATCH, D), 1.0),
        'c_ctx': nrm(ks[4], (D,), 1.0),
        'norm1_g': 1.0 + nrm(ks[5], (L, D), 0.02),
        'norm2_g': 1.0 + nrm(ks[6], (L, D), 0.02),
        'w_mod': nrm(ks[7], (L, D, 6 * D), 0.3 * D ** -0.5),
        'b_mod': nrm(ks[8], (L, 6 * D), 0.02),
        'w_in': nrm(ks[9], (L, D, D_IN), D ** -0.5),
        'conv_dw': nrm(ks[10], (L, CONV_K, CONV_W), CONV_K ** -0.5),
        'conv_b': nrm(ks[11], (L, CONV_W), 0.02),
        'conv_ln_g': 1.0 + nrm(ks[12], (L, CONV_W), 0.02),
        'conv_ln_b': nrm(ks[13], (L, CONV_W), 0.02),
        'rwkv_w0': jax.random.uniform(ks[14], (L, N_DIR, RWKV_W), f32, -2.5, 0.5),
        'rwkv_w_up': nrm(ks[15], (L, N_DIR, DECAY_LORA, RWKV_W), 0.1 * DECAY_LORA ** -0.5),
        'rwkv_a0': nrm(ks[16], (L, N_DIR, RWKV_W), 0.5),
        'rwkv_a_up': nrm(ks[17], (L, N_DIR, AAA_LORA, RWKV_W), 0.3 * AAA_LORA ** -0.5),
        'rwkv_g_up': nrm(ks[18], (L, GATE_LORA, RWKV_W), GATE_LORA ** -0.5),
        'rwkv_k_k': 0.85 + nrm(ks[19], (L, RWKV_W), 0.05),
        'rwkv_k_a': 1.0 + nrm(ks[20], (L, RWKV_W), 0.05),
        'rwkv_r_k': nrm(ks[21], (L, H, N), 0.1),
        'rwkv_gn_g': 1.0 + nrm(ks[22], (L, RWKV_W), 0.02),
        'rwkv_gn_b': nrm(ks[23], (L, RWKV_W), 0.02),
        'w_out': nrm(ks[24], (L, D_MIX, D), D_MIX ** -0.5),
        'router': nrm(ks[25], (L, D, E), D ** -0.5),
        'exp_w1': nrm(ks[26], (L, E, D, F), D ** -0.5),
        'exp_w3': nrm(ks[27], (L, E, D, F), D ** -0.5),
        'exp_w2': nrm(ks[28], (L, E, F, D), F ** -0.5),
        'final_norm_g': 1.0 + nrm(ks[29], (D,), 0.02),
    }

def reference(x_prompt, x_sample, state_wkv, c, c_ctx, norm1_g, norm2_g, w_mod, b_mod, w_in, conv_dw, conv_b,
              conv_ln_g, conv_ln_b, rwkv_w0, rwkv_w_up, rwkv_a0, rwkv_a_up, rwkv_g_up, rwkv_k_k, rwkv_k_a, rwkv_r_k,
              rwkv_gn_g, rwkv_gn_b, w_out, router, exp_w1, exp_w3, exp_w2, final_norm_g):
    stacked = (norm1_g, norm2_g, w_mod, b_mod, w_in, conv_dw, conv_b, conv_ln_g, conv_ln_b, rwkv_w0, rwkv_w_up,
               rwkv_a0, rwkv_a_up, rwkv_g_up, rwkv_k_k, rwkv_k_a, rwkv_r_k, rwkv_gn_g, rwkv_gn_b, w_out, router,
               exp_w1, exp_w3, exp_w2)
    xp = x_prompt
    bp = xp.shape[0]
    states = []
    for l in range(DEPTH):
        lp = tuple(w[l] for w in stacked)
        S0 = jnp.zeros((N_DIR, bp, N_RWKV_HEADS, HEAD_SIZE, HEAD_SIZE), jnp.float32)
        xp, S_fin = _layer(xp, c_ctx[None, :], S0, False, *lp)
        states.append(jnp.transpose(S_fin, (1, 0, 2, 3, 4)))
    new_state_wkv = jnp.stack(states, axis=1)
    xs = x_sample
    for l in range(DEPTH):
        lp = tuple(w[l] for w in stacked)
        S0 = jnp.transpose(state_wkv[:, l], (1, 0, 2, 3, 4))
        xs, _ = _layer(xs, c, S0, True, *lp)
    y_prompt = _rmsnorm(xp, final_norm_g)
    y_sample = _rmsnorm(xs, final_norm_g)
    return (y_prompt, y_sample, new_state_wkv)


_drawn_inputs = setup_inputs


def setup_inputs(seed=0):
    import zlib

    import numpy as np

    out = dict(_drawn_inputs(seed))
    spreads = {}
    factors = {'state_wkv': 8.0,
     'norm2_g': 8.0,
     'conv_b': 8.0,
     'conv_ln_g': 8.0,
     'conv_ln_b': 8.0,
     'rwkv_w_up': 4.783,
     'rwkv_k_k': 4.374,
     'rwkv_gn_g': 8.0,
     'rwkv_gn_b': 8.0,
     'final_norm_g': 2.932}
    for name, (base, spread) in spreads.items():
        noise = np.random.default_rng([zlib.crc32(name.encode()), seed]).standard_normal(out[name].shape)
        drawn = base * np.exp(spread * noise) if base else spread * noise
        out[name] = __import__('jax').numpy.asarray(drawn.astype(out[name].dtype))
    for name, factor in factors.items():
        out[name] = (out[name] * factor).astype(out[name].dtype)
    return out
```

```python
import concourse.bass as bass
from concourse import mybir
from contextlib import ExitStack
import numpy as np

P = 128
D = 1024
KC = D // P
TS, TP = 1024, 256
T = TS + TP
NT = T // P
NTS = TS // P
CW = 512
NP_ = CW // P
HS = 64
NH = CW // HS
KW = 31
PAD = (KW - 1) // 2
GRID = 64
WIN = GRID + 2 * PAD
NWIN = T // GRID
C = 64
NCH = T // C
NCS = TS // C
NCP = TP // C
E = 16
FF = 2816
NFC = FF // P
CAP_S = 2 * TS // E
CAP_P = 2 * TP // E
CAP = CAP_S + CAP_P
PB = 32
LEVELS = (2, 4, 8, 16, 32)
C0 = float(np.exp(-0.5))
RMS_EPS, LN_EPS, GN_EPS = 1e-6, 1e-5, 64e-5
STEP_CHUNKS = (4, 4, 4, 4, 3, 3)
SLOTS = 3
COLS3 = ((0, 512), (512, 512), (1024, 256))


def constant_table():
    t = {}
    i = np.arange(P)
    ident = np.eye(P, dtype=np.float32)
    t["ident"] = ident
    same = (i[:, None] // HS == i[None] // HS)
    t["blockones"] = same.astype(np.float32)
    t["fold"] = (i[:, None] % HS == np.arange(HS)[None]).astype(np.float32)
    t["lnmean"] = np.full((P, P), 1.0 / CW, np.float32)
    r, c = i[:, None] % C, i[None] % C
    for d in (0, 1):
        before = (r < c) if d == 0 else (r > c)
        t[f"strict{d}"] = (same & before).astype(np.float32)
        t[f"incl{d}"] = (same & (before | (r == c))).astype(np.float32)
        t[f"nincl{d}"] = -t[f"incl{d}"]
        after = (r > c) if d == 0 else (r < c)
        for b in (1,) + LEVELS:
            off = (r // (2 * b) == c // (2 * b)) & (r // b != c // b)
            m = ident - (same & after & off)
            t[f"lev{d}_{b}"] = m.astype(np.float32)
            col = np.arange(HS)[None]
            rr = i[:, None] % C
            aft = (rr > col) if d == 0 else (rr < col)
            of = (rr // (2 * b) == col // (2 * b)) & (rr // b != col // b)
            mc = (rr == col).astype(np.float32) - (aft & of)
            t[f"levc{d}_{b}"] = mc.astype(np.float32)
            if b == 1:
                t[f"first{d}"] = m.T.astype(np.float32)
                t[f"firstc{d}"] = (-(aft & of).astype(np.float32))
                del t[f"lev{d}_1"], t[f"levc{d}_1"]
    reset = np.ones((P, NP_ * C), np.float32)
    reset[:, ::C] = 0
    t["reset"] = reset
    return t


def table_columns(t):
    at, cols = 0, {}
    for n, a in t.items():
        cols[n] = (at, a.shape[1])
        at += a.shape[1]
    return cols, at


VECTORS = (("n1", 8), ("n2", 8), ("bmod", 48), ("dw", NP_ * KW), ("db", 4), ("lng", 4), ("lnb", 4),
           ("bias_wa", 16), ("k_k", 4), ("k_a", 4), ("r_k", 4), ("gng", 4), ("gnb", 4), ("cond", 16))


class Chain:

    def __init__(self, eng, sem):
        self.eng, self.sem, self.n, self.at, self.last = eng, sem, 0, 0, None

    def link(self, ins):
        self.n += 1
        ins.then_inc(self.sem, 1)
        self.eng.wait_ge(self.sem, self.at + self.n)
        self.last = ins
        return ins


class Shared:
    pass


class Arena:

    def __init__(self, main, size, at=0):
        self.main, self.size, self.at = main, size, at

    def get(self, *shape, rows=P):
        n = int(np.prod(shape))
        v = self.main[0:rows, self.at:self.at + n]
        self.at += n
        assert self.at <= self.size, (self.at, self.size)
        if len(shape) == 2:
            v = v.rearrange("p (a b) -> p a b", b=shape[1])
        if len(shape) == 3:
            v = v.rearrange("p (a b c) -> p a b c", b=shape[1], c=shape[2])
        return v


def hold(pool, turns, *waits):
    for sm, value in waits:
        pool.wait_ge(sm, value)
        pool.sem_inc(turns, 1)


F32, I32, U32 = mybir.dt.float32, mybir.dt.int32, mybir.dt.uint32
ALU, ACT, AX = mybir.AluOpType, mybir.ActivationFunctionType, mybir.AxisListType
ds = bass.ds


def build(nc, a, phases=5):
    with ExitStack() as ctx:
        s = Shared()
        s.a = a

        def sem(name):
            return ctx.enter_context(nc.semaphore(name))

        def dram(name, shape):
            return nc.dram_tensor(name, shape, F32, kind="Internal").ap()

        def small(name, shape, dt=F32):
            return ctx.enter_context(nc.sbuf_tensor(name, shape, dt))

        s.sem, s.small = sem, small
        s.g1_d = dram("gate1_rows", (2, D))
        s.conv_d = dram("conv_out", (P, NP_ * T))
        s.y_d = dram("wkv_out", (2, NCH, P, NP_ * HS))
        s.kd_d = dram("keys_out", (2, P, NP_, T))
        s.xn_d = dram("normed_rows", (T, D))
        s.acc_d = dram("residual_rows", (T, D))

        cols, n_const = table_columns(constant_table())
        s.consts = small("consts", [P, n_const])
        s.K = {n: s.consts[:, o:o + w] for n, (o, w) in cols.items()}
        s.vecs = small("vecs", [P, sum(w for _, w in VECTORS)])
        s.V, at = {}, 0
        for n, w in VECTORS:
            s.V[n] = s.vecs[:, at:at + w]
            at += w
        s.condT = small("condT", [P, KC, 2])
        s.modT = small("modT", [P, 48, 2])
        s.A1, s.A2 = small("A1", [P, KC, 2]), small("A2", [P, KC, 2])
        s.lora_up = small("lora_up", [P, 4, CW])
        s.g_up = small("g_up", [P, CW])
        s.st = small("row_stats", [P, 12])
        s.taps = small("taps", [P, KW])
        s.B1, s.B2, s.G2 = s.modT[:, 0:8, :], s.modT[:, 24:32, :], s.modT[:, 40:48, :]
        s.gateT, s.idxF = s.lora_up[:, 0, 0:64], s.lora_up[:, 0, 64:128]
        s.idxT = s.lora_up[:, 0, 128:192].bitcast(I32)
        s.w13_in = [sem(f"w1_w3_in{i}") for i in range(SLOTS)]
        s.w2_in = [sem(f"w2_in{i}") for i in range(SLOTS)]
        n_main = (nc.sbuf_usable_end - nc.sbuf_base) // 4 - 64
        s.M = small("main", [P, n_main])
        s.n_main = n_main
        s.PS = ctx.enter_context(nc.psum_tensor("PS", [P, 8 * 512], F32))
        s.ar = Arena(s.M, n_main)
        s.rkv = s.ar.get(3 * NP_, T)
        s.rT, s.kT, s.vT = s.rkv[:, 0:4, :], s.rkv[:, 4:8, :], s.rkv[:, 8:12, :]
        s.loraT = s.ar.get(3, T)
        s.mark = s.ar.at
        for phase in (phase_project, phase_wkv, phase_mix, phase_experts, phase_final)[:phases]:
            own = []

            def phase_sem(name, own=own):
                own.append(nc.alloc_semaphore(name))
                return own[-1]

            s.sem = phase_sem
            phase(nc, s)
            nc.clear_and_free_semaphores(own)
            nc.all_engine_barrier()


def phase_project(nc, s):
    a, K, V, PS, M, sem = s.a, s.K, s.V, s.PS, s.M, s.sem
    ar = Arena(M, s.n_main, s.mark)
    hT = ar.get(KC, T)
    late = [M[:, s.mark + i * 4096:s.mark + (i + 1) * 4096].rearrange("p (k n) -> p k n", n=512)
            for i in range(2)]
    mark = ar.at
    u = ar.get(NP_, NWIN * WIN)
    sq = M[:, mark:mark + NP_ * T].rearrange("p (k n) -> p k n", n=T)
    lrs = M[:, mark + NP_ * T:mark + NP_ * T + T]
    mark = ar.at
    cv = ar.get(NP_, T)
    xt = [M[:, mark + i * D:mark + (i + 1) * D] for i in (0, 1)]
    xn = [M[:, mark + i * D:mark + (i + 1) * D] for i in (2, 3)]
    junk = [M[:, mark + 4 * D:mark + 5 * D], s.loraT[:, 0, 0:D]]
    ws = [ar.get(KC, P) for _ in range(4)]
    slab = [M[:, i * 4096:(i + 1) * 4096].rearrange("p (k n) -> p k n", n=512) for i in range(2)]
    ge = [s.rkv[:, i, :] for i in (0, 1)]
    modps = PS[:, 6 * 512:6 * 512 + 96].rearrange("p (m j) -> p m j", j=2)
    trp = [PS[:, 0:1024], PS[:, 1024:2048]]
    pset = [PS[:, 0:T], PS[:, 3 * 512:3 * 512 + T]]
    w_mod = a["w_mod"].rearrange("(k p) n -> p k n", p=P)
    w_in = a["w_in"].rearrange("(k p) n -> p k n", p=P)
    ssq = [s.st[:, i:i + 1] for i in (0, 1)]
    ms = [s.st[:, i:i + 1] for i in (2, 3)]
    root = [s.st[:, i:i + 1] for i in (4, 5)]
    rstd = [s.st[:, i:i + 1] for i in (8, 9)]
    BODY, FULL = 4, 5
    NPC = 23

    tables, ups, zero = sem("tables_loaded"), sem("up_weights_loaded"), sem("zeros_written")
    x_in = [sem(f"x_in{i}") for i in range(2)]
    mod_in = [sem(f"w_mod_in{i}") for i in range(2)]
    late_in = [sem(f"w_mod_late_in{i}") for i in range(2)]
    mod_used, late_used = sem("w_mod_used"), sem("w_mod_late_used")
    cond_sig, cond_ready, mod_ready = sem("cond_sigmoid"), sem("cond_ready"), sem("mod_ready")
    sq_done, ms_done, rs_done = sem("row_squares"), sem("row_mean_square"), sem("row_root")
    rr_done = sem("row_rstd")
    xn_done, tr_done = sem("xn_ready"), sem("x_transposed")
    h_act, h_dve = sem("h_by_act"), sem("h_by_dve")
    win = [sem(f"w_in_in{i}") for i in range(4)]
    pr_done = sem("projected")
    free = [sem(f"psum_set_free{i}") for i in range(2)]
    gate_sig, u_done = sem("gate_sigmoid"), sem("u_ready")
    g1_ready, g1_out = sem("g1_ready"), sem("g1_written")
    dvo, conv_own = sem("dve_own_a"), sem("taps_staged")
    conv_done, mean_ps, cen = sem("conv_summed"), sem("ln_mean_psum"), sem("ln_centered")
    csq, var_ps, var_done, lrs_done = (sem("ln_squared"), sem("ln_var_psum"), sem("ln_var"),
                                       sem("ln_rstd"))
    scaled, aff_done, sil_sig, cout = (sem("ln_scaled"), sem("ln_affine"), sem("silu_sigmoid"),
                                       sem("conv_out_ready"))
    conv_spill = sem("conv_written")

    with nc.Block() as block:

        @block.sync
        def _(sp):
            sp.dma_start(s.vecs[:, :], a["vectors"]).then_inc(tables, 16)
            sp.dma_start(s.consts[:, :], a["table"]).then_inc(tables, 16)
            for i in range(2):
                sp.dma_start(slab[i], w_mod[:, :, i * 512:(i + 1) * 512]).then_inc(mod_in[i], 16)
            for i in range(2):
                sp.dma_start(xt[i], a["x"][i * P:(i + 1) * P, :]).then_inc(x_in[i], 16)
            for i in range(2):
                sp.wait_ge(mod_used, i + 1)
                sp.dma_start(slab[i], w_mod[:, :, (i + 2) * 512:(i + 3) * 512]).then_inc(mod_in[i], 16)
            sp.wait_ge(zero, 1)
            for d in (0, 1):
                sp.dma_start(s.lora_up[d * HS:(d + 1) * HS, d, :], a["w_up"][d]).then_inc(ups, 16)
                sp.dma_start(s.lora_up[d * HS:(d + 1) * HS, 2 + d, :], a["a_up"][d]).then_inc(ups, 16)
            sp.dma_start(s.g_up[:, :], a["g_up"]).then_inc(ups, 16)
            with sp.Fori(1, NT // 2) as j:
                for i in range(2):
                    sp.wait_ge(xn_done, j * 2 + (i - 1))
                    sp.dma_start(xt[i], a["x"][ds(j * (2 * P) + i * P, P), :]).then_inc(x_in[i], 16)
            for n, ch in enumerate((4, 0, 5, 1, 6, 2, 7, 3)):
                if n >= 4:
                    sp.wait_ge(pr_done, n - 3)
                sp.dma_start(ws[n % 4], w_in[:, :, ch * P:(ch + 1) * P]).then_inc(win[n % 4], 16)
            with sp.Fori(2, FULL) as j:
                for i in range(4):
                    sp.wait_ge(pr_done, j * 4 + (i - 3))
                    sp.dma_start(ws[i], w_in[:, :, ds(j * 512 + i * P, P)]).then_inc(win[i], 16)
            for n in range(4 * FULL, NPC):
                sp.wait_ge(pr_done, n - 3)
                sp.dma_start(ws[n % 4], w_in[:, :, n * P:(n + 1) * P]).then_inc(win[n % 4], 16)
            sp.wait_ge(pr_done, NPC)
            for i in range(2):
                sp.dma_start(late[i], w_mod[:, :, (4 + i) * 512:(5 + i) * 512]).then_inc(late_in[i], 16)
            with sp.Fori(1, 4) as j:
                for i in range(2):
                    sp.wait_ge(late_used, j * 2 + (i - 1))
                    sp.dma_start(late[i], w_mod[:, :, ds(j * 1024 + (4 + i) * 512, 512)])\
                        .then_inc(late_in[i], 16)
            sp.wait_ge(g1_ready, 1)
            for j in range(2):
                sp.dma_start(s.g1_d[j].rearrange("(k p) -> p k", p=P), s.modT[:, 16:24, j],
                             allow_slow_non_contiguous=True).then_inc(g1_out, 16)
            sp.wait_ge(g1_out, 32)
            sp.wait_ge(cout, NP_)
            sp.dma_start(s.conv_d, cv.rearrange("p a b -> p (a b)")).then_inc(conv_spill, 16)
            sp.wait_ge(conv_spill, 16)
            sp.wait_ge(ups, 80)

        @block.gpsimd
        def _(pool):
            nc.gpsimd.memset(s.lora_up[:, :, :], 0.0).then_inc(zero, 1)
            nc.gpsimd.memset(u[:, :, :], 0.0).then_inc(zero, 1)

        @block.tensor
        def _(pe):
            for sm in (h_act, h_dve):
                pe.sem_inc(sm, 2)
            for sm in free:
                pe.sem_inc(sm, 1)

            def modulate(weights, col0, used):
                for m in range(4):
                    for k in range(KC):
                        last = nc.tensor.matmul(modps[:, col0 + m, :],
                                                weights[:, k, m * P:(m + 1) * P], s.condT[:, k, :],
                                                start=(k == 0), stop=(k == KC - 1))
                last.then_inc(used, 1)

            pe.wait_ge(cond_ready, 1)
            for n in range(4):
                pe.wait_ge(mod_in[n % 2], 16 * (n // 2 + 1))
                modulate(slab[n % 2], 4 * n, mod_used)

            def transposes(j):
                for i in range(2):
                    pe.wait_ge(xn_done, j * 2 + (i + 1))
                    pe.wait_ge(h_act, j * 2 + (i + 1))
                    pe.wait_ge(h_dve, j * 2 + (i + 1))
                    for k in range(KC):
                        last = nc.tensor.transpose(trp[i][:, k * P:(k + 1) * P],
                                                   xn[i][:, k * P:(k + 1) * P], K["ident"])
                    last.then_inc(tr_done, 1)

            with pe.Fori(0, NT // 2) as j:
                transposes(j)
            pe.wait_ge(h_act, NT + 2)
            pe.wait_ge(h_dve, NT + 2)

            def project(j, i):
                pe.wait_ge(win[i], j * 16 + 16)
                pe.wait_ge(free[i % 2], j * 2 + (i // 2 + 1))
                for c0, w in COLS3:
                    for k in range(KC):
                        last = nc.tensor.matmul(pset[i % 2][:, c0:c0 + w], ws[i][:, k, :],
                                                hT[:, k, c0:c0 + w], start=(k == 0), stop=(k == KC - 1))
                last.then_inc(pr_done, 1)

            with pe.Fori(0, FULL) as j:
                for i in range(BODY):
                    project(j, i)
            for i in range(NPC - BODY * FULL):
                project(FULL, i)

            pe.wait_ge(conv_done, NP_)
            pe.wait_ge(free[0], 13)
            pe.wait_ge(free[1], 12)
            for c0, w in COLS3:
                for k in range(NP_):
                    last = nc.tensor.matmul(PS[:, c0:c0 + w], K["lnmean"], cv[:, k, c0:c0 + w],
                                            start=(k == 0), stop=(k == NP_ - 1))
            last.then_inc(mean_ps, 1)
            for n in range(8):
                pe.wait_ge(late_in[n % 2], 16 * (n // 2 + 1))
                modulate(late[n % 2], 16 + 4 * n, late_used)
            for k in range(NP_):
                pe.wait_ge(csq, k + 1)
                for c0, w in COLS3:
                    last = nc.tensor.matmul(PS[:, 3 * 512 + c0:3 * 512 + c0 + w], K["lnmean"],
                                            sq[:, k, c0:c0 + w], start=(k == 0), stop=(k == NP_ - 1))
            last.then_inc(var_ps, 1)

        @block.scalar
        def _(act):
            act.wait_ge(tables, 32)
            cond = V["cond"].rearrange("p (k j) -> p k j", j=2)
            nc.scalar.activation(s.condT[:, :, :], cond, ACT.Sigmoid).then_inc(cond_sig, 1)

            def pair(j, g):
                for i in range(2):
                    act.wait_ge(x_in[i], j * 16 + 16)
                    nc.scalar.activation(junk[i], xt[i], ACT.Square, accum_out=ssq[i]).then_inc(sq_done, 1)
                for i in range(2):
                    act.wait_ge(ms_done, j * 2 + (i + 1))
                    nc.scalar.activation(root[i], ms[i], ACT.Sqrt).then_inc(rs_done, 1)
                for i in range(2):
                    act.wait_ge(tr_done, j * 2 + (i + 1))
                    for k in range(4):
                        last = nc.scalar.activation(hT[:, k, ds(j * (2 * P) + i * P, P)],
                                                    trp[i][:, k * P:(k + 1) * P], ACT.Identity,
                                                    scale=s.A1[:, k, g:g + 1], bias=s.B1[:, k, g:g + 1])
                    last.then_inc(h_act, 1)

            act.wait_ge(mod_ready, 1)
            with act.Fori(0, NTS // 2) as j:
                pair(j, 0)
            pair(NTS // 2, 1)

            with act.Fori(0, 4) as j:
                act.wait_ge(pr_done, j * 2 + 1)
                act.wait_ge(u_done, j + 1)
                nc.scalar.activation(ge[0], pset[0], ACT.Sigmoid).then_inc(gate_sig, 1)
                act.wait_ge(gate_sig, j + 1)
                act.sem_inc(free[0], 1)
            act.wait_ge(u_done, 5)
            with act.Fori(0, 6) as j:
                for i in range(2):
                    act.wait_ge(pr_done, j * 2 + (9 + i))
                    nc.scalar.activation(s.rkv[:, ds(j * 2 + i, 1), :].rearrange("p a b -> p (a b)"),
                                         pset[i], ACT.Copy).then_inc(free[i], 1)
            for n, fn in enumerate((ACT.Tanh, ACT.Copy, ACT.Sigmoid)):
                act.wait_ge(pr_done, 21 + n)
                nc.scalar.activation(s.loraT[:, n, :], pset[n % 2], fn)\
                    .then_inc(free[n % 2], 1)
            for k in range(NP_):
                act.wait_ge(cen, k + 1)
                nc.scalar.activation(sq[:, k, :], cv[:, k, :], ACT.Square).then_inc(csq, 1)
            act.wait_ge(var_done, 1)
            nc.scalar.activation(lrs, lrs, ACT.Sqrt).then_inc(lrs_done, 1)
            for k in range(NP_):
                act.wait_ge(scaled, k + 1)
                nc.scalar.activation(cv[:, k, :], cv[:, k, :], ACT.Identity, scale=V["lng"][:, k:k + 1],
                                     bias=V["lnb"][:, k:k + 1]).then_inc(aff_done, 1)
                act.wait_ge(aff_done, k + 1)
                nc.scalar.activation(sq[:, k, :], cv[:, k, :], ACT.Sigmoid).then_inc(sil_sig, 1)

        @block.vector
        def _(dve):
            own = Chain(dve, dvo)
            dve.sem_inc(u_done, 1)
            cond = V["cond"].rearrange("p (k j) -> p k j", j=2)
            dve.wait_ge(cond_sig, 1)
            nc.vector.tensor_tensor(s.condT[:, :, :], s.condT[:, :, :], cond, ALU.mult)\
                .then_inc(cond_ready, 1)

            def mod_out(lo, n):
                b = V["bmod"][:, lo:lo + n].unsqueeze(2).to_broadcast([P, n, 2])
                return nc.vector.tensor_tensor(s.modT[:, lo:lo + n, :], modps[:, lo:lo + n, :], b, ALU.add)

            def one_plus_times(out, sc, norm):
                g = norm.unsqueeze(2).to_broadcast([P, KC, 2])
                return nc.vector.scalar_tensor_tensor(out=out[:, :, :], in0=sc, scalar=1.0, in1=g,
                                                      op0=ALU.add, op1=ALU.mult)

            dve.wait_ge(mod_used, 4)
            own.link(mod_out(0, 16))
            one_plus_times(s.A1, s.modT[:, 8:16, :], V["n1"]).then_inc(mod_ready, 1)
            dve.wait_ge(mod_ready, 1)

            def pair(j, g):
                for i in range(2):
                    dve.wait_ge(sq_done, j * 2 + (i + 1))
                    nc.vector.tensor_scalar(ms[i], ssq[i], 1.0 / D, RMS_EPS, ALU.mult, ALU.add)\
                        .then_inc(ms_done, 1)
                for i in range(2):
                    dve.wait_ge(rs_done, j * 2 + (i + 1))
                    nc.vector.reciprocal(rstd[i], root[i]).then_inc(rr_done, 1)
                    dve.wait_ge(rr_done, j * 2 + (i + 1))
                    nc.vector.tensor_scalar(xn[i], xt[i], rstd[i], None, ALU.mult).then_inc(xn_done, 1)
                for i in range(2):
                    dve.wait_ge(tr_done, j * 2 + (i + 1))
                    for k in range(4, KC):
                        last = nc.vector.tensor_scalar(hT[:, k, ds(j * (2 * P) + i * P, P)],
                                                       trp[i][:, k * P:(k + 1) * P],
                                                       s.A1[:, k, g:g + 1], s.B1[:, k, g:g + 1],
                                                       ALU.mult, ALU.add)
                    last.then_inc(h_dve, 1)

            with dve.Fori(0, NTS // 2) as j:
                pair(j, 0)
            pair(NTS // 2, 1)

            dve.wait_ge(zero, 2)
            base, n0 = own.n, 2
            with dve.Fori(0, NP_) as j:
                own.at = j * n0
                dve.wait_ge(gate_sig, j + 1)
                dve.wait_ge(pr_done, j * 2 + 2)
                uc = u[:, ds(j, 1), :].rearrange("p a (w x) -> p (a w) x", x=WIN)
                own.link(nc.vector.tensor_tensor(
                    uc[:, :, PAD:PAD + GRID], ge[0].rearrange("p (w x) -> p w x", x=GRID),
                    pset[1].rearrange("p (w x) -> p w x", x=GRID), ALU.mult))
                dve.sem_inc(free[1], 1)
                w0 = TS // GRID
                nc.vector.tensor_copy(uc[:, w0 + 1:NWIN, 0:PAD], uc[:, w0:NWIN - 1, GRID:GRID + PAD])
                own.link(nc.vector.tensor_copy(uc[:, w0:NWIN - 1, PAD + GRID:WIN],
                                               uc[:, w0 + 1:NWIN, PAD:2 * PAD]))
                dve.sem_inc(u_done, 1)
            assert own.n == base + n0
            own.n, own.at = base + n0 * NP_, 0
            base = own.n
            with dve.Fori(0, NP_) as j:
                own.at = j * KW
                uc = u[:, ds(j, 1), :].rearrange("p a (w x) -> p (a w) x", x=WIN)
                out = cv[:, ds(j, 1), :].rearrange("p a (w x) -> p (a w) x", x=GRID)
                nc.vector.tensor_copy(s.st[:, 6:7], V["db"][:, ds(j, 1)]).then_inc(conv_own, 1)
                taps = s.taps
                nc.vector.tensor_copy(taps[:, :], V["dw"][:, ds(j * KW, KW)]).then_inc(conv_own, 1)
                dve.wait_ge(conv_own, j * 2 + 2)
                for k in range(KW):
                    src = uc[:, :, k:k + GRID]
                    if k == 0:
                        ins = nc.vector.tensor_scalar(out, src, taps[:, 0:1], s.st[:, 6:7],
                                                      ALU.mult, ALU.add)
                    else:
                        ins = nc.vector.scalar_tensor_tensor(out=out, in0=src, scalar=taps[:, k:k + 1],
                                                             in1=out, op0=ALU.mult, op1=ALU.add)
                    own.link(ins)
                dve.sem_inc(conv_done, 1)
            own.n, own.at = base + NP_ * KW, 0
            dve.wait_ge(mean_ps, 1)
            for k in range(NP_):
                nc.vector.tensor_tensor(cv[:, k, :], cv[:, k, :], PS[:, 0:T], ALU.subtract)\
                    .then_inc(cen, 1)
            dve.wait_ge(late_used, 8)
            own.link(mod_out(16, 32))
            dve.sem_inc(g1_ready, 1)
            own.link(one_plus_times(s.A2, s.modT[:, 32:40, :], V["n2"]))
            dve.wait_ge(var_ps, 1)
            nc.vector.tensor_scalar(lrs, PS[:, 3 * 512:3 * 512 + T], LN_EPS, None, ALU.add)\
                .then_inc(var_done, 1)
            dve.wait_ge(lrs_done, 1)
            own.link(nc.vector.reciprocal(lrs, lrs))
            for k in range(NP_):
                nc.vector.tensor_tensor(cv[:, k, :], cv[:, k, :], lrs, ALU.mult).then_inc(scaled, 1)
            for k in range(NP_):
                dve.wait_ge(sil_sig, k + 1)
                nc.vector.tensor_tensor(cv[:, k, :], cv[:, k, :], sq[:, k, :], ALU.mult).then_inc(cout, 1)


def looped(eng, own, lo, hi, links, body):
    base = own.n
    with eng.Fori(lo, hi) as i:
        own.at = i * links + (-lo * links)
        body(i)
    assert own.n == base + links, (own.n - base, links)
    own.n, own.at = base + (hi - lo) * links, 0


SEGMENTS = ((0, NCP), (NCP, NCS), (NCS, NCH))


def phase_wkv(nc, s):
    a, K, V, PS, M, sem = s.a, s.K, s.V, s.PS, s.M, s.sem
    ar = Arena(M, s.n_main, s.mark)
    PC = NP_ * C
    kk = ar.get(NP_, T)
    kk_flat = kk.rearrange("p a b -> p (a b)")
    at_work = ar.at
    two = (0, 1)

    def pair_of(*shape):
        return [ar.get(*shape) for _ in two]

    wa = pair_of(2, NP_, C)
    cum = pair_of(2, NP_, C)
    inv = pair_of(NP_, C)
    kd = pair_of(NP_, C)
    ba = pair_of(NP_, C)
    kr = pair_of(NP_, 2 * C)
    bet = pair_of(NP_, C)
    key = pair_of(NP_, C)
    at_bd = ar.at
    bds = {n: pair_of(NP_, P) for n in ("AT", "M", "P", "Q", "Z", "NT", "keyt", "bett",
                                        "kap", "rho", "bet", "key", "val")}
    N, Z = pair_of(NP_, C), ba
    Vt, X, U, S = pair_of(NP_, HS), pair_of(NP_, HS), pair_of(NP_, HS), pair_of(NP_, HS)
    Yo = X
    S_next = ar.get(NP_, HS)
    S_keep = ar.get(NP_, HS)
    fin = bds["P"][0]
    st_rows = M[0:HS, at_bd:at_bd + 2 * NH * HS].rearrange("p (d n) -> p d n", d=2)
    sqt = [bds["bett"][i].rearrange("p a b -> p (a b)") for i in two]
    root_t = M[:, at_work:at_work + NP_ * T]
    BA, BB, BC, BD = [[PS[:, (4 * d + b) * 512:(4 * d + b + 1) * 512] for d in two] for b in range(4)]

    def both(name):
        return [sem(f"{name}{d}") for d in two]

    dvo, ready = sem("dve_own_b"), sem("kk_ready")
    zeroed, turns = sem("bd_zeroed"), sem("pool_turns")
    st_loaded, st_ps, st_set = sem("state_loaded"), sem("state_transposed"), sem("state_set")
    kraw, ksq, kn_ps, kn, kroot = (sem("kk_raw"), sem("kk_squared"), sem("kk_norm_psum"),
                                   sem("kk_norm"), sem("kk_root"))
    aw, t1b, t1t = both("lora_out"), both("lora_biased"), both("lora_tanh")
    inv_e = both("inv_ready")
    cr, er, kdr = both("sums_ready"), both("exps_ready"), both("kd_ready")
    krr, bkr = both("kap_rho_ready"), both("bet_key_ready")
    vbd, kbd, bbd = both("v_bd_ready"), both("kap_rho_bd"), both("bet_key_bd")
    v_ps, g1_ps, a5_ps, g2_ps, kt_ps, bt_ps = (both("v_psum"), both("gram_bet_psum"), both("gram_l_psum"),
                                               both("gram_key_psum"), both("keyt_psum"), both("bett_psum"))
    v_r, kt_r, bt_r = both("v_rows"), both("keyt_ready"), both("bett_ready")
    inv_r, mpq = both("inverse_started"), both("masked_grams")
    y_ps, z_r, n_ps, n_r = both("level_y_psum"), both("level_z"), both("level_n_psum"), both("level_n")
    x_ps, x_r, u_ps, u_r = both("x_psum"), both("x_ready"), both("u_psum"), both("u_ready")
    o_ps, o_r, o_sp = both("y_psum"), both("y_ready"), both("y_written")
    kd_sp, o_free, kd_free = both("kd_written"), both("y_buffer_free"), both("kd_buffer_free")
    done, st_r = both("round_psum_done"), both("state_ready")
    sw = sem("state_switched")
    out_ps, out_r, out_w = sem("final_psum"), sem("final_ready"), sem("final_written")

    def cols(i, d, n=C):
        return ds(i * C, n) if d == 0 else ds(i * (-C) + (NCH - 1) * C, n)

    def q4(ap):
        return ap.rearrange("p (a b) -> p a b", a=NP_)

    def bd4(ap):
        return ap.rearrange("p a (h t) -> p a h t", h=2)

    def over_h(ap):
        return ap.unsqueeze(2).to_broadcast([P, NP_, 2, C])

    def mask_bd(m):
        return m.rearrange("p (h t) -> p h t", h=2).unsqueeze(1).to_broadcast([P, NP_, 2, C])

    def mask_c(m):
        return m.unsqueeze(1).to_broadcast([P, NP_, C])

    NK = NP_ * T // 512

    with nc.Block() as block:

        @block.sync
        def _(sp):
            for d in two:
                sp.dma_start(st_rows[:, d, :].rearrange("v (h k) -> v h k", h=NH),
                             a["state"][d].rearrange("h v k -> v h k")).then_inc(st_loaded, 16)
                sp.sem_inc(o_free[d], 1)
                sp.sem_inc(kd_free[d], 1)
            with sp.Fori(0, NCH) as i:
                for d in two:
                    sp.wait_ge(kdr[d], i + 1)
                    sp.dma_start(s.kd_d[d][:, :, cols(i, d)], kd[d]).then_inc(kd_sp[d], 16)
                for d in two:
                    chunk = i if d == 0 else i * (-1) + (NCH - 1)
                    sp.wait_ge(o_r[d], i + 1)
                    sp.dma_start(s.y_d[d][ds(chunk, 1)].rearrange("a p n -> (a p) n"),
                                 Yo[d].rearrange("p a b -> p (a b)")).then_inc(o_sp[d], 16)
                    sp.wait_ge(kd_sp[d], i * 16 + 16)
                    sp.sem_inc(kd_free[d], 1)
                for d in two:
                    sp.wait_ge(o_sp[d], i * 16 + 16)
                    sp.sem_inc(o_free[d], 1)
            sp.wait_ge(out_r, 1)
            for d in two:
                for q in range(2):
                    for j in range(2):
                        h0 = 2 * (2 * q + j)
                        src = fin[j * HS:(j + 1) * HS, d * 2 + q, :].rearrange("v (h k) -> v h k", h=2)
                        sp.dma_start(a["out_state"][d, h0:h0 + 2].rearrange("h v k -> v h k"), src)\
                            .then_inc(out_w, 16)
            sp.wait_ge(out_w, 16 * 8)

        @block.gpsimd
        def _(pool):
            for n in ("kap", "rho", "bet", "key", "val"):
                for d in two:
                    last = nc.gpsimd.memset(bds[n][d], 0.0)
            last.then_inc(zeroed, 1)
            pool.wait_ge(zeroed, 1)

            def spread(dst, src):
                nc.gpsimd.tensor_copy(dst[0:HS, :, 0:C], src[0:HS])
                return nc.gpsimd.tensor_copy(dst[HS:P, :, C:P], src[HS:P])

            with pool.Fori(0, NCH) as i:
                for d in two:
                    hold(pool, turns, (done[d], i + 1))
                    spread(bds["val"][d], s.vT[:, :, cols(i, d)]).then_inc(vbd[d], 1)
                for d in two:
                    hold(pool, turns, (krr[d], i + 1))
                    spread(bds["kap"][d], kr[d][:, :, 0:C])
                    spread(bds["rho"][d], kr[d][:, :, C:2 * C]).then_inc(kbd[d], 1)

        @block.tensor
        def _(pe):
            for d in two:
                pe.sem_inc(done[d], 1)
            pe.wait_ge(st_loaded, 32)
            for d in two:
                for p in range(NP_):
                    last = nc.tensor.transpose(BA[0][:, (d * NP_ + p) * HS:(d * NP_ + p + 1) * HS],
                                               st_rows[:, d, p * P:(p + 1) * P], K["ident"][0:HS, 0:HS])
            last.then_inc(st_ps, 1)
            for n in range(NK):
                pe.wait_ge(ksq, n + 1)
                if n >= 2:
                    pe.wait_ge(kn, n - 1)
                nc.tensor.matmul(BB[n % 2], K["blockones"], sqt[n % 2], start=True, stop=True)\
                    .then_inc(kn_ps, 1)
            pe.wait_ge(ready, 1)
            pe.wait_ge(st_set, 1)

            def each(out, lhsT, rhs, w, acc=None):
                for p in range(NP_):
                    terms = [(lhsT, rhs)] + (acc or [])
                    for n, (l, r) in enumerate(terms):
                        last = nc.tensor.matmul(out[:, p * w:(p + 1) * w], l[:, p, :], r[:, p, :],
                                                start=(n == 0), stop=(n == len(terms) - 1))
                return last

            def body(i):
                for d in two:
                    for q in range(2):
                        for p in range(NP_):
                            o = (q * NP_ + p) * C
                            last = nc.tensor.matmul(BA[d][:, o:o + C],
                                                    s.lora_up[:, 2 * q + d, p * P:(p + 1) * P],
                                                    s.loraT[:, q, cols(i, d)], start=True, stop=True)
                    last.then_inc(aw[d], 1)
                for d in two:
                    b = {n: v[d] for n, v in bds.items()}
                    pe.wait_ge(vbd[d], i + 1)
                    for p in range(NP_):
                        last = nc.tensor.matmul(BC[d][:, p * HS:(p + 1) * HS], b["val"][:, p, :],
                                                K["fold"], start=True, stop=True)
                    last.then_inc(v_ps[d], 1)
                    pe.wait_ge(krr[d], i + 1)
                    pe.wait_ge(bbd[d], i + 1)
                    each(BB[d], b["bet"], kr[d], 2 * C).then_inc(g1_ps[d], 1)
                    pe.wait_ge(kbd[d], i + 1)
                    each(BD[d], b["kap"], bet[d], C).then_inc(a5_ps[d], 1)
                    pe.wait_ge(v_r[d], i + 1)
                    each(BC[d], b["key"], kr[d], 2 * C).then_inc(g2_ps[d], 1)
                    for p in range(NP_):
                        last = nc.tensor.transpose(BA[d][:, p * P:(p + 1) * P], b["key"][:, p, :], K["ident"])
                    last.then_inc(kt_ps[d], 1)
                for lv in range(len(LEVELS)):
                    for d in two:
                        b = {n: v[d] for n, v in bds.items()}
                        if lv == 0:
                            pe.wait_ge(inv_r[d], i + 1)
                        else:
                            pe.wait_ge(n_r[d], i * 5 + lv)
                        each(BB[d], b["AT"], N[d], C).then_inc(y_ps[d], 1)
                        if lv == 0:
                            pe.wait_ge(kt_r[d], i + 1)
                            for p in range(NP_):
                                last = nc.tensor.transpose(BA[d][:, p * P:(p + 1) * P], b["bet"][:, p, :],
                                                           K["ident"])
                            last.then_inc(bt_ps[d], 1)
                    for d in two:
                        b = {n: v[d] for n, v in bds.items()}
                        pe.wait_ge(z_r[d], i * 5 + (lv + 1))
                        if lv < len(LEVELS) - 1:
                            each(BC[d], b["NT"], Z[d], C)
                        each(BD[d], b["Z"], b["NT"], P).then_inc(n_ps[d], 1)
                for d in two:
                    b = {n: v[d] for n, v in bds.items()}
                    pe.wait_ge(st_r[d], i + 1)
                    pe.wait_ge(mpq[d], i + 1)
                    each(BB[d], b["kap"], S[d], HS, [(b["M"], Vt[d])]).then_inc(x_ps[d], 1)
                for d in two:
                    pe.wait_ge(n_r[d], i * 5 + 5)
                    pe.wait_ge(x_r[d], i + 1)
                    each(BC[d], bds["NT"][d], X[d], HS).then_inc(u_ps[d], 1)
                for d in two:
                    b = {n: v[d] for n, v in bds.items()}
                    pe.wait_ge(u_r[d], i + 1)
                    pe.wait_ge(bt_r[d], i + 1)
                    each(BD[d], b["rho"], S[d], HS, [(b["P"], U[d]), (b["Q"], Vt[d])]).then_inc(o_ps[d], 1)
                    each(BB[d][:, 256:512], b["keyt"], Vt[d], HS, [(b["bett"], U[d])]).then_inc(done[d], 1)

            for n, (lo, hi) in enumerate(SEGMENTS):
                with pe.Fori(lo, hi) as i:
                    body(i)
                pe.wait_ge(sw, n + 1)
            for d, src in enumerate((S[0], S_keep)):
                for q in range(2):
                    last = nc.tensor.transpose(BA[0][:, (d * 2 + q) * P:(d * 2 + q + 1) * P],
                                               src[:, 2 * q:2 * q + 2, :].rearrange("p a b -> p (a b)"),
                                               K["ident"])
            last.then_inc(out_ps, 1)

        @block.scalar
        def _(act):
            for n in range(NK):
                act.wait_ge(kraw, 1)
                if n >= 2:
                    act.wait_ge(kn_ps, n - 1)
                nc.scalar.activation(sqt[n % 2], kk_flat[:, n * 512:(n + 1) * 512], ACT.Square)\
                    .then_inc(ksq, 1)
            for n in range(NK):
                act.wait_ge(kn, n + 1)
                nc.scalar.activation(root_t[:, n * 512:(n + 1) * 512], root_t[:, n * 512:(n + 1) * 512],
                                     ACT.Sqrt).then_inc(kroot, 1)

            def spread(dst, src):
                nc.scalar.activation(dst[0:HS, :, 0:C], src[0:HS], ACT.Copy)
                return nc.scalar.activation(dst[HS:P, :, C:P], src[HS:P], ACT.Copy)

            act.wait_ge(zeroed, 1)

            def body(i):
                for d in two:
                    act.wait_ge(t1b[d], i + 1)
                    nc.scalar.activation(wa[d], wa[d], ACT.Tanh, scale=0.5).then_inc(t1t[d], 1)
                for d in two:
                    act.wait_ge(cr[d], i + 1)
                    nc.scalar.activation(inv[d], cum[d][:, 1], ACT.Exp, scale=C0).then_inc(inv_e[d], 1)
                for d in two:
                    act.wait_ge(inv_e[d], i + 1)
                    nc.scalar.activation(cum[d], cum[d], ACT.Exp, scale=-C0).then_inc(er[d], 1)
                for d in two:
                    act.wait_ge(bkr[d], i + 1)
                    spread(bds["bet"][d], bet[d])
                    spread(bds["key"][d], key[d]).then_inc(bbd[d], 1)
                for d in two:
                    act.wait_ge(v_ps[d], i + 1)
                    nc.scalar.activation(Vt[d], q4(BC[d][:, 0:PC]), ACT.Copy).then_inc(v_r[d], 1)
                    act.wait_ge(kt_ps[d], i + 1)
                    nc.scalar.activation(bds["keyt"][d], q4(BA[d]), ACT.Copy).then_inc(kt_r[d], 1)
                for lv in range(len(LEVELS)):
                    if lv == 1:
                        for d in two:
                            act.wait_ge(bt_ps[d], i + 1)
                            nc.scalar.activation(bds["bett"][d], q4(BA[d]), ACT.Copy, scale=-1.0)\
                                .then_inc(bt_r[d], 1)
                    for d in two:
                        act.wait_ge(n_ps[d], i * 5 + (lv + 1))
                        if lv < len(LEVELS) - 1:
                            nc.scalar.activation(N[d], q4(BC[d][:, 0:PC]), ACT.Copy)
                        nc.scalar.activation(bds["NT"][d], q4(BD[d]), ACT.Copy).then_inc(n_r[d], 1)
                for d in two:
                    act.wait_ge(x_ps[d], i + 1)
                    act.wait_ge(o_free[d], i + 1)
                    nc.scalar.activation(X[d], q4(BB[d][:, 0:PC]), ACT.Copy).then_inc(x_r[d], 1)
                for d in two:
                    act.wait_ge(u_ps[d], i + 1)
                    nc.scalar.activation(U[d], q4(BC[d][:, 0:PC]), ACT.Copy).then_inc(u_r[d], 1)
                for d in two:
                    act.wait_ge(o_ps[d], i + 1)
                    nc.scalar.activation(Yo[d], q4(BD[d][:, 0:PC]), ACT.Copy).then_inc(o_r[d], 1)

            with act.Fori(0, NCH) as i:
                body(i)
            act.wait_ge(out_ps, 1)
            nc.scalar.activation(fin, BA[0].rearrange("p (a b) -> p a b", b=P), ACT.Copy).then_inc(out_r, 1)

        @block.vector
        def _(dve):
            own = Chain(dve, dvo)
            for p in range(NP_):
                last = nc.vector.tensor_scalar(kk[:, p, :], s.kT[:, p, :], V["k_k"][:, p:p + 1], None, ALU.mult)
            last.then_inc(kraw, 1)
            for n in range(NK):
                dve.wait_ge(kn_ps, n + 1)
                nc.vector.tensor_scalar(root_t[:, n * 512:(n + 1) * 512], BB[n % 2], 1e-24, None, ALU.max)\
                    .then_inc(kn, 1)
            for n in range(NK):
                dve.wait_ge(kroot, n + 1)
                own.link(nc.vector.reciprocal(root_t[:, n * 512:(n + 1) * 512],
                                              root_t[:, n * 512:(n + 1) * 512]))
            nc.vector.tensor_tensor(kk_flat, kk_flat, root_t, ALU.mult).then_inc(ready, 1)
            dve.wait_ge(ready, 1)
            dve.wait_ge(st_ps, 1)
            st = BA[0].rearrange("p (d a b) -> p d a b", d=2, a=NP_)
            nc.vector.memset(S[1], 0.0)
            nc.vector.tensor_copy(S[0], st[:, 0])
            own.link(nc.vector.tensor_copy(S_next, st[:, 1]))
            dve.sem_inc(st_set, 1)
            for d in two:
                dve.sem_inc(st_r[d], 1)

            def body(i):
                for d in two:
                    dve.wait_ge(aw[d], i + 1)
                    bias = V["bias_wa"][:, 8 * d:8 * d + 8].unsqueeze(2).to_broadcast([P, 8, C])
                    nc.vector.tensor_tensor(wa[d].rearrange("p q a t -> p (q a) t"),
                                            BA[d].rearrange("p (a t) -> p a t", t=C), bias, ALU.add)\
                        .then_inc(t1b[d], 1)
                for d in two:
                    dve.wait_ge(t1t[d], i + 1)
                    own.link(nc.vector.tensor_scalar(wa[d], wa[d], 0.5, 0.5, ALU.mult, ALU.add))
                    sg, ga = wa[d][:, 0], wa[d][:, 1]
                    first = cum[d][:, 1] if d == 0 else ba[d]
                    own.link(nc.vector.tensor_tensor_scan(first.rearrange("p a t -> p (a t)"), K["reset"],
                                                          sg.rearrange("p a t -> p (a t)"), 0.0,
                                                          ALU.mult, ALU.add))
                    if d == 0:
                        nc.vector.tensor_tensor(cum[d][:, 0], cum[d][:, 1], sg, ALU.subtract)\
                            .then_inc(cr[d], 1)
                    else:
                        total = first[:, :, C - 1:C].to_broadcast([P, NP_, C])
                        own.link(nc.vector.tensor_tensor(cum[d][:, 0], total, first, ALU.subtract))
                        nc.vector.tensor_tensor(cum[d][:, 1], cum[d][:, 0], sg, ALU.add).then_inc(cr[d], 1)
                    dve.wait_ge(kd_free[d], i + 1)
                    k_a = V["k_a"].unsqueeze(2).to_broadcast([P, NP_, C])
                    own.link(nc.vector.scalar_tensor_tensor(out=kd[d], in0=ga, scalar=1.0, in1=k_a,
                                                            op0=ALU.subtract, op1=ALU.mult))
                    nc.vector.scalar_tensor_tensor(out=kd[d], in0=kd[d], scalar=1.0,
                                                   in1=s.kT[:, :, cols(i, d)], op0=ALU.add, op1=ALU.mult)\
                        .then_inc(kdr[d], 1)
                    own.link(nc.vector.tensor_tensor(ba[d], kk[:, :, cols(i, d)], ga, ALU.mult))
                for d in two:
                    dve.wait_ge(er[d], i + 1)
                    nc.vector.tensor_tensor(kr[d][:, :, 0:C], cum[d][:, 0], kk[:, :, cols(i, d)], ALU.mult)
                    nc.vector.tensor_tensor(kr[d][:, :, C:2 * C], cum[d][:, 1], s.rT[:, :, cols(i, d)],
                                            ALU.mult).then_inc(krr[d], 1)
                    nc.vector.tensor_tensor(bet[d], inv[d], ba[d], ALU.mult)
                    dve.wait_ge(kdr[d], i + 1)
                    nc.vector.tensor_tensor(key[d], inv[d], kd[d], ALU.mult).then_inc(bkr[d], 1)
                for d in two:
                    b = {n: v[d] for n, v in bds.items()}
                    g1, g2 = q4(BB[d]), q4(BC[d])
                    dve.wait_ge(g1_ps[d], i + 1)
                    own.link(nc.vector.tensor_tensor(bd4(b["AT"]), over_h(g1[:, :, 0:C]),
                                                     mask_bd(K[f"strict{d}"]), ALU.mult))
                    own.link(nc.vector.tensor_tensor(b["AT"], b["AT"],
                                                     K["ident"].unsqueeze(1).to_broadcast([P, NP_, P]),
                                                     ALU.add))
                    nc.vector.tensor_tensor(b["NT"], b["AT"],
                                            K[f"first{d}"].unsqueeze(1).to_broadcast([P, NP_, P]), ALU.mult)
                    nc.vector.tensor_tensor(bd4(b["P"]), over_h(g1[:, :, C:2 * C]),
                                            mask_bd(K[f"nincl{d}"]), ALU.mult)
                    dve.wait_ge(a5_ps[d], i + 1)
                    own.link(nc.vector.tensor_tensor(N[d], q4(BD[d][:, 0:PC]), mask_c(K[f"firstc{d}"]),
                                                     ALU.mult))
                    nc.vector.tensor_tensor(N[d], N[d], mask_c(K["fold"]), ALU.add).then_inc(inv_r[d], 1)
                    dve.wait_ge(g2_ps[d], i + 1)
                    nc.vector.tensor_tensor(bd4(b["M"]), over_h(g2[:, :, 0:C]), mask_bd(K[f"strict{d}"]),
                                            ALU.mult)
                    nc.vector.tensor_tensor(bd4(b["Q"]), over_h(g2[:, :, C:2 * C]), mask_bd(K[f"incl{d}"]),
                                            ALU.mult).then_inc(mpq[d], 1)
                for lv, size in enumerate(LEVELS):
                    for d in two:
                        dve.wait_ge(y_ps[d], i * 5 + (lv + 1))
                        y = q4(BB[d][:, 0:PC])
                        if lv < len(LEVELS) - 1:
                            nc.vector.tensor_tensor(Z[d], y, mask_c(K[f"levc{d}_{size}"]), ALU.mult)
                        nc.vector.tensor_tensor(bd4(bds["Z"][d]), over_h(y), mask_bd(K[f"lev{d}_{size}"]),
                                                ALU.mult).then_inc(z_r[d], 1)
                for d in two:
                    end = C - 1 if d == 0 else 0
                    decay = cum[d][:, 1, :, end:end + 1].to_broadcast([P, NP_, HS])
                    dve.wait_ge(done[d], i + 2)
                    own.link(nc.vector.tensor_tensor(S[d], S[d], q4(BB[d][:, 256:512]), ALU.add))
                    nc.vector.tensor_tensor(S[d], S[d], decay, ALU.mult).then_inc(st_r[d], 1)

            LINKS = 17
            for n, (lo, hi) in enumerate(SEGMENTS):
                looped(dve, own, lo, hi, LINKS, body)
                for d in two:
                    dve.wait_ge(st_r[d], hi + 1)
                if n == 0:
                    own.link(nc.vector.tensor_copy(S_keep, S[1]))
                    nc.vector.tensor_copy(S[1], S_next).then_inc(sw, 1)
                elif n == 1:
                    nc.vector.memset(S[0], 0.0).then_inc(sw, 1)
                else:
                    dve.sem_inc(sw, 1)
                dve.wait_ge(sw, n + 1)


def phase_mix(nc, s):
    a, K, V, PS, M, sem = s.a, s.K, s.V, s.PS, s.M, s.sem
    ar = Arena(M, s.n_main, s.mark)
    NG = NCH * NP_
    at_y0 = ar.at
    y0 = ar.get(NG, HS)
    at_k0 = ar.at
    kd0 = ar.get(NP_, T)
    at_y1 = ar.at
    y1 = ar.get(NG, HS)
    kd1 = ar.get(NP_, T)
    cvT = ar.get(NP_, T)
    ybd = [ar.get(NP_, P) for _ in (0, 1)]
    gs = ar.get(3, NG)
    ynT = s.kT
    bon = s.rT
    w_o = M[:, at_y1:at_y1 + KC * D].rearrange("p (k n) -> p k n", n=D)
    t0 = at_y1 + KC * D
    assert t0 >= RING
    TB = 64
    aff = M[0:TB, t0:t0 + TS]
    vals = M[0:TB, t0 + TS:t0 + TS + P]
    idx = M[0:TB, t0 + TS + P:t0 + TS + 2 * P].bitcast(U32)
    idxf = M[0:TB, t0 + TS + 2 * P:t0 + TS + 3 * P]
    aft = [M[:, t0 + TS + (3 + i) * P:t0 + TS + (4 + i) * P] for i in (0, 1)]
    g1b = M[:, at_y0:at_y0 + 2 * D].rearrange("p (j n) -> p j n", n=D)
    xt = [M[:, at_y0 + (2 + i) * D:at_y0 + (3 + i) * D] for i in (0, 1)]
    junk = [M[:, at_y0 + 4 * D:at_y0 + 5 * D], M[:, at_k0 + 4 * D:at_k0 + 5 * D]]
    x2 = [M[:, at_k0 + i * D:at_k0 + (i + 1) * D] for i in (0, 1)]
    xn = [M[:, at_k0 + (2 + i) * D:at_k0 + (3 + i) * D] for i in (0, 1)]
    h2 = [s.rkv[:, 0:4, :].rearrange("p a b -> p (a b)")[:, i * D:(i + 1) * D]
          .rearrange("p (k t) -> p k t", t=P) for i in (0, 1)]
    rt = s.vT.rearrange("p a b -> p (a b)")[:, 0:KC * E].rearrange("p (k e) -> p k e", e=E)
    ex = [s.vT[:, 1, i * E:(i + 1) * E] for i in (0, 1)]
    mixps = [PS[:, 0:D], PS[:, D:2 * D]]
    trp = PS[:, 4 * 512:4 * 512 + D]
    lg, afp = PS[:, 6 * 512:6 * 512 + E], PS[:, 7 * 512:7 * 512 + P]
    ssq = [s.st[:, i:i + 1] for i in (0, 1)]
    ms = [s.st[:, i:i + 1] for i in (2, 3)]
    root = [s.st[:, i:i + 1] for i in (4, 5)]
    rstd = [s.st[:, i:i + 1] for i in (8, 9)]
    nmx = [s.st[:, i:i + 1] for i in (6, 7)]
    esum = [s.st[:, i:i + 1] for i in (10, 11)]
    tiles = [(p, c0, w) for p in range(NP_) for c0, w in COLS3]

    y_in, kd_in, c_in, wo_in, misc_in = (sem("y_in"), sem("kd_in"), sem("conv_in"), sem("w_out_in"),
                                         sem("gate1_router_in"))
    gsq, gvar, groot, y1_free = sem("gn_squared"), sem("gn_var"), sem("gn_root"), sem("y1_free")
    yc_done, kd_free = sem("gn_centered"), sem("kd1_free")
    ybz, yb_r, yn_ps, yn_r = sem("ybd_zeroed"), sem("ybd_ready"), sem("yn_psum"), sem("yn_ready")
    bprod, bon_ps, rw_r = sem("bonus_product"), sem("bonus_gate_psum"), sem("rwkv_out_ready")
    x_in = [sem(f"x_again{i}") for i in (0, 1)]
    acc_w = [sem(f"residual_written{i}") for i in (0, 1)]
    xn_w = [sem(f"normed_written{i}") for i in (0, 1)]
    mx, x2_r, sq_r, ms_r, rt_r, xn_r = (sem("mix_psum"), sem("x2_ready"), sem("x2_squared"),
                                        sem("x2_mean_square"), sem("x2_root"), sem("x2_normed"))
    tr, h_a, h_d, lg_r, mx_r, ex_r, af_r, at_r, ac_r = (
        sem("x2_transposed"), sem("h2_by_act"), sem("h2_by_dve"), sem("logits"), sem("logit_max"),
        sem("exp_logits"), sem("affinity_rows"), sem("affinity_psum"), sem("affinity_ready"))
    az, dvo, tab, tabt = sem("affinity_zeroed"), sem("dve_own_c"), sem("lists_ready"), sem("lists_psum")

    with nc.Block() as block:

        @block.sync
        def _(sp):
            for d, dst in enumerate((y0, y1)):
                sp.dma_start(dst.rearrange("p (c a) b -> p c (a b)", a=NP_),
                             s.y_d[d].rearrange("c p n -> p c n")).then_inc(y_in, 16)
            for d, dst in enumerate((kd0, kd1)):
                sp.dma_start(dst, s.kd_d[d]).then_inc(kd_in, 16)
            sp.dma_start(cvT.rearrange("p a b -> p (a b)"), s.conv_d).then_inc(c_in, 16)
            sp.wait_ge(y1_free, 1)
            sp.wait_ge(kd_free, 1)
            sp.dma_start(w_o, a["w_out"].rearrange("(k p) n -> p k n", p=P)).then_inc(wo_in, 16)
            sp.wait_ge(rw_r, len(tiles))
            for j in range(2):
                sp.dma_start(g1b[:, j, :], s.g1_d[j:j + 1, :].to_broadcast([P, D])).then_inc(misc_in, 16)
            sp.dma_start(rt, a["router"].rearrange("(k p) e -> p k e", p=P)).then_inc(misc_in, 16)
            for n in range(NT + 1):
                if n < NT:
                    if n >= 2:
                        sp.wait_ge(x2_r, n - 1)
                    sp.dma_start(xt[n % 2], a["x"][n * P:(n + 1) * P, :]).then_inc(x_in[n % 2], 16)
                if n >= 1:
                    m = n - 1
                    sp.wait_ge(x2_r, m + 1)
                    sp.dma_start(s.acc_d[m * P:(m + 1) * P, :], x2[m % 2]).then_inc(acc_w[m % 2], 16)
                    sp.wait_ge(xn_r, m + 1)
                    sp.dma_start(s.xn_d[m * P:(m + 1) * P, :], xn[m % 2]).then_inc(xn_w[m % 2], 16)
            for i in (0, 1):
                sp.wait_ge(acc_w[i], 16 * NT // 2)
                sp.wait_ge(xn_w[i], 16 * NT // 2)
            sp.wait_ge(lg_r, NT)
            sp.wait_ge(ex_r, NT)
            sp.wait_ge(af_r, NT)
            for n in range(SLOTS):
                load_step(sp, s, 0, n)

        @block.gpsimd
        def _(pool):
            for i in (0, 1):
                nc.gpsimd.memset(ybd[i], 0.0).then_inc(ybz, 1)
            pool.wait_ge(y1_free, 1)
            pool.wait_ge(kd_free, 1)
            for i in (0, 1):
                nc.gpsimd.memset(aft[i], 0.0).then_inc(az, 1)
            nc.gpsimd.memset(M[0:TB, t0:t0 + TS + 3 * P], -1.0).then_inc(az, 1)

        @block.tensor
        def _(pe):
            for sm in (yn_r,):
                pe.sem_inc(sm, 2)
            with pe.Fori(0, NCH // 2) as j:
                for i in (0, 1):
                    pe.wait_ge(yb_r, j * 2 + (i + 1))
                    pe.wait_ge(yn_r, j * 2 + (i + 1))
                    for p in range(NP_):
                        last = nc.tensor.matmul(PS[:, i * 512 + p * C:i * 512 + (p + 1) * C],
                                                ybd[i][:, p, :], K["fold"], start=True, stop=True)
                    last.then_inc(yn_ps, 1)
            pe.wait_ge(bprod, 1)
            for n, (p, c0, w) in enumerate(tiles):
                if n >= 2:
                    pe.wait_ge(rw_r, n - 1)
                nc.tensor.matmul(PS[:, (2 + n % 2) * 512:(2 + n % 2) * 512 + w], K["blockones"],
                                 kd0[:, p, c0:c0 + w], start=True, stop=True)
                nc.tensor.matmul(PS[:, (4 + n % 2) * 512:(4 + n % 2) * 512 + w],
                                 s.g_up[:, p * P:(p + 1) * P], s.loraT[:, 2, c0:c0 + w],
                                 start=True, stop=True).then_inc(bon_ps, 1)
            pe.wait_ge(rw_r, len(tiles))
            pe.wait_ge(yn_r, NCH + 2)
            pe.wait_ge(wo_in, 16)
            pe.wait_ge(c_in, 16)
            pe.wait_ge(misc_in, 48)
            for n in range(NT + 3):
                if n < NT:
                    if n >= 2:
                        pe.wait_ge(x2_r, n - 1)
                    for half in (0, 1):
                        for k in range(KC):
                            src = cvT if k < NP_ else ynT
                            last = nc.tensor.matmul(mixps[n % 2][:, half * 512:(half + 1) * 512],
                                                    src[:, k % NP_, n * P:(n + 1) * P],
                                                    w_o[:, k, half * 512:(half + 1) * 512],
                                                    start=(k == 0), stop=(k == KC - 1))
                    last.then_inc(mx, 1)
                m = n - 1
                if 0 <= m < NT:
                    pe.wait_ge(xn_r, m + 1)
                    if m >= 1:
                        pe.wait_ge(h_a, m)
                        pe.wait_ge(h_d, m)
                    for k in range(KC):
                        last = nc.tensor.transpose(trp[:, k * P:(k + 1) * P],
                                                   xn[m % 2][:, k * P:(k + 1) * P], K["ident"])
                    last.then_inc(tr, 1)
                m = n - 2
                if 0 <= m < NT:
                    pe.wait_ge(h_a, m + 1)
                    pe.wait_ge(h_d, m + 1)
                    if m >= 1:
                        pe.wait_ge(ex_r, m)
                        pe.wait_ge(mx_r, m)
                    for k in range(KC):
                        last = nc.tensor.matmul(lg, h2[m % 2][:, k, :], rt[:, k, :],
                                                start=(k == 0), stop=(k == KC - 1))
                    last.then_inc(lg_r, 1)
                m = n - 3
                if 0 <= m < NT:
                    pe.wait_ge(af_r, m + 1)
                    if m >= 1:
                        pe.wait_ge(ac_r, m)
                    nc.tensor.transpose(afp, aft[m % 2], K["ident"]).then_inc(at_r, 1)
            pe.wait_ge(tab, 1)
            nc.tensor.transpose(PS[:, 0:TB], vals, K["ident"][0:TB, 0:TB])
            nc.tensor.transpose(PS[:, TB:2 * TB], idxf, K["ident"][0:TB, 0:TB]).then_inc(tabt, 1)

        @block.scalar
        def _(act):
            act.wait_ge(yc_done, 1)
            nc.scalar.activation(y1, y0, ACT.Square).then_inc(gsq, 1)
            act.wait_ge(gvar, 1)
            nc.scalar.activation(gs[:, 1, :], gs[:, 1, :], ACT.Sqrt).then_inc(groot, 1)
            with act.Fori(0, NCH // 2) as j:
                for i in (0, 1):
                    act.wait_ge(yn_ps, j * 2 + (i + 1))
                    for p in range(NP_):
                        last = nc.scalar.activation(ynT[:, p, ds(j * (2 * C) + i * C, C)],
                                                    PS[:, i * 512 + p * C:i * 512 + (p + 1) * C],
                                                    ACT.Identity, scale=V["gng"][:, p:p + 1],
                                                    bias=V["gnb"][:, p:p + 1])
                    last.then_inc(yn_r, 1)
            for n in range(NT + 2):
                if n < NT:
                    i = n % 2
                    act.wait_ge(x2_r, n + 1)
                    nc.scalar.activation(junk[i], x2[i], ACT.Square, accum_out=ssq[i]).then_inc(sq_r, 1)
                    act.wait_ge(ms_r, n + 1)
                    nc.scalar.activation(root[i], ms[i], ACT.Sqrt).then_inc(rt_r, 1)
                m = n - 1
                if 0 <= m < NT:
                    g = 0 if m < NTS else 1
                    act.wait_ge(tr, m + 1)
                    for k in range(4):
                        last = nc.scalar.activation(h2[m % 2][:, k, :], trp[:, k * P:(k + 1) * P],
                                                    ACT.Identity, scale=s.A2[:, k, g:g + 1],
                                                    bias=s.B2[:, k, g:g + 1])
                    last.then_inc(h_a, 1)
                m = n - 2
                if 0 <= m < NT:
                    act.wait_ge(mx_r, m + 1)
                    nc.scalar.activation(ex[m % 2], lg, ACT.Exp, bias=nmx[m % 2],
                                         accum_out=esum[m % 2]).then_inc(ex_r, 1)

        @block.vector
        def _(dve):
            own = Chain(dve, dvo)
            dve.wait_ge(y_in, 32)
            own.link(nc.vector.tensor_tensor(y0, y0, y1, ALU.add))
            own.link(nc.vector.tensor_reduce(gs[:, 0, :], y0, AX.X, ALU.add))
            own.link(nc.vector.tensor_scalar(gs[:, 0, :], gs[:, 0, :], 1.0 / HS, None, ALU.mult))
            nc.vector.tensor_tensor(y0, y0, gs[:, 0, :].unsqueeze(2).to_broadcast([P, NG, HS]),
                                    ALU.subtract).then_inc(yc_done, 1)
            dve.wait_ge(kd_in, 32)
            own.link(nc.vector.tensor_tensor(kd0, kd0, kd1, ALU.add))
            dve.sem_inc(kd_free, 1)
            for p in range(NP_):
                last = nc.vector.scalar_tensor_tensor(out=kd0[:, p, :], in0=s.rT[:, p, :],
                                                      scalar=V["r_k"][:, p:p + 1], in1=kd0[:, p, :],
                                                      op0=ALU.mult, op1=ALU.mult)
            last.then_inc(bprod, 1)
            dve.wait_ge(gsq, 1)
            own.link(nc.vector.tensor_reduce(gs[:, 1, :], y1, AX.X, ALU.add))
            dve.sem_inc(y1_free, 1)
            nc.vector.tensor_scalar(gs[:, 1, :], gs[:, 1, :], 1.0 / HS, GN_EPS, ALU.mult, ALU.add)\
                .then_inc(gvar, 1)
            dve.wait_ge(groot, 1)
            own.link(nc.vector.reciprocal(gs[:, 2, :], gs[:, 1, :]))
            dve.wait_ge(ybz, 2)
            with dve.Fori(0, NCH // 2) as j:
                for i in (0, 1):
                    dve.wait_ge(yn_r, j * 2 + (i + 1))
                    for h in (0, 1):
                        rows = slice(h * HS, (h + 1) * HS)
                        r = gs[rows, 2, ds(j * (2 * NP_) + i * NP_, NP_)].unsqueeze(2)\
                            .to_broadcast([HS, NP_, HS])
                        last = nc.vector.tensor_tensor(ybd[i][rows, :, h * HS:(h + 1) * HS],
                                                       y0[rows, ds(j * (2 * NP_) + i * NP_, NP_), :], r,
                                                       ALU.mult)
                    last.then_inc(yb_r, 1)
            dve.wait_ge(yn_r, NCH + 2)
            for n, (p, c0, w) in enumerate(tiles):
                dve.wait_ge(bon_ps, n + 1)
                c = slice(c0, c0 + w)
                own.link(nc.vector.tensor_tensor(bon[:, p, c], PS[:, (2 + n % 2) * 512:][:, 0:w],
                                                 s.vT[:, p, c], ALU.mult))
                own.link(nc.vector.tensor_tensor(ynT[:, p, c], ynT[:, p, c], bon[:, p, c], ALU.add))
                nc.vector.tensor_tensor(ynT[:, p, c], ynT[:, p, c], PS[:, (4 + n % 2) * 512:][:, 0:w],
                                        ALU.mult).then_inc(rw_r, 1)
            dve.wait_ge(misc_in, 48)
            dve.wait_ge(az, 3)
            for n in range(NT + 3):
                if n < NT:
                    i, g = n % 2, 0 if n < NTS else 1
                    dve.wait_ge(mx, n + 1)
                    dve.wait_ge(x_in[i], 16 * (n // 2 + 1))
                    if n >= 2:
                        dve.wait_ge(acc_w[i], 16 * (n // 2))
                        dve.wait_ge(xn_w[i], 16 * (n // 2))
                    own.link(nc.vector.tensor_tensor(x2[i], mixps[i], g1b[:, g, :], ALU.mult))
                    nc.vector.tensor_tensor(x2[i], x2[i], xt[i], ALU.add).then_inc(x2_r, 1)
                    dve.wait_ge(sq_r, n + 1)
                    nc.vector.tensor_scalar(ms[i], ssq[i], 1.0 / D, RMS_EPS, ALU.mult, ALU.add)\
                        .then_inc(ms_r, 1)
                    dve.wait_ge(rt_r, n + 1)
                    own.link(nc.vector.reciprocal(rstd[i], root[i]))
                    nc.vector.tensor_scalar(xn[i], x2[i], rstd[i], None, ALU.mult).then_inc(xn_r, 1)
                m = n - 1
                if 0 <= m < NT:
                    g = 0 if m < NTS else 1
                    dve.wait_ge(tr, m + 1)
                    for k in range(4, KC):
                        last = nc.vector.tensor_scalar(h2[m % 2][:, k, :], trp[:, k * P:(k + 1) * P],
                                                       s.A2[:, k, g:g + 1], s.B2[:, k, g:g + 1],
                                                       ALU.mult, ALU.add)
                    last.then_inc(h_d, 1)
                m = n - 2
                if 0 <= m < NT:
                    i, o = m % 2, 0 if m < NTS else PB
                    dve.wait_ge(lg_r, m + 1)
                    nc.vector.tensor_reduce(nmx[i], lg, AX.X, ALU.max, negate=True).then_inc(mx_r, 1)
                    dve.wait_ge(ex_r, m + 1)
                    own.link(nc.vector.reciprocal(esum[i], esum[i]))
                    nc.vector.tensor_scalar(aft[i][:, o:o + E], ex[i], esum[i], None, ALU.mult)\
                        .then_inc(af_r, 1)
                m = n - 3
                if 0 <= m < NT:
                    o, t = (0, m) if m < NTS else (PB, m - NTS)
                    dve.wait_ge(at_r, m + 1)
                    nc.vector.tensor_copy(aff[o:o + E, t * P:(t + 1) * P], afp[o:o + E, :]).then_inc(ac_r, 1)
            dve.wait_ge(ac_r, NT)
            for n in range(CAP_S // 8):
                v8 = vals[:, 8 * n:8 * n + 8]
                own.link(nc.vector.max(v8, aff))
                own.link(nc.vector.max_index(idx[:, 8 * n:8 * n + 8], v8, aff))
                own.link(nc.vector.match_replace(aff, v8, aff, -2.0))
            nc.vector.tensor_copy(idxf, idx).then_inc(tab, 1)
            dve.wait_ge(tabt, 1)
            own.link(nc.vector.tensor_copy(s.gateT, PS[:, 0:TB]))
            own.link(nc.vector.tensor_scalar(s.idxF[:, PB:TB], PS[:, TB + PB:2 * TB], float(TS), None,
                                             ALU.add))
            own.link(nc.vector.tensor_copy(s.idxF[:, 0:PB], PS[:, TB:TB + PB]))
            own.link(nc.vector.tensor_copy(s.idxT, s.idxF))


SC = max(STEP_CHUNKS)
PIECE = KC * SC * P
RING = SLOTS * 3 * PIECE
STEP_AT = tuple(sum(STEP_CHUNKS[:i]) for i in range(len(STEP_CHUNKS)))
NSTEP = len(STEP_CHUNKS)


def slot_views(s, slot, nch):
    v = [s.M[:, (slot * 3 + i) * PIECE:(slot * 3 + i) * PIECE + KC * nch * P] for i in range(3)]
    return (v[0].rearrange("p (k n) -> p k n", k=KC), v[1].rearrange("p (k n) -> p k n", k=KC),
            v[2].rearrange("p (c n) -> p c n", n=D))


def load_step(sp, s, e, step, w13_free=None, w2_free=None):
    slot, nch, f0 = step % SLOTS, STEP_CHUNKS[step], STEP_AT[step] * P
    v1, v3, v2 = slot_views(s, slot, nch)

    def of(w):
        return w[e] if isinstance(e, int) else w[ds(e, 1)].rearrange("a r n -> (a r) n")

    if w13_free:
        w13_free()
    for dst, name in ((v1, "w1"), (v3, "w3")):
        sp.dma_start(dst, of(s.a[name]).rearrange("(k p) n -> p k n", p=P)[:, :, f0:f0 + nch * P])\
            .then_inc(s.w13_in[slot], 16)
    if w2_free:
        w2_free()
    sp.dma_start(v2, of(s.a["w2"])[f0:f0 + nch * P, :].rearrange("(c p) n -> p c n", p=P))\
        .then_inc(s.w2_in[slot], 16)


def phase_experts(nc, s):
    a, K, V, PS, M, sem = s.a, s.K, s.V, s.PS, s.M, s.sem
    ar = Arena(M, s.n_main, RING)
    xe = ar.get(KC, CAP)
    xg, xgp = ar.get(D), ar.get(D, rows=CAP_P)
    yeT = ar.get(KC, CAP)
    ye, yep = ar.get(D), ar.get(D, rows=CAP_P)
    NB = 4
    sg = [ar.get(CAP) for _ in range(NB)]
    hid = [ar.get(CAP) for _ in range(NB)]
    ig, igp, iw, iwp = (s.lora_up[0:r, 2, o:o + 1].bitcast(I32)
                        for r, o in ((P, 0), (CAP_P, 1), (P, 2), (CAP_P, 3)))
    gt, gtp = s.lora_up[:, 2, 4:5], s.lora_up[0:CAP_P, 2, 5:6]
    accps = [PS[:, (m // 3) * 512 + (m % 3) * CAP:(m // 3) * 512 + (m % 3 + 1) * CAP] for m in range(KC)]
    hps = [PS[:, (3 + b) * 512:(3 + b) * 512 + 2 * CAP] for b in range(NB)]
    inps = [PS[:, (3 + k // 2) * 512 + (k % 2) * CAP:(3 + k // 2) * 512 + (k % 2 + 1) * CAP]
            for k in range(KC)]
    ops, opp = PS[:, 3 * 512:5 * 512], PS[0:CAP_P, 5 * 512:7 * 512]

    ixg, gath, turns = sem("gather_index"), sem("gathered"), sem("pool_turns_e")
    in_ps, xe_a, xe_d = sem("inputs_psum"), sem("inputs_by_act"), sem("inputs_by_dve")
    h_ps, sg_r, h_r = sem("hidden_psum"), sem("hidden_sigmoid"), sem("hidden_ready")
    dn_ps = sem("hidden_used")
    y_a, y_d, o_ps = (sem("expert_out_by_act"), sem("expert_out_by_dve"),
                              sem("expert_rows_psum"))
    gate_r, ye_a, ye_d = sem("gates_staged"), sem("rows_by_act"), sem("rows_by_dve")
    rows_free = sem("row_buffers_free")
    ixw, scat, dvo = sem("scatter_index"), sem("scattered"), sem("dve_own_d")

    with nc.Block() as block:

        @block.sync
        def _(sp):
            def reload(e, step, chunks):
                load_step(sp, s, e, step, lambda: sp.wait_ge(h_ps, chunks),
                          lambda: sp.wait_ge(dn_ps, chunks))

            def end(step):
                return STEP_AT[step] + STEP_CHUNKS[step]

            with sp.Fori(0, E - 1) as e:
                for step in range(SLOTS, NSTEP):
                    reload(e, step, e * NFC + end(step - SLOTS))
                for step in range(SLOTS):
                    reload(e + 1, step, e * NFC + end(step + NSTEP - SLOTS))
            for step in range(SLOTS, NSTEP):
                reload(E - 1, step, (E - 1) * NFC + end(step - SLOTS))

        @block.gpsimd
        def _(pool):
            def gather(e):
                nc.gpsimd.tensor_copy(ig, s.idxT[:, ds(e, 1)])
                nc.gpsimd.tensor_copy(igp, s.idxT[0:CAP_P, ds(e + PB, 1)]).then_inc(ixg, 1)
                hold(pool, turns, (ixg, e + 1))
                for dst, ix in ((xg, ig), (xgp, igp)):
                    nc.gpsimd.indirect_dma_start(dst, None, s.xn_d,
                                                 bass.IndirectOffsetOnAxis(ap=ix, axis=0))\
                        .then_inc(gath, 16)

            def scatter(e):
                nc.gpsimd.tensor_copy(iw, s.idxT[:, ds(e, 1)])
                nc.gpsimd.tensor_copy(iwp, s.idxT[0:CAP_P, ds(e + PB, 1)]).then_inc(ixw, 1)
                hold(pool, turns, (ixw, e + 1), (ye_a, e + 2), (ye_d, e + 2))
                for src, ix in ((ye, iw), (yep, iwp)):
                    nc.gpsimd.indirect_dma_start(s.acc_d, bass.IndirectOffsetOnAxis(ap=ix, axis=0),
                                                 src, None, compute_op=ALU.add).then_inc(scat, 16)
                pool.wait_ge(scat, e * 32 + 32)
                pool.sem_inc(rows_free, 1)

            pool.sem_inc(rows_free, 1)
            gather(0)
            with pool.Fori(0, E - 1) as e:
                hold(pool, turns, (in_ps, e + 1))
                gather(e + 1)
                scatter(e)
            scatter(E - 1)

        @block.tensor
        def _(pe):
            pe.sem_inc(h_r, NB)
            with pe.Fori(0, E) as e:
                pe.wait_ge(gath, e * 32 + 32)
                pe.wait_ge(h_r, e * NFC + NB)
                pe.wait_ge(ye_a, e + 1)
                pe.wait_ge(ye_d, e + 1)
                for k in range(KC):
                    nc.tensor.transpose(inps[k][:, 0:CAP_S], xg[:, k * P:(k + 1) * P], K["ident"])
                    last = nc.tensor.transpose(inps[k][:, CAP_S:CAP], xgp[:, k * P:(k + 1) * P],
                                               K["ident"][0:CAP_P, 0:CAP_P])
                last.then_inc(in_ps, 1)
                pe.wait_ge(xe_a, e + 1)
                pe.wait_ge(xe_d, e + 1)

                def up(ch, step):
                    c = ch - STEP_AT[step]
                    v1, v3, _ = slot_views(s, step % SLOTS, STEP_CHUNKS[step])
                    if c == 0:
                        pe.wait_ge(s.w13_in[step % SLOTS], e * 64 + (step // SLOTS * 32 + 32))
                    pe.wait_ge(h_r, e * NFC + (ch + 1))
                    for half, w in enumerate((v1, v3)):
                        for k in range(KC):
                            last = nc.tensor.matmul(hps[ch % NB][:, half * CAP:(half + 1) * CAP],
                                                    w[:, k, c * P:(c + 1) * P], xe[:, k, :],
                                                    start=(k == 0), stop=(k == KC - 1))
                    last.then_inc(h_ps, 1)

                def down(ch, step):
                    c = ch - STEP_AT[step]
                    v2 = slot_views(s, step % SLOTS, STEP_CHUNKS[step])[2]
                    if c == 0:
                        pe.wait_ge(s.w2_in[step % SLOTS], e * 32 + (step // SLOTS * 16 + 16))
                    pe.wait_ge(h_r, e * NFC + (ch + 1 + NB))
                    if ch == 0:
                        pe.wait_ge(y_a, e + 1)
                        pe.wait_ge(y_d, e + 1)
                    for m in range(KC):
                        last = nc.tensor.matmul(accps[m], v2[:, c, m * P:(m + 1) * P], hid[ch % NB],
                                                start=(ch == 0 and m % 3 == 0), stop=(ch == NFC - 1),
                                                skip_group_check=True)
                    last.then_inc(dn_ps, 1)

                of = [st for st in range(NSTEP) for _ in range(STEP_CHUNKS[st])]
                for ch in range(NFC + 1):
                    if ch < NFC:
                        up(ch, of[ch])
                    if ch >= 1:
                        down(ch - 1, of[ch - 1])
                pe.wait_ge(y_a, e + 2)
                pe.wait_ge(y_d, e + 2)
                for m in range(KC):
                    nc.tensor.transpose(ops[:, m * P:(m + 1) * P], yeT[:, m, 0:CAP_S], K["ident"])
                for m in range(KC):
                    last = nc.tensor.transpose(opp[:, m * P:(m + 1) * P], yeT[:, m, CAP_S:CAP],
                                               K["ident"])
                last.then_inc(o_ps, 1)


        @block.scalar
        def _(act):
            for sm in (y_a, ye_a):
                act.sem_inc(sm, 1)
            with act.Fori(0, E) as e:
                act.wait_ge(in_ps, e + 1)
                for k in range(4):
                    for g, c in ((0, slice(0, CAP_S)), (1, slice(CAP_S, CAP))):
                        last = nc.scalar.activation(xe[:, k, c], inps[k][:, c], ACT.Identity,
                                                    scale=s.A2[:, k, g:g + 1], bias=s.B2[:, k, g:g + 1])
                last.then_inc(xe_a, 1)
                for ch in range(NFC):
                    act.wait_ge(h_ps, e * NFC + (ch + 1))
                    nc.scalar.activation(sg[ch % NB], hps[ch % NB][:, 0:CAP], ACT.Sigmoid).then_inc(sg_r, 1)
                act.wait_ge(dn_ps, e * NFC + NFC)
                for m in range(3):
                    for g, c in ((0, slice(0, CAP_S)), (1, slice(CAP_S, CAP))):
                        last = nc.scalar.activation(yeT[:, m, c], accps[m][:, c], ACT.Copy,
                                                    scale=s.G2[:, m, g:g + 1])
                last.then_inc(y_a, 1)
                act.wait_ge(o_ps, e + 1)
                act.wait_ge(gate_r, e + 1)
                act.wait_ge(rows_free, e + 1)
                nc.scalar.activation(ye, ops, ACT.Copy, scale=gt).then_inc(ye_a, 1)

        @block.vector
        def _(dve):
            own = Chain(dve, dvo)
            for sm in (y_d, ye_d):
                dve.sem_inc(sm, 1)

            def body(e):
                dve.wait_ge(ye_a, e + 1)
                dve.wait_ge(ye_d, e + 1)
                nc.vector.tensor_copy(gt, s.gateT[:, ds(e, 1)])
                nc.vector.tensor_copy(gtp, s.gateT[0:CAP_P, ds(e + PB, 1)]).then_inc(gate_r, 1)
                dve.wait_ge(in_ps, e + 1)
                for k in range(4, KC):
                    for g, c in ((0, slice(0, CAP_S)), (1, slice(CAP_S, CAP))):
                        last = nc.vector.tensor_scalar(xe[:, k, c], inps[k][:, c], s.A2[:, k, g:g + 1],
                                                       s.B2[:, k, g:g + 1], ALU.mult, ALU.add)
                last.then_inc(xe_d, 1)
                for ch in range(NFC):
                    b = ch % NB
                    dve.wait_ge(sg_r, e * NFC + (ch + 1))
                    own.link(nc.vector.tensor_tensor(sg[b], sg[b], hps[b][:, 0:CAP], ALU.mult))
                    nc.vector.tensor_tensor(hid[b], sg[b], hps[b][:, CAP:2 * CAP], ALU.mult)\
                        .then_inc(h_r, 1)
                dve.wait_ge(dn_ps, e * NFC + NFC)
                for m in range(3, KC):
                    for g, c in ((0, slice(0, CAP_S)), (1, slice(CAP_S, CAP))):
                        last = nc.vector.tensor_scalar(yeT[:, m, c], accps[m][:, c],
                                                       s.G2[:, m, g:g + 1], None, ALU.mult)
                last.then_inc(y_d, 1)
                dve.wait_ge(o_ps, e + 1)
                dve.wait_ge(gate_r, e + 1)
                dve.wait_ge(rows_free, e + 1)
                nc.vector.tensor_scalar(yep, opp, gtp, None, ALU.mult).then_inc(ye_d, 1)

            looped(dve, own, 0, E, NFC, body)


def phase_final(nc, s):
    a, M, sem = s.a, s.M, s.sem
    ar = Arena(M, s.n_main)
    gf = ar.get(D)
    xt, yo, junk = [[ar.get(D) for _ in (0, 1)] for _ in range(3)]
    ssq, ms, root, rstd = [[s.st[:, i:i + 1] for i in (o, o + 1)] for o in (0, 2, 4, 8)]
    out_free = [sem(f"result_buffer_free{i}") for i in (0, 1)]
    g_in = sem("final_g_in")
    x_in = [sem(f"row_in{i}") for i in (0, 1)]
    y_out = [sem(f"result_written{i}") for i in (0, 1)]
    sq_r, ms_r, rt_r, rr_r, y_r = (sem("final_squared"), sem("final_mean_square"), sem("final_root"),
                                   sem("final_rstd"), sem("result_ready"))

    with nc.Block() as block:

        @block.sync
        def _(sp):
            sp.dma_start(gf, a["final_g"].to_broadcast([P, D])).then_inc(g_in, 16)
            for i in (0, 1):
                sp.sem_inc(out_free[i], 1)
                sp.dma_start(xt[i], s.acc_d[i * P:(i + 1) * P, :]).then_inc(x_in[i], 16)
            with sp.Fori(0, NT // 2 - 1) as j:
                for i in (0, 1):
                    sp.wait_ge(y_r, j * 2 + (i + 1))
                    sp.dma_start(a["out_y"][ds(j * (2 * P) + i * P, P), :], yo[i]).then_inc(y_out[i], 16)
                    sp.dma_start(xt[i], s.acc_d[ds(j * (2 * P) + (i + 2) * P, P), :])\
                        .then_inc(x_in[i], 16)
                for i in (0, 1):
                    sp.wait_ge(y_out[i], j * 16 + 16)
                    sp.sem_inc(out_free[i], 1)
            for i in (0, 1):
                n = NT - 2 + i
                sp.wait_ge(y_r, n + 1)
                sp.dma_start(a["out_y"][n * P:(n + 1) * P, :], yo[i]).then_inc(y_out[i], 16)
            for i in (0, 1):
                sp.wait_ge(y_out[i], 16 * (NT // 2))

        @block.scalar
        def _(act):
            with act.Fori(0, NT // 2) as j:
                for i in (0, 1):
                    act.wait_ge(x_in[i], j * 16 + 16)
                    nc.scalar.activation(junk[i], xt[i], ACT.Square, accum_out=ssq[i]).then_inc(sq_r, 1)
                for i in (0, 1):
                    act.wait_ge(ms_r, j * 2 + (i + 1))
                    nc.scalar.activation(root[i], ms[i], ACT.Sqrt).then_inc(rt_r, 1)

        @block.vector
        def _(dve):
            dve.wait_ge(g_in, 16)
            with dve.Fori(0, NT // 2) as j:
                for i in (0, 1):
                    dve.wait_ge(sq_r, j * 2 + (i + 1))
                    nc.vector.tensor_scalar(ms[i], ssq[i], 1.0 / D, RMS_EPS, ALU.mult, ALU.add)\
                        .then_inc(ms_r, 1)
                for i in (0, 1):
                    dve.wait_ge(rt_r, j * 2 + (i + 1))
                    nc.vector.reciprocal(rstd[i], root[i]).then_inc(rr_r, 1)
                    dve.wait_ge(rr_r, j * 2 + (i + 1))
                    dve.wait_ge(out_free[i], j + 1)
                    nc.vector.scalar_tensor_tensor(out=yo[i], in0=xt[i], scalar=rstd[i], in1=gf,
                                                   op0=ALU.mult, op1=ALU.mult).then_inc(y_r, 1)


_OUT = (("out_y", (T, D)), ("out_state", (2, NH, HS, HS)))


def kernel(x_prompt, x_sample, state_wkv, c, c_ctx, norm1_g, norm2_g, w_mod, b_mod, w_in, conv_dw, conv_b,
           conv_ln_g, conv_ln_b, rwkv_w0, rwkv_w_up, rwkv_a0, rwkv_a_up, rwkv_g_up, rwkv_k_k, rwkv_k_a,
           rwkv_r_k, rwkv_gn_g, rwkv_gn_b, w_out, router, exp_w1, exp_w3, exp_w2, final_norm_g):
    import numpy as _np
    import concourse.bacc as _bacc
    from concourse import mybir as _mybir
    from concourse.bass_utils import run_bass_kernel_spmd as _run

    def columns(v):
        return _np.asarray(v).reshape(-1, P).T

    taps = _np.asarray(conv_dw)[0].reshape(KW, NP_, P).transpose(2, 1, 0).reshape(P, NP_ * KW)
    bias = _np.concatenate([columns(v) for d in (0, 1) for v in (rwkv_w0[0, d], rwkv_a0[0, d])], 1)
    cond = _np.stack([columns(c[0]), columns(c_ctx)], 2).reshape(P, 16)
    vectors = _np.concatenate([columns(norm1_g[0]), columns(norm2_g[0]), columns(b_mod[0]), taps,
                               columns(conv_b[0]), columns(conv_ln_g[0]), columns(conv_ln_b[0]), bias,
                               columns(rwkv_k_k[0]), columns(rwkv_k_a[0]), columns(rwkv_r_k[0].reshape(-1)),
                               columns(rwkv_gn_g[0]), columns(rwkv_gn_b[0]), cond], 1)
    arrays = {
        "x": _np.concatenate([_np.asarray(x_sample)[0], _np.asarray(x_prompt)[0]], 0),
        "vectors": vectors, "table": _np.concatenate(list(constant_table().values()), 1),
        "w_mod": w_mod[0], "w_in": w_in[0], "w_up": rwkv_w_up[0], "a_up": rwkv_a_up[0],
        "g_up": rwkv_g_up[0], "state": state_wkv[0, 0], "w_out": w_out[0], "router": router[0],
        "w1": exp_w1[0], "w3": exp_w3[0], "w2": exp_w2[0],
        "final_g": _np.asarray(final_norm_g).reshape(1, D),
    }
    nc = _bacc.Bacc("TRN2", target_bir_lowering=False, num_devices=1)
    f32 = _mybir.dt.float32
    data, a = {}, {}
    for name, v in arrays.items():
        data[f"in_{name}"] = _np.ascontiguousarray(v)
        a[name] = nc.dram_tensor(f"in_{name}", data[f"in_{name}"].shape, f32, kind="ExternalInput").ap()
    for name, shape in _OUT:
        a[name] = nc.dram_tensor(name, shape, f32, kind="ExternalOutput").ap()
    build(nc, a)
    r = _run(nc, [data], core_ids=[0]).results[0]
    y, state = r["out_y"], r["out_state"]
    return y[None, TS:], y[None, :TS], state[None, None]
```

```python
import concourse.bass as bass
from concourse import mybir
from contextlib import ExitStack
import numpy as np

P = 128
D = 1024
KC = D // P
TS, TP = 1024, 256
T = TS + TP
NT = T // P
NTS = TS // P
CW = 512
NP_ = CW // P
HS = 64
NH = CW // HS
KW = 31
PAD = (KW - 1) // 2
GRID = 64
WIN = GRID + 2 * PAD
NWIN = T // GRID
C = 64
NCH = T // C
NCS = TS // C
NCP = TP // C
E = 16
FF = 2816
NFC = FF // P
CAP_S = 2 * TS // E
CAP_P = 2 * TP // E
CAP = CAP_S + CAP_P
PB = 32
LEVELS = (2, 4, 8, 16, 32)
C0 = float(np.exp(-0.5))
RMS_EPS, LN_EPS, GN_EPS = 1e-6, 1e-5, 64e-5
STEP_CHUNKS = (4, 4, 4, 4, 3, 3)
SLOTS = 3
COLS3 = ((0, 512), (512, 512), (1024, 256))


def constant_table():
    t = {}
    i = np.arange(P)
    ident = np.eye(P, dtype=np.float32)
    t["ident"] = ident
    same = (i[:, None] // HS == i[None] // HS)
    t["blockones"] = same.astype(np.float32)
    t["fold"] = (i[:, None] % HS == np.arange(HS)[None]).astype(np.float32)
    t["lnmean"] = np.full((P, P), 1.0 / CW, np.float32)
    r, c = i[:, None] % C, i[None] % C
    for d in (0, 1):
        before = (r < c) if d == 0 else (r > c)
        t[f"strict{d}"] = (same & before).astype(np.float32)
        t[f"incl{d}"] = (same & (before | (r == c))).astype(np.float32)
        after = (r > c) if d == 0 else (r < c)
        for b in (1,) + LEVELS:
            off = (r // (2 * b) == c // (2 * b)) & (r // b != c // b)
            m = ident - (same & after & off)
            t[f"lev{d}_{b}"] = m.astype(np.float32)
            col = np.arange(HS)[None]
            rr = i[:, None] % C
            aft = (rr > col) if d == 0 else (rr < col)
            of = (rr // (2 * b) == col // (2 * b)) & (rr // b != col // b)
            mc = (rr == col).astype(np.float32) - (aft & of)
            t[f"levc{d}_{b}"] = mc.astype(np.float32)
            if b == 1:
                t[f"first{d}"] = m.T.astype(np.float32)
                t[f"firstc{d}"] = (-(aft & of).astype(np.float32))
                del t[f"lev{d}_1"], t[f"levc{d}_1"]
    reset = np.ones((P, NP_ * C), np.float32)
    reset[:, ::C] = 0
    t["reset"] = reset
    return t


def table_columns(t):
    at, cols = 0, {}
    for n, a in t.items():
        cols[n] = (at, a.shape[1])
        at += a.shape[1]
    return cols, at


VECTORS = (("n1", 8), ("n2", 8), ("bmod", 48), ("dw", NP_ * KW), ("db", 4), ("lng", 4), ("lnb", 4),
           ("bias_wa", 16), ("k_k", 4), ("k_a", 4), ("r_k", 4), ("gng", 4), ("gnb", 4), ("cond", 16))


class Chain:

    def __init__(self, eng, sem):
        self.eng, self.sem, self.n, self.at, self.last = eng, sem, 0, 0, None

    def link(self, ins):
        self.n += 1
        ins.then_inc(self.sem, 1)
        self.eng.wait_ge(self.sem, self.at + self.n)
        self.last = ins
        return ins


class Shared:
    pass


class Arena:

    def __init__(self, main, size, at=0):
        self.main, self.size, self.at = main, size, at

    def get(self, *shape, rows=P):
        n = int(np.prod(shape))
        v = self.main[0:rows, self.at:self.at + n]
        self.at += n
        assert self.at <= self.size, (self.at, self.size)
        if len(shape) == 2:
            v = v.rearrange("p (a b) -> p a b", b=shape[1])
        if len(shape) == 3:
            v = v.rearrange("p (a b c) -> p a b c", b=shape[1], c=shape[2])
        return v


def hold(pool, turns, *waits):
    for sm, value in waits:
        pool.wait_ge(sm, value)
        pool.sem_inc(turns, 1)


F32, I32, U32 = mybir.dt.float32, mybir.dt.int32, mybir.dt.uint32
ALU, ACT, AX = mybir.AluOpType, mybir.ActivationFunctionType, mybir.AxisListType
ds = bass.ds


def build(nc, a, phases=5):
    with ExitStack() as ctx:
        s = Shared()
        s.a = a

        def sem(name):
            return ctx.enter_context(nc.semaphore(name))

        def dram(name, shape):
            return nc.dram_tensor(name, shape, F32, kind="Internal").ap()

        def small(name, shape, dt=F32):
            return ctx.enter_context(nc.sbuf_tensor(name, shape, dt))

        s.sem, s.small = sem, small
        s.g1_d = dram("gate1_rows", (2, D))
        s.conv_d = dram("conv_out", (P, NP_ * T))
        s.y_d = dram("wkv_out", (2, NCH, P, NP_ * HS))
        s.xg_d = dram("gate_lora", (P, T))
        s.kd_d = dram("keys_out", (2, P, NP_, T))
        s.xn_d = dram("normed_rows", (T, D))
        s.acc_d = dram("residual_rows", (T, D))

        cols, n_const = table_columns(constant_table())
        s.consts = small("consts", [P, n_const])
        s.K = {n: s.consts[:, o:o + w] for n, (o, w) in cols.items()}
        s.vecs = small("vecs", [P, sum(w for _, w in VECTORS)])
        s.V, at = {}, 0
        for n, w in VECTORS:
            s.V[n] = s.vecs[:, at:at + w]
            at += w
        s.condT = small("condT", [P, KC, 2])
        s.modT = small("modT", [P, 48, 2])
        s.A1, s.A2 = small("A1", [P, KC, 2]), small("A2", [P, KC, 2])
        s.lora_up = small("lora_up", [P, 4, CW])
        s.st = small("row_stats", [P, 12])
        s.taps = small("taps", [P, KW])
        s.B1, s.B2, s.G2 = s.modT[:, 0:8, :], s.modT[:, 24:32, :], s.modT[:, 40:48, :]
        s.gateT, s.idxF = s.lora_up[:, 0, 0:64], s.lora_up[:, 0, 64:128]
        s.idxT = s.lora_up[:, 0, 128:192].bitcast(I32)
        s.w13_in = [sem(f"w1_w3_in{i}") for i in range(SLOTS)]
        s.w2_in = [sem(f"w2_in{i}") for i in range(SLOTS)]
        n_main = (nc.sbuf_usable_end - nc.sbuf_base) // 4 - 64
        s.M = small("main", [P, n_main])
        s.n_main = n_main
        s.PS = ctx.enter_context(nc.psum_tensor("PS", [P, 8 * 512], F32))
        s.ar = Arena(s.M, n_main)
        s.rkv = s.ar.get(3 * NP_, T)
        s.rT, s.kT, s.vT = s.rkv[:, 0:4, :], s.rkv[:, 4:8, :], s.rkv[:, 8:12, :]
        s.loraT = s.ar.get(2, T)
        s.mark = s.ar.at
        for phase in (phase_project, phase_wkv, phase_mix, phase_experts, phase_final)[:phases]:
            own = []

            def phase_sem(name, own=own):
                own.append(nc.alloc_semaphore(name))
                return own[-1]

            s.sem = phase_sem
            phase(nc, s)
            nc.clear_and_free_semaphores(own)
            nc.all_engine_barrier()


def phase_project(nc, s):
    a, K, V, PS, M, sem = s.a, s.K, s.V, s.PS, s.M, s.sem
    ar = Arena(M, s.n_main, s.mark)
    hT = ar.get(KC, T)
    late = [M[:, s.mark + i * 4096:s.mark + (i + 1) * 4096].rearrange("p (k n) -> p k n", n=512)
            for i in range(2)]
    mark = ar.at
    u = ar.get(NP_, NWIN * WIN)
    sq = M[:, mark:mark + NP_ * T].rearrange("p (k n) -> p k n", n=T)
    lrs = M[:, mark + NP_ * T:mark + NP_ * T + T]
    mark = ar.at
    cv = ar.get(NP_, T)
    xt = [M[:, mark + i * D:mark + (i + 1) * D] for i in (0, 1)]
    xn = [M[:, mark + i * D:mark + (i + 1) * D] for i in (2, 3)]
    junk = [M[:, mark + 4 * D:mark + 5 * D], s.loraT[:, 0, 0:D]]
    ws = [ar.get(KC, P) for _ in range(4)]
    xgT = ar.get(T)
    slab = [M[:, i * 4096:(i + 1) * 4096].rearrange("p (k n) -> p k n", n=512) for i in range(2)]
    ge = [s.rkv[:, i, :] for i in (0, 1)]
    modps = PS[:, 6 * 512:6 * 512 + 96].rearrange("p (m j) -> p m j", j=2)
    trp = [PS[:, 0:1024], PS[:, 1024:2048]]
    pset = [PS[:, 0:T], PS[:, 3 * 512:3 * 512 + T]]
    w_mod = a["w_mod"].rearrange("(k p) n -> p k n", p=P)
    w_in = a["w_in"].rearrange("(k p) n -> p k n", p=P)
    ssq = [s.st[:, i:i + 1] for i in (0, 1)]
    ms = [s.st[:, i:i + 1] for i in (2, 3)]
    root = [s.st[:, i:i + 1] for i in (4, 5)]
    rstd = [s.st[:, i:i + 1] for i in (8, 9)]
    BODY, FULL = 4, 5
    NPC = 23

    tables, ups, zero = sem("tables_loaded"), sem("up_weights_loaded"), sem("zeros_written")
    x_in = [sem(f"x_in{i}") for i in range(2)]
    mod_in = [sem(f"w_mod_in{i}") for i in range(2)]
    late_in = [sem(f"w_mod_late_in{i}") for i in range(2)]
    mod_used, late_used = sem("w_mod_used"), sem("w_mod_late_used")
    cond_sig, cond_ready, mod_ready = sem("cond_sigmoid"), sem("cond_ready"), sem("mod_ready")
    sq_done, ms_done, rs_done = sem("row_squares"), sem("row_mean_square"), sem("row_root")
    rr_done = sem("row_rstd")
    xn_done, tr_done = sem("xn_ready"), sem("x_transposed")
    h_act, h_dve = sem("h_by_act"), sem("h_by_dve")
    win = [sem(f"w_in_in{i}") for i in range(4)]
    pr_done = sem("projected")
    free = [sem(f"psum_set_free{i}") for i in range(2)]
    gate_sig, u_done = sem("gate_sigmoid"), sem("u_ready")
    xg_out = sem("gate_lora_written")
    g1_ready, g1_out = sem("g1_ready"), sem("g1_written")
    dvo, conv_own = sem("dve_own_a"), sem("taps_staged")
    conv_done, mean_ps, cen = sem("conv_summed"), sem("ln_mean_psum"), sem("ln_centered")
    csq, var_ps, var_done, lrs_done = (sem("ln_squared"), sem("ln_var_psum"), sem("ln_var"),
                                       sem("ln_rstd"))
    scaled, aff_done, sil_sig, cout = (sem("ln_scaled"), sem("ln_affine"), sem("silu_sigmoid"),
                                       sem("conv_out_ready"))
    conv_spill = sem("conv_written")

    with nc.Block() as block:

        @block.sync
        def _(sp):
            sp.dma_start(s.vecs[:, :], a["vectors"]).then_inc(tables, 16)
            sp.dma_start(s.consts[:, :], a["table"]).then_inc(tables, 16)
            for i in range(2):
                sp.dma_start(slab[i], w_mod[:, :, i * 512:(i + 1) * 512]).then_inc(mod_in[i], 16)
            for i in range(2):
                sp.dma_start(xt[i], a["x"][i * P:(i + 1) * P, :]).then_inc(x_in[i], 16)
            for i in range(2):
                sp.wait_ge(mod_used, i + 1)
                sp.dma_start(slab[i], w_mod[:, :, (i + 2) * 512:(i + 3) * 512]).then_inc(mod_in[i], 16)
            sp.wait_ge(zero, 1)
            for d in (0, 1):
                sp.dma_start(s.lora_up[d * HS:(d + 1) * HS, d, :], a["w_up"][d]).then_inc(ups, 16)
                sp.dma_start(s.lora_up[d * HS:(d + 1) * HS, 2 + d, :], a["a_up"][d]).then_inc(ups, 16)
            with sp.Fori(1, NT // 2) as j:
                for i in range(2):
                    sp.wait_ge(xn_done, j * 2 + (i - 1))
                    sp.dma_start(xt[i], a["x"][ds(j * (2 * P) + i * P, P), :]).then_inc(x_in[i], 16)
            for n, ch in enumerate((4, 0, 5, 1, 6, 2, 7, 3)):
                if n >= 4:
                    sp.wait_ge(pr_done, n - 3)
                sp.dma_start(ws[n % 4], w_in[:, :, ch * P:(ch + 1) * P]).then_inc(win[n % 4], 16)
            with sp.Fori(2, FULL) as j:
                for i in range(4):
                    sp.wait_ge(pr_done, j * 4 + (i - 3))
                    sp.dma_start(ws[i], w_in[:, :, ds(j * 512 + i * P, P)]).then_inc(win[i], 16)
            for n in range(4 * FULL, NPC):
                sp.wait_ge(pr_done, n - 3)
                sp.dma_start(ws[n % 4], w_in[:, :, n * P:(n + 1) * P]).then_inc(win[n % 4], 16)
            sp.wait_ge(pr_done, NPC)
            for i in range(2):
                sp.dma_start(late[i], w_mod[:, :, (4 + i) * 512:(5 + i) * 512]).then_inc(late_in[i], 16)
            with sp.Fori(1, 4) as j:
                for i in range(2):
                    sp.wait_ge(late_used, j * 2 + (i - 1))
                    sp.dma_start(late[i], w_mod[:, :, ds(j * 1024 + (4 + i) * 512, 512)])\
                        .then_inc(late_in[i], 16)
            sp.wait_ge(free[0], 13)
            sp.dma_start(s.xg_d, xgT).then_inc(xg_out, 16)
            sp.wait_ge(g1_ready, 1)
            for j in range(2):
                sp.dma_start(s.g1_d[j].rearrange("(k p) -> p k", p=P), s.modT[:, 16:24, j],
                             allow_slow_non_contiguous=True).then_inc(g1_out, 16)
            sp.wait_ge(g1_out, 32)
            sp.wait_ge(cout, NP_)
            sp.dma_start(s.conv_d, cv.rearrange("p a b -> p (a b)")).then_inc(conv_spill, 16)
            sp.wait_ge(conv_spill, 16)
            sp.wait_ge(ups, 64)
            sp.wait_ge(xg_out, 16)

        @block.gpsimd
        def _(pool):
            nc.gpsimd.memset(s.lora_up[:, :, :], 0.0).then_inc(zero, 1)
            nc.gpsimd.memset(u[:, :, :], 0.0).then_inc(zero, 1)

        @block.tensor
        def _(pe):
            for sm in (h_act, h_dve):
                pe.sem_inc(sm, 2)
            for sm in free:
                pe.sem_inc(sm, 1)

            def modulate(weights, col0, used):
                for m in range(4):
                    for k in range(KC):
                        last = nc.tensor.matmul(modps[:, col0 + m, :],
                                                weights[:, k, m * P:(m + 1) * P], s.condT[:, k, :],
                                                start=(k == 0), stop=(k == KC - 1))
                last.then_inc(used, 1)

            pe.wait_ge(cond_ready, 1)
            for n in range(4):
                pe.wait_ge(mod_in[n % 2], 16 * (n // 2 + 1))
                modulate(slab[n % 2], 4 * n, mod_used)

            def transposes(j):
                for i in range(2):
                    pe.wait_ge(xn_done, j * 2 + (i + 1))
                    pe.wait_ge(h_act, j * 2 + (i + 1))
                    pe.wait_ge(h_dve, j * 2 + (i + 1))
                    for k in range(KC):
                        last = nc.tensor.transpose(trp[i][:, k * P:(k + 1) * P],
                                                   xn[i][:, k * P:(k + 1) * P], K["ident"])
                    last.then_inc(tr_done, 1)

            with pe.Fori(0, NT // 2) as j:
                transposes(j)
            pe.wait_ge(h_act, NT + 2)
            pe.wait_ge(h_dve, NT + 2)

            def project(j, i):
                pe.wait_ge(win[i], j * 16 + 16)
                pe.wait_ge(free[i % 2], j * 2 + (i // 2 + 1))
                for c0, w in COLS3:
                    for k in range(KC):
                        last = nc.tensor.matmul(pset[i % 2][:, c0:c0 + w], ws[i][:, k, :],
                                                hT[:, k, c0:c0 + w], start=(k == 0), stop=(k == KC - 1))
                last.then_inc(pr_done, 1)

            with pe.Fori(0, FULL) as j:
                for i in range(BODY):
                    project(j, i)
            for i in range(NPC - BODY * FULL):
                project(FULL, i)

            pe.wait_ge(conv_done, NP_)
            pe.wait_ge(free[0], 13)
            pe.wait_ge(free[1], 12)
            for c0, w in COLS3:
                for k in range(NP_):
                    last = nc.tensor.matmul(PS[:, c0:c0 + w], K["lnmean"], cv[:, k, c0:c0 + w],
                                            start=(k == 0), stop=(k == NP_ - 1))
            last.then_inc(mean_ps, 1)
            for n in range(8):
                pe.wait_ge(late_in[n % 2], 16 * (n // 2 + 1))
                modulate(late[n % 2], 16 + 4 * n, late_used)
            for k in range(NP_):
                pe.wait_ge(csq, k + 1)
                for c0, w in COLS3:
                    last = nc.tensor.matmul(PS[:, 3 * 512 + c0:3 * 512 + c0 + w], K["lnmean"],
                                            sq[:, k, c0:c0 + w], start=(k == 0), stop=(k == NP_ - 1))
            last.then_inc(var_ps, 1)

        @block.scalar
        def _(act):
            act.wait_ge(tables, 32)
            cond = V["cond"].rearrange("p (k j) -> p k j", j=2)
            nc.scalar.activation(s.condT[:, :, :], cond, ACT.Sigmoid).then_inc(cond_sig, 1)

            def pair(j, g):
                for i in range(2):
                    act.wait_ge(x_in[i], j * 16 + 16)
                    nc.scalar.activation(junk[i], xt[i], ACT.Square, accum_out=ssq[i]).then_inc(sq_done, 1)
                for i in range(2):
                    act.wait_ge(ms_done, j * 2 + (i + 1))
                    nc.scalar.activation(root[i], ms[i], ACT.Sqrt).then_inc(rs_done, 1)
                for i in range(2):
                    act.wait_ge(tr_done, j * 2 + (i + 1))
                    for k in range(4):
                        last = nc.scalar.activation(hT[:, k, ds(j * (2 * P) + i * P, P)],
                                                    trp[i][:, k * P:(k + 1) * P], ACT.Identity,
                                                    scale=s.A1[:, k, g:g + 1], bias=s.B1[:, k, g:g + 1])
                    last.then_inc(h_act, 1)

            act.wait_ge(mod_ready, 1)
            with act.Fori(0, NTS // 2) as j:
                pair(j, 0)
            pair(NTS // 2, 1)

            with act.Fori(0, 4) as j:
                act.wait_ge(pr_done, j * 2 + 1)
                act.wait_ge(u_done, j + 1)
                nc.scalar.activation(ge[0], pset[0], ACT.Sigmoid).then_inc(gate_sig, 1)
                act.wait_ge(gate_sig, j + 1)
                act.sem_inc(free[0], 1)
            act.wait_ge(u_done, 5)
            with act.Fori(0, 6) as j:
                for i in range(2):
                    act.wait_ge(pr_done, j * 2 + (9 + i))
                    nc.scalar.activation(s.rkv[:, ds(j * 2 + i, 1), :].rearrange("p a b -> p (a b)"),
                                         pset[i], ACT.Copy).then_inc(free[i], 1)
            for n, fn in enumerate((ACT.Tanh, ACT.Copy, ACT.Sigmoid)):
                act.wait_ge(pr_done, 21 + n)
                nc.scalar.activation(s.loraT[:, n, :] if n < 2 else xgT, pset[n % 2], fn)\
                    .then_inc(free[n % 2], 1)
            for k in range(NP_):
                act.wait_ge(cen, k + 1)
                nc.scalar.activation(sq[:, k, :], cv[:, k, :], ACT.Square).then_inc(csq, 1)
            act.wait_ge(var_done, 1)
            nc.scalar.activation(lrs, lrs, ACT.Sqrt).then_inc(lrs_done, 1)
            for k in range(NP_):
                act.wait_ge(scaled, k + 1)
                nc.scalar.activation(cv[:, k, :], cv[:, k, :], ACT.Identity, scale=V["lng"][:, k:k + 1],
                                     bias=V["lnb"][:, k:k + 1]).then_inc(aff_done, 1)
                act.wait_ge(aff_done, k + 1)
                nc.scalar.activation(sq[:, k, :], cv[:, k, :], ACT.Sigmoid).then_inc(sil_sig, 1)

        @block.vector
        def _(dve):
            own = Chain(dve, dvo)
            dve.sem_inc(u_done, 1)
            cond = V["cond"].rearrange("p (k j) -> p k j", j=2)
            dve.wait_ge(cond_sig, 1)
            nc.vector.tensor_tensor(s.condT[:, :, :], s.condT[:, :, :], cond, ALU.mult)\
                .then_inc(cond_ready, 1)

            def mod_out(lo, n):
                b = V["bmod"][:, lo:lo + n].unsqueeze(2).to_broadcast([P, n, 2])
                return nc.vector.tensor_tensor(s.modT[:, lo:lo + n, :], modps[:, lo:lo + n, :], b, ALU.add)

            def one_plus_times(out, sc, norm):
                g = norm.unsqueeze(2).to_broadcast([P, KC, 2])
                return nc.vector.scalar_tensor_tensor(out=out[:, :, :], in0=sc, scalar=1.0, in1=g,
                                                      op0=ALU.add, op1=ALU.mult)

            dve.wait_ge(mod_used, 4)
            own.link(mod_out(0, 16))
            one_plus_times(s.A1, s.modT[:, 8:16, :], V["n1"]).then_inc(mod_ready, 1)
            dve.wait_ge(mod_ready, 1)

            def pair(j, g):
                for i in range(2):
                    dve.wait_ge(sq_done, j * 2 + (i + 1))
                    nc.vector.tensor_scalar(ms[i], ssq[i], 1.0 / D, RMS_EPS, ALU.mult, ALU.add)\
                        .then_inc(ms_done, 1)
                for i in range(2):
                    dve.wait_ge(rs_done, j * 2 + (i + 1))
                    nc.vector.reciprocal(rstd[i], root[i]).then_inc(rr_done, 1)
                    dve.wait_ge(rr_done, j * 2 + (i + 1))
                    nc.vector.tensor_scalar(xn[i], xt[i], rstd[i], None, ALU.mult).then_inc(xn_done, 1)
                for i in range(2):
                    dve.wait_ge(tr_done, j * 2 + (i + 1))
                    for k in range(4, KC):
                        last = nc.vector.tensor_scalar(hT[:, k, ds(j * (2 * P) + i * P, P)],
                                                       trp[i][:, k * P:(k + 1) * P],
                                                       s.A1[:, k, g:g + 1], s.B1[:, k, g:g + 1],
                                                       ALU.mult, ALU.add)
                    last.then_inc(h_dve, 1)

            with dve.Fori(0, NTS // 2) as j:
                pair(j, 0)
            pair(NTS // 2, 1)

            dve.wait_ge(zero, 2)
            base, n0 = own.n, 2
            with dve.Fori(0, NP_) as j:
                own.at = j * n0
                dve.wait_ge(gate_sig, j + 1)
                dve.wait_ge(pr_done, j * 2 + 2)
                uc = u[:, ds(j, 1), :].rearrange("p a (w x) -> p (a w) x", x=WIN)
                own.link(nc.vector.tensor_tensor(
                    uc[:, :, PAD:PAD + GRID], ge[0].rearrange("p (w x) -> p w x", x=GRID),
                    pset[1].rearrange("p (w x) -> p w x", x=GRID), ALU.mult))
                dve.sem_inc(free[1], 1)
                w0 = TS // GRID
                nc.vector.tensor_copy(uc[:, w0 + 1:NWIN, 0:PAD], uc[:, w0:NWIN - 1, GRID:GRID + PAD])
                own.link(nc.vector.tensor_copy(uc[:, w0:NWIN - 1, PAD + GRID:WIN],
                                               uc[:, w0 + 1:NWIN, PAD:2 * PAD]))
                dve.sem_inc(u_done, 1)
            assert own.n == base + n0
            own.n, own.at = base + n0 * NP_, 0
            base = own.n
            with dve.Fori(0, NP_) as j:
                own.at = j * KW
                uc = u[:, ds(j, 1), :].rearrange("p a (w x) -> p (a w) x", x=WIN)
                out = cv[:, ds(j, 1), :].rearrange("p a (w x) -> p (a w) x", x=GRID)
                nc.vector.tensor_copy(s.st[:, 6:7], V["db"][:, ds(j, 1)]).then_inc(conv_own, 1)
                taps = s.taps
                nc.vector.tensor_copy(taps[:, :], V["dw"][:, ds(j * KW, KW)]).then_inc(conv_own, 1)
                dve.wait_ge(conv_own, j * 2 + 2)
                for k in range(KW):
                    src = uc[:, :, k:k + GRID]
                    if k == 0:
                        ins = nc.vector.tensor_scalar(out, src, taps[:, 0:1], s.st[:, 6:7],
                                                      ALU.mult, ALU.add)
                    else:
                        ins = nc.vector.scalar_tensor_tensor(out=out, in0=src, scalar=taps[:, k:k + 1],
                                                             in1=out, op0=ALU.mult, op1=ALU.add)
                    own.link(ins)
                dve.sem_inc(conv_done, 1)
            own.n, own.at = base + NP_ * KW, 0
            dve.wait_ge(mean_ps, 1)
            for k in range(NP_):
                nc.vector.tensor_tensor(cv[:, k, :], cv[:, k, :], PS[:, 0:T], ALU.subtract)\
                    .then_inc(cen, 1)
            dve.wait_ge(late_used, 8)
            own.link(mod_out(16, 32))
            dve.sem_inc(g1_ready, 1)
            own.link(one_plus_times(s.A2, s.modT[:, 32:40, :], V["n2"]))
            dve.wait_ge(var_ps, 1)
            nc.vector.tensor_scalar(lrs, PS[:, 3 * 512:3 * 512 + T], LN_EPS, None, ALU.add)\
                .then_inc(var_done, 1)
            dve.wait_ge(lrs_done, 1)
            own.link(nc.vector.reciprocal(lrs, lrs))
            for k in range(NP_):
                nc.vector.tensor_tensor(cv[:, k, :], cv[:, k, :], lrs, ALU.mult).then_inc(scaled, 1)
            for k in range(NP_):
                dve.wait_ge(sil_sig, k + 1)
                nc.vector.tensor_tensor(cv[:, k, :], cv[:, k, :], sq[:, k, :], ALU.mult).then_inc(cout, 1)


def looped(eng, own, lo, hi, links, body):
    base = own.n
    with eng.Fori(lo, hi) as i:
        own.at = i * links + (-lo * links)
        body(i)
    assert own.n == base + links, (own.n - base, links)
    own.n, own.at = base + (hi - lo) * links, 0


def phase_wkv(nc, s):
    a, K, V, PS, M, sem = s.a, s.K, s.V, s.PS, s.M, s.sem
    ar = Arena(M, s.n_main, s.mark)
    PC = NP_ * C
    kk = ar.get(NP_, T)
    kk_flat = kk.rearrange("p a b -> p (a b)")
    at_work = ar.at
    two = (0, 1)

    def pair_of(*shape):
        return [ar.get(*shape) for _ in two]

    wa = pair_of(2, NP_, C)
    cum = pair_of(2, NP_, C)
    inv = pair_of(NP_, C)
    kd = pair_of(NP_, C)
    ba = pair_of(NP_, C)
    kr = pair_of(NP_, 2 * C)
    bet = pair_of(NP_, C)
    key = pair_of(NP_, C)
    at_bd = ar.at
    bds = {n: pair_of(NP_, P) for n in ("AT", "M", "P", "Q", "Z", "NT", "NI", "keyt", "bett",
                                        "kap", "rho", "bet", "key", "val")}
    N, Z = pair_of(NP_, C), pair_of(NP_, C)
    wc = [ar.get(NP_) for _ in two]
    Vt, X, U, S = pair_of(NP_, HS), pair_of(NP_, HS), pair_of(NP_, HS), pair_of(NP_, HS)
    Yo = X
    S_next = ar.get(NP_, HS)
    S_keep = ar.get(NP_, HS)
    fin = bds["P"][0]
    st_rows = M[0:HS, at_bd:at_bd + 2 * NH * HS].rearrange("p (d n) -> p d n", d=2)
    sqt = [bds["bett"][i].rearrange("p a b -> p (a b)") for i in two]
    root_t = M[:, at_work:at_work + NP_ * T]
    BA, BB, BC, BD = [[PS[:, (4 * d + b) * 512:(4 * d + b + 1) * 512] for d in two] for b in range(4)]

    def both(name):
        return [sem(f"{name}{d}") for d in two]

    dvo, ready = sem("dve_own_b"), sem("kk_ready")
    zeroed, turns = sem("bd_zeroed"), sem("pool_turns")
    st_loaded, st_ps, st_set = sem("state_loaded"), sem("state_transposed"), sem("state_set")
    kraw, ksq, kn_ps, kn, kroot = (sem("kk_raw"), sem("kk_squared"), sem("kk_norm_psum"),
                                   sem("kk_norm"), sem("kk_root"))
    aw, t1b, t1t = both("lora_out"), both("lora_biased"), both("lora_tanh")
    inv_e = both("inv_ready")
    cr, er, kdr = both("sums_ready"), both("exps_ready"), both("kd_ready")
    krr, bkr = both("kap_rho_ready"), both("bet_key_ready")
    vbd, kbd, rbd, bbd, kyb = (both("v_bd_ready"), both("kap_bd_ready"), both("rho_bd_ready"),
                               both("bet_bd_ready"), both("key_bd_ready"))
    v_ps, g1_ps, a5_ps, g2_ps, kt_ps, bt_ps = (both("v_psum"), both("gram_bet_psum"), both("gram_l_psum"),
                                               both("gram_key_psum"), both("keyt_psum"), both("bett_psum"))
    p_r, kt_r, bt_r = both("p_ready"), both("keyt_ready"), both("bett_ready")
    inv_r, mpq = both("inverse_started"), both("masked_grams")
    y_ps, z_r, n_ps, n_r = both("level_y_psum"), both("level_z"), both("level_n_psum"), both("level_n")
    x_ps, x_r, u_ps, u_r = both("x_psum"), both("x_ready"), both("u_psum"), both("u_ready")
    o_r, o_sp = both("y_ready"), both("y_written")
    kd_sp, o_free, kd_free = both("kd_written"), both("y_buffer_free"), both("kd_buffer_free")
    done, st_r = both("round_psum_done"), both("state_ready")
    out_ps, out_r, out_w = sem("final_psum"), sem("final_ready"), sem("final_written")

    def cols(i, d, n=C):
        return ds(i * C, n) if d == 0 else ds(i * (-C) + (NCH - 1) * C, n)

    def q4(ap):
        return ap.rearrange("p (a b) -> p a b", a=NP_)

    def bd4(ap):
        return ap.rearrange("p a (h t) -> p a h t", h=2)

    def over_h(ap):
        return ap.unsqueeze(2).to_broadcast([P, NP_, 2, C])

    def mask_bd(m):
        return m.rearrange("p (h t) -> p h t", h=2).unsqueeze(1).to_broadcast([P, NP_, 2, C])

    def mask_c(m):
        return m.unsqueeze(1).to_broadcast([P, NP_, C])

    NK = NP_ * T // 512

    with nc.Block() as block:

        @block.sync
        def _(sp):
            for d in two:
                sp.dma_start(st_rows[:, d, :].rearrange("v (h k) -> v h k", h=NH),
                             a["state"][d].rearrange("h v k -> v h k")).then_inc(st_loaded, 16)
                sp.sem_inc(o_free[d], 1)
                sp.sem_inc(kd_free[d], 1)

            def keys_out(i):
                for d in two:
                    sp.wait_ge(kdr[d], i + 1)
                    sp.dma_start(s.kd_d[d][:, :, cols(i, d)], kd[d]).then_inc(kd_sp[d], 16)
                for d in two:
                    sp.wait_ge(kd_sp[d], i * 16 + 16)
                    sp.sem_inc(kd_free[d], 1)

            def y_out(i):
                for d in two:
                    chunk = i if d == 0 else i * (-1) + (NCH - 1)
                    sp.wait_ge(o_r[d], i + 1)
                    sp.dma_start(s.y_d[d][ds(chunk, 1)].rearrange("a p n -> (a p) n"),
                                 Yo[d].rearrange("p a b -> p (a b)")).then_inc(o_sp[d], 16)
                for d in two:
                    sp.wait_ge(o_sp[d], i * 16 + 16)
                    sp.sem_inc(o_free[d], 1)

            keys_out(0)
            with sp.Fori(0, NCH - 1) as i:
                keys_out(i + 1)
                y_out(i)
            y_out(NCH - 1)
            sp.wait_ge(out_r, 1)
            for d in two:
                for q in range(2):
                    for j in range(2):
                        h0 = 2 * (2 * q + j)
                        src = fin[j * HS:(j + 1) * HS, d * 2 + q, :].rearrange("v (h k) -> v h k", h=2)
                        sp.dma_start(a["out_state"][d, h0:h0 + 2].rearrange("h v k -> v h k"), src)\
                            .then_inc(out_w, 16)
            sp.wait_ge(out_w, 16 * 8)

        @block.gpsimd
        def _(pool):
            for n in ("kap", "rho", "bet", "key", "val"):
                for d in two:
                    last = nc.gpsimd.memset(bds[n][d], 0.0)
            last.then_inc(zeroed, 1)
            pool.wait_ge(zeroed, 1)

            def spread(dst, src):
                nc.gpsimd.tensor_copy(dst[0:HS, :, 0:C], src[0:HS])
                return nc.gpsimd.tensor_copy(dst[HS:P, :, C:P], src[HS:P])

            with pool.Fori(0, NCH) as i:
                for d in two:
                    hold(pool, turns, (v_ps[d], i + 1))
                    spread(bds["val"][d], s.vT[:, :, cols(i, d)]).then_inc(vbd[d], 1)
                for d in two:
                    hold(pool, turns, (bkr[d], i + 1), (kt_ps[d], i + 1))
                    spread(bds["key"][d], key[d]).then_inc(kyb[d], 1)
                for d in two:
                    hold(pool, turns, (done[d], i + 1))
                    spread(bds["rho"][d], kr[d][:, :, C:2 * C]).then_inc(rbd[d], 1)

        @block.tensor
        def _(pe):
            for d in two:
                pe.sem_inc(done[d], 1)
                pe.sem_inc(v_ps[d], 1)
                pe.sem_inc(kt_ps[d], 1)
            pe.wait_ge(st_loaded, 32)
            for d in two:
                for p in range(NP_):
                    last = nc.tensor.transpose(BA[0][:, (d * NP_ + p) * HS:(d * NP_ + p + 1) * HS],
                                               st_rows[:, d, p * P:(p + 1) * P], K["ident"][0:HS, 0:HS])
            last.then_inc(st_ps, 1)
            for n in range(NK):
                pe.wait_ge(ksq, n + 1)
                if n >= 2:
                    pe.wait_ge(kn, n - 1)
                nc.tensor.matmul(BB[n % 2], K["blockones"], sqt[n % 2], start=True, stop=True)\
                    .then_inc(kn_ps, 1)
            pe.wait_ge(ready, 1)
            pe.wait_ge(st_set, 1)

            def each(out, lhsT, rhs, w, acc=None):
                for p in range(NP_):
                    terms = [(lhsT, rhs)] + (acc or [])
                    for n, (l, r) in enumerate(terms):
                        last = nc.tensor.matmul(out[:, p * w:(p + 1) * w], l[:, p, :], r[:, p, :],
                                                start=(n == 0), stop=(n == len(terms) - 1))
                return last

            def rows(d, name, done_sem):
                for p in range(NP_):
                    last = nc.tensor.transpose(BA[d][:, p * P:(p + 1) * P], bds[name][d][:, p, :],
                                               K["ident"])
                last.then_inc(done_sem[d], 1)

            def lora(i):
                for d in two:
                    for q in range(2):
                        for p in range(NP_):
                            o = (q * NP_ + p) * C
                            last = nc.tensor.matmul(BA[d][:, o:o + C],
                                                    s.lora_up[:, 2 * q + d, p * P:(p + 1) * P],
                                                    s.loraT[:, q, cols(i, d)], start=True, stop=True)
                    last.then_inc(aw[d], 1)

            def solve(i):
                for d in two:
                    pe.wait_ge(n_r[d], i * 5 + 5)
                    pe.wait_ge(x_r[d], i + 1)
                    each(BC[d], bds["NI"][d], X[d], HS).then_inc(u_ps[d], 1)

            def results(i):
                for d in two:
                    b = {n: v[d] for n, v in bds.items()}
                    pe.wait_ge(u_r[d], i + 1)
                    pe.wait_ge(rbd[d], i + 1)
                    each(BA[d], b["rho"], S[d], HS, [(b["P"], U[d]), (b["Q"], Vt[d])])
                    each(BA[d][:, 256:512], b["keyt"], Vt[d], HS, [(b["bett"], U[d])]).then_inc(done[d], 1)

            def body(i, prev=True, ahead=True):
                for d in two:
                    pe.wait_ge(bbd[d], i + 1)
                    pe.wait_ge(krr[d], i + 1)
                    each(BB[d], bds["bet"][d], kr[d][:, :, 0:C], C).then_inc(g1_ps[d], 1)
                    pe.wait_ge(kbd[d], i + 1)
                    if prev:
                        pe.wait_ge(n_r[d], i * 5)
                    each(BD[d], bds["kap"][d], bet[d], C).then_inc(a5_ps[d], 1)
                if ahead:
                    for d in two:
                        if prev:
                            pe.wait_ge(kt_r[d], i)
                        else:
                            pe.wait_ge(t1b[d], 1)
                    lora(i + 1)
                if prev:
                    solve(i - 1)
                for lv in range(len(LEVELS)):
                    for d in two:
                        b = {n: v[d] for n, v in bds.items()}
                        if lv == 0:
                            pe.wait_ge(inv_r[d], i + 1)
                        else:
                            pe.wait_ge(n_r[d], i * 5 + lv)
                        if lv == 3:
                            pe.wait_ge(p_r[d], i + 1)
                        if lv == 2:
                            each(BB[d][:, 256:512], b["bet"], kr[d][:, :, C:2 * C], C)
                        each(BB[d], b["AT"], N[d], C).then_inc(y_ps[d], 1)
                    if lv == 4:
                        for d in two:
                            pe.wait_ge(mpq[d], i + 1)
                            rows(d, "key", kt_ps)
                        for d in two:
                            b = {n: v[d] for n, v in bds.items()}
                            if prev:
                                pe.wait_ge(st_r[d], i)
                            each(BC[d], b["kap"], S[d], HS, [(b["M"], Vt[d])]).then_inc(x_ps[d], 1)
                    for d in two:
                        b = {n: v[d] for n, v in bds.items()}
                        if lv == 2:
                            pe.wait_ge(vbd[d], i + 1)
                            for p in range(NP_):
                                last = nc.tensor.matmul(BC[d][:, 256 + p * HS:256 + (p + 1) * HS],
                                                        b["val"][:, p, :], K["fold"], start=True, stop=True)
                            last.then_inc(v_ps[d], 1)
                        if lv == 0 and prev:
                            pe.wait_ge(u_r[d], i)
                        pe.wait_ge(z_r[d], i * 5 + (lv + 1))
                        if lv < len(LEVELS) - 1:
                            each(BC[d], b["NT"], Z[d], C)
                        each(BD[d], b["Z"], b["NT"], P).then_inc(n_ps[d], 1)
                    if lv == 0 and prev:
                        for d in two:
                            if ahead:
                                pe.wait_ge(t1b[d], i + 2)
                            else:
                                pe.wait_ge(kt_r[d], i)
                        results(i - 1)
                    if lv == 1:
                        for d in two:
                            if prev:
                                pe.wait_ge(o_r[d], i)
                                pe.wait_ge(st_r[d], i)
                            elif ahead:
                                pe.wait_ge(t1b[d], 2)
                            rows(d, "bet", bt_ps)
                    if lv == 2:
                        for d in two:
                            pe.wait_ge(bt_r[d], i + 1)
                            pe.wait_ge(kyb[d], i + 1)
                            each(BA[d], bds["key"][d], kr[d], 2 * C).then_inc(g2_ps[d], 1)

            lora(0)
            body(0, prev=False)
            with pe.Fori(1, NCH - 1) as i:
                body(i)
            body(NCH - 1, ahead=False)
            solve(NCH - 1)
            for d in two:
                pe.wait_ge(kt_r[d], NCH)
            results(NCH - 1)
            for d in two:
                pe.wait_ge(st_r[d], NCH)
                pe.wait_ge(o_r[d], NCH)
            for d, src in enumerate((S[0], S_keep)):
                for q in range(2):
                    last = nc.tensor.transpose(BA[0][:, (d * 2 + q) * P:(d * 2 + q + 1) * P],
                                               src[:, 2 * q:2 * q + 2, :].rearrange("p a b -> p (a b)"),
                                               K["ident"])
            last.then_inc(out_ps, 1)

        @block.scalar
        def _(act):
            for n in range(NK):
                act.wait_ge(kraw, 1)
                if n >= 2:
                    act.wait_ge(kn_ps, n - 1)
                nc.scalar.activation(sqt[n % 2], kk_flat[:, n * 512:(n + 1) * 512], ACT.Square)\
                    .then_inc(ksq, 1)
            for n in range(NK):
                act.wait_ge(kn, n + 1)
                nc.scalar.activation(root_t[:, n * 512:(n + 1) * 512], root_t[:, n * 512:(n + 1) * 512],
                                     ACT.Sqrt).then_inc(kroot, 1)

            def spread(dst, src):
                nc.scalar.activation(dst[0:HS, :, 0:C], src[0:HS], ACT.Copy)
                return nc.scalar.activation(dst[HS:P, :, C:P], src[HS:P], ACT.Copy)

            act.wait_ge(zeroed, 1)

            def tanh(i):
                for d in two:
                    act.wait_ge(t1b[d], i + 1)
                    nc.scalar.activation(wa[d], wa[d], ACT.Tanh, scale=0.5).then_inc(t1t[d], 1)

            def exps(i):
                for d in two:
                    act.wait_ge(cr[d], i + 1)
                    nc.scalar.activation(inv[d], cum[d][:, 1], ACT.Exp, scale=C0).then_inc(inv_e[d], 1)
                for d in two:
                    act.wait_ge(inv_e[d], i + 1)
                    nc.scalar.activation(cum[d], cum[d], ACT.Exp, scale=-C0).then_inc(er[d], 1)

            def spread_bet(i):
                for d in two:
                    act.wait_ge(bkr[d], i + 1)
                    spread(bds["bet"][d], bet[d]).then_inc(bbd[d], 1)

            def spread_kap(i):
                for d in two:
                    act.wait_ge(krr[d], i + 1)
                    spread(bds["kap"][d], kr[d][:, :, 0:C]).then_inc(kbd[d], 1)

            def take_u(i):
                for d in two:
                    act.wait_ge(u_ps[d], i + 1)
                    nc.scalar.activation(U[d], q4(BC[d][:, 0:PC]), ACT.Copy, scale=-1.0).then_inc(u_r[d], 1)

            def take_y(i):
                for d in two:
                    act.wait_ge(done[d], i + 2)
                    nc.scalar.activation(Yo[d], q4(BA[d][:, 0:PC]), ACT.Copy).then_inc(o_r[d], 1)

            def body(i, prev=True, ahead=True):
                if prev:
                    take_u(i - 1)
                for lv in range(len(LEVELS)):
                    if lv == 2:
                        for d in two:
                            act.wait_ge(bt_ps[d], i + 1)
                            nc.scalar.activation(bds["bett"][d], q4(BA[d]), ACT.Copy).then_inc(bt_r[d], 1)
                    if lv == 4:
                        for d in two:
                            act.wait_ge(kt_ps[d], i + 2)
                            nc.scalar.activation(bds["keyt"][d], q4(BA[d]), ACT.Copy).then_inc(kt_r[d], 1)
                        for d in two:
                            act.wait_ge(x_ps[d], i + 1)
                            act.wait_ge(o_free[d], i + 1)
                            nc.scalar.activation(X[d], q4(BC[d][:, 0:PC]), ACT.Copy).then_inc(x_r[d], 1)
                        if ahead:
                            spread_bet(i + 1)
                            spread_kap(i + 1)
                    for d in two:
                        act.wait_ge(n_ps[d], i * 5 + (lv + 1))
                        if lv < len(LEVELS) - 1:
                            nc.scalar.activation(N[d], q4(BC[d][:, 0:PC]), ACT.Copy)
                        if lv == 2:
                            nc.scalar.activation(Vt[d], q4(BC[d][:, PC:2 * PC]), ACT.Copy)
                        nc.scalar.activation(bds["NT" if lv < len(LEVELS) - 1 else "NI"][d], q4(BD[d]),
                                             ACT.Copy).then_inc(n_r[d], 1)
                    if lv == 0 and ahead:
                        tanh(i + 1)
                    if lv == 0 and prev:
                        take_y(i - 1)
                    if lv == 2 and ahead:
                        exps(i + 1)

            tanh(0)
            exps(0)
            spread_bet(0)
            spread_kap(0)
            body(0, prev=False)
            with act.Fori(1, NCH - 1) as i:
                body(i)
            body(NCH - 1, ahead=False)
            take_u(NCH - 1)
            take_y(NCH - 1)
            act.wait_ge(out_ps, 1)
            nc.scalar.activation(fin, BA[0].rearrange("p (a b) -> p a b", b=P), ACT.Copy).then_inc(out_r, 1)

        @block.vector
        def _(dve):
            own = Chain(dve, dvo)
            for p in range(NP_):
                last = nc.vector.tensor_scalar(kk[:, p, :], s.kT[:, p, :], V["k_k"][:, p:p + 1], None, ALU.mult)
            last.then_inc(kraw, 1)
            for n in range(NK):
                dve.wait_ge(kn_ps, n + 1)
                nc.vector.tensor_scalar(root_t[:, n * 512:(n + 1) * 512], BB[n % 2], 1e-24, None, ALU.max)\
                    .then_inc(kn, 1)
            for n in range(NK):
                dve.wait_ge(kroot, n + 1)
                own.link(nc.vector.reciprocal(root_t[:, n * 512:(n + 1) * 512],
                                              root_t[:, n * 512:(n + 1) * 512]))
            nc.vector.tensor_tensor(kk_flat, kk_flat, root_t, ALU.mult).then_inc(ready, 1)
            dve.wait_ge(ready, 1)
            dve.wait_ge(st_ps, 1)
            st = BA[0].rearrange("p (d a b) -> p d a b", d=2, a=NP_)
            nc.vector.memset(S[1], 0.0)
            nc.vector.tensor_copy(S[0], st[:, 0])
            own.link(nc.vector.tensor_copy(S_next, st[:, 1]))
            dve.sem_inc(st_set, 1)

            def bias(i):
                for d in two:
                    dve.wait_ge(aw[d], i + 1)
                    b = V["bias_wa"][:, 8 * d:8 * d + 8].unsqueeze(2).to_broadcast([P, 8, C])
                    nc.vector.tensor_tensor(wa[d].rearrange("p q a t -> p (q a) t"),
                                            BA[d].rearrange("p (a t) -> p a t", t=C), b, ALU.add)\
                        .then_inc(t1b[d], 1)

            def sums(i):
                for d in two:
                    dve.wait_ge(t1t[d], i + 1)
                    own.link(nc.vector.tensor_scalar(wa[d], wa[d], 0.5, 0.5, ALU.mult, ALU.add))
                    sg = wa[d][:, 0]
                    first = cum[d][:, 1] if d == 0 else ba[d]
                    own.link(nc.vector.tensor_tensor_scan(first.rearrange("p a t -> p (a t)"), K["reset"],
                                                          sg.rearrange("p a t -> p (a t)"), 0.0,
                                                          ALU.mult, ALU.add))
                    if d == 0:
                        nc.vector.tensor_tensor(cum[d][:, 0], cum[d][:, 1], sg, ALU.subtract)\
                            .then_inc(cr[d], 1)
                    else:
                        total = first[:, :, C - 1:C].to_broadcast([P, NP_, C])
                        own.link(nc.vector.tensor_tensor(cum[d][:, 0], total, first, ALU.subtract))
                        nc.vector.tensor_tensor(cum[d][:, 1], cum[d][:, 0], sg, ALU.add).then_inc(cr[d], 1)

            def keys(i):
                k_a = V["k_a"].unsqueeze(2).to_broadcast([P, NP_, C])
                for d in two:
                    ga = wa[d][:, 1]
                    dve.wait_ge(kd_free[d], i + 1)
                    own.link(nc.vector.scalar_tensor_tensor(out=kd[d], in0=ga, scalar=1.0, in1=k_a,
                                                            op0=ALU.subtract, op1=ALU.mult))
                    nc.vector.scalar_tensor_tensor(out=kd[d], in0=kd[d], scalar=1.0,
                                                   in1=s.kT[:, :, cols(i, d)], op0=ALU.add, op1=ALU.mult)\
                        .then_inc(kdr[d], 1)
                    own.link(nc.vector.tensor_tensor(ba[d], kk[:, :, cols(i, d)], ga, ALU.mult))

            def decayed(i, first=False):
                for d in two:
                    if not first:
                        dve.wait_ge(rbd[d], i)
                        dve.wait_ge(g2_ps[d], i)
                    dve.wait_ge(er[d], i + 1)
                    nc.vector.tensor_tensor(kr[d][:, :, 0:C], cum[d][:, 0], kk[:, :, cols(i, d)], ALU.mult)
                    nc.vector.tensor_tensor(kr[d][:, :, C:2 * C], cum[d][:, 1], s.rT[:, :, cols(i, d)],
                                            ALU.mult).then_inc(krr[d], 1)
                    nc.vector.tensor_tensor(bet[d], inv[d], ba[d], ALU.mult)
                    dve.wait_ge(kdr[d], i + 1)
                    nc.vector.tensor_tensor(key[d], inv[d], kd[d], ALU.mult).then_inc(bkr[d], 1)

            def keep_decay(i, prev=True):
                for d in two:
                    end = C - 1 if d == 0 else 0
                    if prev:
                        dve.wait_ge(st_r[d], i)
                    last = nc.vector.tensor_copy(wc[d], cum[d][:, 1, :, end])
                own.link(last)

            def state(i, switch=None):
                for d in two:
                    dve.wait_ge(done[d], i + 2)
                    dve.wait_ge(o_r[d], i + 1)
                    if switch == "prompt" and d == 0:
                        nc.vector.memset(S[0], 0.0).then_inc(st_r[0], 1)
                        continue
                    own.link(nc.vector.tensor_tensor(S[d], S[d], q4(BA[d][:, 256:512]), ALU.add))
                    out = nc.vector.tensor_tensor(S[d], S[d], wc[d].unsqueeze(2).to_broadcast([P, NP_, HS]),
                                                  ALU.mult)
                    if switch == "sample" and d == 1:
                        own.link(out)
                        own.link(nc.vector.tensor_copy(S_keep, S[1]))
                        out = nc.vector.tensor_copy(S[1], S_next)
                    out.then_inc(st_r[d], 1)

            def body(i, prev=True, ahead=True, switch=None):
                for d in two:
                    b = {n: v[d] for n, v in bds.items()}
                    dve.wait_ge(g1_ps[d], i + 1)
                    own.link(nc.vector.tensor_tensor(bd4(b["AT"]), over_h(q4(BB[d][:, 0:PC])),
                                                     mask_bd(K[f"strict{d}"]), ALU.mult))
                    own.link(nc.vector.tensor_tensor(b["AT"], b["AT"],
                                                     K["ident"].unsqueeze(1).to_broadcast([P, NP_, P]),
                                                     ALU.add))
                    nc.vector.tensor_tensor(b["NT"], b["AT"],
                                            K[f"first{d}"].unsqueeze(1).to_broadcast([P, NP_, P]), ALU.mult)
                    dve.wait_ge(a5_ps[d], i + 1)
                    own.link(nc.vector.tensor_tensor(N[d], q4(BD[d][:, 0:PC]), mask_c(K[f"firstc{d}"]),
                                                     ALU.mult))
                    nc.vector.tensor_tensor(N[d], N[d], mask_c(K["fold"]), ALU.add).then_inc(inv_r[d], 1)
                for lv, size in enumerate(LEVELS):
                    for d in two:
                        dve.wait_ge(y_ps[d], i * 5 + (lv + 1))
                        y = q4(BB[d][:, 0:PC])
                        if lv < len(LEVELS) - 1:
                            nc.vector.tensor_tensor(Z[d], y, mask_c(K[f"levc{d}_{size}"]), ALU.mult)
                        nc.vector.tensor_tensor(bd4(bds["Z"][d]), over_h(y), mask_bd(K[f"lev{d}_{size}"]),
                                                ALU.mult).then_inc(z_r[d], 1)
                    if lv == 0 and ahead:
                        bias(i + 1)
                    if lv == 1:
                        if prev:
                            state(i - 1, switch)
                        keep_decay(i, prev)
                        if ahead:
                            sums(i + 1)
                    if lv == 2:
                        for d in two:
                            nc.vector.tensor_tensor(bd4(bds["P"][d]), over_h(q4(BB[d][:, PC:2 * PC])),
                                                    mask_bd(K[f"incl{d}"]), ALU.mult).then_inc(p_r[d], 1)
                        if ahead:
                            keys(i + 1)
                    if lv == 3:
                        for d in two:
                            b, g2 = {n: v[d] for n, v in bds.items()}, q4(BA[d])
                            dve.wait_ge(g2_ps[d], i + 1)
                            nc.vector.tensor_tensor(bd4(b["M"]), over_h(g2[:, :, 0:C]),
                                                    mask_bd(K[f"strict{d}"]), ALU.mult)
                            nc.vector.tensor_tensor(bd4(b["Q"]), over_h(g2[:, :, C:2 * C]),
                                                    mask_bd(K[f"incl{d}"]), ALU.mult).then_inc(mpq[d], 1)
                        if ahead:
                            decayed(i + 1)

            LINKS = 18
            bias(0)
            sums(0)
            keys(0)
            decayed(0, True)
            body(0, prev=False)
            looped(dve, own, 1, NCP, LINKS, body)
            body(NCP, switch="sample")
            looped(dve, own, NCP + 1, NCS, LINKS, body)
            body(NCS, switch="prompt")
            looped(dve, own, NCS + 1, NCH - 1, LINKS, body)
            body(NCH - 1, ahead=False)
            state(NCH - 1)
def phase_mix(nc, s):
    a, K, V, PS, M, sem = s.a, s.K, s.V, s.PS, s.M, s.sem
    ar = Arena(M, s.n_main, s.mark)
    NG = NCH * NP_
    ybd = [ar.get(NP_, P) for _ in (0, 1)]
    at_y0 = ar.at
    y0 = ar.get(NG, HS)
    at_k0 = ar.at
    kd0 = ar.get(NP_, T)
    at_y1 = ar.at
    y1 = ar.get(NG, HS)
    kd1 = ar.get(NP_, T)
    cvT = ar.get(NP_, T)
    xgT, g_up = ar.get(T), ar.get(CW)
    gs = ar.get(3, NG)
    ynT = s.kT
    bon = s.rT
    w_o = M[:, at_y1:at_y1 + KC * D].rearrange("p (k n) -> p k n", n=D)
    t0 = at_y1 + KC * D
    assert t0 >= RING
    TB = 64
    aff = M[0:TB, t0:t0 + TS]
    vals = M[0:TB, t0 + TS:t0 + TS + P]
    idx = M[0:TB, t0 + TS + P:t0 + TS + 2 * P].bitcast(U32)
    idxf = M[0:TB, t0 + TS + 2 * P:t0 + TS + 3 * P]
    aft = [M[:, t0 + TS + (3 + i) * P:t0 + TS + (4 + i) * P] for i in (0, 1)]
    g1b = M[:, at_y0:at_y0 + 2 * D].rearrange("p (j n) -> p j n", n=D)
    xt = [M[:, at_y0 + (2 + i) * D:at_y0 + (3 + i) * D] for i in (0, 1)]
    junk = [M[:, at_y0 + 4 * D:at_y0 + 5 * D], M[:, at_k0 + 4 * D:at_k0 + 5 * D]]
    x2 = [M[:, at_k0 + i * D:at_k0 + (i + 1) * D] for i in (0, 1)]
    xn = [M[:, at_k0 + (2 + i) * D:at_k0 + (3 + i) * D] for i in (0, 1)]
    h2 = [s.rkv[:, 0:4, :].rearrange("p a b -> p (a b)")[:, i * D:(i + 1) * D]
          .rearrange("p (k t) -> p k t", t=P) for i in (0, 1)]
    rt = s.vT.rearrange("p a b -> p (a b)")[:, 0:KC * E].rearrange("p (k e) -> p k e", e=E)
    ex = [s.vT[:, 1, i * E:(i + 1) * E] for i in (0, 1)]
    mixps = [PS[:, 0:D], PS[:, D:2 * D]]
    trp = PS[:, 4 * 512:4 * 512 + D]
    lg, afp = PS[:, 6 * 512:6 * 512 + E], PS[:, 7 * 512:7 * 512 + P]
    ssq = [s.st[:, i:i + 1] for i in (0, 1)]
    ms = [s.st[:, i:i + 1] for i in (2, 3)]
    root = [s.st[:, i:i + 1] for i in (4, 5)]
    rstd = [s.st[:, i:i + 1] for i in (8, 9)]
    nmx = [s.st[:, i:i + 1] for i in (6, 7)]
    esum = [s.st[:, i:i + 1] for i in (10, 11)]
    tiles = [(p, c0, w) for p in range(NP_) for c0, w in COLS3]

    y_in, kd_in, c_in, wo_in, misc_in = (sem("y_in"), sem("kd_in"), sem("conv_in"), sem("w_out_in"),
                                         sem("gate1_router_in"))
    g_in = sem("gate_lora_in")
    gsq, gvar, groot, y1_free = sem("gn_squared"), sem("gn_var"), sem("gn_root"), sem("y1_free")
    yc_done, kd_free = sem("gn_centered"), sem("kd1_free")
    ybz, yb_r, yn_ps, yn_r = sem("ybd_zeroed"), sem("ybd_ready"), sem("yn_psum"), sem("yn_ready")
    bprod, bon_ps, rw_r = sem("bonus_product"), sem("bonus_gate_psum"), sem("rwkv_out_ready")
    x_in = [sem(f"x_again{i}") for i in (0, 1)]
    acc_w = [sem(f"residual_written{i}") for i in (0, 1)]
    xn_w = [sem(f"normed_written{i}") for i in (0, 1)]
    mx, x2_r, sq_r, ms_r, rt_r, xn_r = (sem("mix_psum"), sem("x2_ready"), sem("x2_squared"),
                                        sem("x2_mean_square"), sem("x2_root"), sem("x2_normed"))
    tr, h_a, h_d, lg_r, mx_r, ex_r, af_r, at_r, ac_r = (
        sem("x2_transposed"), sem("h2_by_act"), sem("h2_by_dve"), sem("logits"), sem("logit_max"),
        sem("exp_logits"), sem("affinity_rows"), sem("affinity_psum"), sem("affinity_ready"))
    az, dvo, tab, tabt = sem("affinity_zeroed"), sem("dve_own_c"), sem("lists_ready"), sem("lists_psum")

    with nc.Block() as block:

        @block.sync
        def _(sp):
            for d, dst in enumerate((y0, y1)):
                sp.dma_start(dst.rearrange("p (c a) b -> p c (a b)", a=NP_),
                             s.y_d[d].rearrange("c p n -> p c n")).then_inc(y_in, 16)
            for d, dst in enumerate((kd0, kd1)):
                sp.dma_start(dst, s.kd_d[d]).then_inc(kd_in, 16)
            sp.dma_start(cvT.rearrange("p a b -> p (a b)"), s.conv_d).then_inc(c_in, 16)
            sp.dma_start(xgT, s.xg_d).then_inc(g_in, 16)
            sp.dma_start(g_up, a["g_up"]).then_inc(g_in, 16)
            sp.wait_ge(y1_free, 1)
            sp.wait_ge(kd_free, 1)
            sp.dma_start(w_o, a["w_out"].rearrange("(k p) n -> p k n", p=P)).then_inc(wo_in, 16)
            sp.wait_ge(rw_r, len(tiles))
            for j in range(2):
                sp.dma_start(g1b[:, j, :], s.g1_d[j:j + 1, :].to_broadcast([P, D])).then_inc(misc_in, 16)
            sp.dma_start(rt, a["router"].rearrange("(k p) e -> p k e", p=P)).then_inc(misc_in, 16)
            for n in range(NT + 1):
                if n < NT:
                    if n >= 2:
                        sp.wait_ge(x2_r, n - 1)
                    sp.dma_start(xt[n % 2], a["x"][n * P:(n + 1) * P, :]).then_inc(x_in[n % 2], 16)
                if n >= 1:
                    m = n - 1
                    sp.wait_ge(x2_r, m + 1)
                    sp.dma_start(s.acc_d[m * P:(m + 1) * P, :], x2[m % 2]).then_inc(acc_w[m % 2], 16)
                    sp.wait_ge(xn_r, m + 1)
                    sp.dma_start(s.xn_d[m * P:(m + 1) * P, :], xn[m % 2]).then_inc(xn_w[m % 2], 16)
            for i in (0, 1):
                sp.wait_ge(acc_w[i], 16 * NT // 2)
                sp.wait_ge(xn_w[i], 16 * NT // 2)
            sp.wait_ge(lg_r, NT)
            sp.wait_ge(ex_r, NT)
            sp.wait_ge(af_r, NT)
            for n in range(SLOTS):
                load_step(sp, s, 0, n)

        @block.gpsimd
        def _(pool):
            for i in (0, 1):
                nc.gpsimd.memset(ybd[i], 0.0).then_inc(ybz, 1)
            pool.wait_ge(y1_free, 1)
            pool.wait_ge(kd_free, 1)
            for i in (0, 1):
                nc.gpsimd.memset(aft[i], 0.0).then_inc(az, 1)
            nc.gpsimd.memset(M[0:TB, t0:t0 + TS + 3 * P], -1.0).then_inc(az, 1)

        @block.tensor
        def _(pe):
            for sm in (yn_r,):
                pe.sem_inc(sm, 2)
            with pe.Fori(0, NCH // 2) as j:
                for i in (0, 1):
                    pe.wait_ge(yb_r, j * 2 + (i + 1))
                    pe.wait_ge(yn_r, j * 2 + (i + 1))
                    for p in range(NP_):
                        last = nc.tensor.matmul(PS[:, i * 512 + p * C:i * 512 + (p + 1) * C],
                                                ybd[i][:, p, :], K["fold"], start=True, stop=True)
                    last.then_inc(yn_ps, 1)
            pe.wait_ge(bprod, 1)
            pe.wait_ge(g_in, 32)
            for n, (p, c0, w) in enumerate(tiles):
                if n >= 2:
                    pe.wait_ge(rw_r, n - 1)
                nc.tensor.matmul(PS[:, (2 + n % 2) * 512:(2 + n % 2) * 512 + w], K["blockones"],
                                 kd0[:, p, c0:c0 + w], start=True, stop=True)
                nc.tensor.matmul(PS[:, (4 + n % 2) * 512:(4 + n % 2) * 512 + w],
                                 g_up[:, p * P:(p + 1) * P], xgT[:, c0:c0 + w],
                                 start=True, stop=True).then_inc(bon_ps, 1)
            pe.wait_ge(rw_r, len(tiles))
            pe.wait_ge(yn_r, NCH + 2)
            pe.wait_ge(wo_in, 16)
            pe.wait_ge(c_in, 16)
            pe.wait_ge(misc_in, 48)
            for n in range(NT + 3):
                if n < NT:
                    if n >= 2:
                        pe.wait_ge(x2_r, n - 1)
                    for half in (0, 1):
                        for k in range(KC):
                            src = cvT if k < NP_ else ynT
                            last = nc.tensor.matmul(mixps[n % 2][:, half * 512:(half + 1) * 512],
                                                    src[:, k % NP_, n * P:(n + 1) * P],
                                                    w_o[:, k, half * 512:(half + 1) * 512],
                                                    start=(k == 0), stop=(k == KC - 1))
                    last.then_inc(mx, 1)
                m = n - 1
                if 0 <= m < NT:
                    pe.wait_ge(xn_r, m + 1)
                    if m >= 1:
                        pe.wait_ge(h_a, m)
                        pe.wait_ge(h_d, m)
                    for k in range(KC):
                        last = nc.tensor.transpose(trp[:, k * P:(k + 1) * P],
                                                   xn[m % 2][:, k * P:(k + 1) * P], K["ident"])
                    last.then_inc(tr, 1)
                m = n - 2
                if 0 <= m < NT:
                    pe.wait_ge(h_a, m + 1)
                    pe.wait_ge(h_d, m + 1)
                    if m >= 1:
                        pe.wait_ge(ex_r, m)
                        pe.wait_ge(mx_r, m)
                    for k in range(KC):
                        last = nc.tensor.matmul(lg, h2[m % 2][:, k, :], rt[:, k, :],
                                                start=(k == 0), stop=(k == KC - 1))
                    last.then_inc(lg_r, 1)
                m = n - 3
                if 0 <= m < NT:
                    pe.wait_ge(af_r, m + 1)
                    if m >= 1:
                        pe.wait_ge(ac_r, m)
                    nc.tensor.transpose(afp, aft[m % 2], K["ident"]).then_inc(at_r, 1)
            pe.wait_ge(tab, 1)
            nc.tensor.transpose(PS[:, 0:TB], vals, K["ident"][0:TB, 0:TB])
            nc.tensor.transpose(PS[:, TB:2 * TB], idxf, K["ident"][0:TB, 0:TB]).then_inc(tabt, 1)

        @block.scalar
        def _(act):
            act.wait_ge(yc_done, 1)
            nc.scalar.activation(y1, y0, ACT.Square).then_inc(gsq, 1)
            act.wait_ge(gvar, 1)
            nc.scalar.activation(gs[:, 1, :], gs[:, 1, :], ACT.Sqrt).then_inc(groot, 1)
            with act.Fori(0, NCH // 2) as j:
                for i in (0, 1):
                    act.wait_ge(yn_ps, j * 2 + (i + 1))
                    for p in range(NP_):
                        last = nc.scalar.activation(ynT[:, p, ds(j * (2 * C) + i * C, C)],
                                                    PS[:, i * 512 + p * C:i * 512 + (p + 1) * C],
                                                    ACT.Identity, scale=V["gng"][:, p:p + 1],
                                                    bias=V["gnb"][:, p:p + 1])
                    last.then_inc(yn_r, 1)
            for n in range(NT + 2):
                if n < NT:
                    i = n % 2
                    act.wait_ge(x2_r, n + 1)
                    nc.scalar.activation(junk[i], x2[i], ACT.Square, accum_out=ssq[i]).then_inc(sq_r, 1)
                    act.wait_ge(ms_r, n + 1)
                    nc.scalar.activation(root[i], ms[i], ACT.Sqrt).then_inc(rt_r, 1)
                m = n - 1
                if 0 <= m < NT:
                    g = 0 if m < NTS else 1
                    act.wait_ge(tr, m + 1)
                    for k in range(4):
                        last = nc.scalar.activation(h2[m % 2][:, k, :], trp[:, k * P:(k + 1) * P],
                                                    ACT.Identity, scale=s.A2[:, k, g:g + 1],
                                                    bias=s.B2[:, k, g:g + 1])
                    last.then_inc(h_a, 1)
                m = n - 2
                if 0 <= m < NT:
                    act.wait_ge(mx_r, m + 1)
                    nc.scalar.activation(ex[m % 2], lg, ACT.Exp, bias=nmx[m % 2],
                                         accum_out=esum[m % 2]).then_inc(ex_r, 1)

        @block.vector
        def _(dve):
            own = Chain(dve, dvo)
            dve.wait_ge(y_in, 32)
            own.link(nc.vector.tensor_tensor(y0, y0, y1, ALU.add))
            own.link(nc.vector.tensor_reduce(gs[:, 0, :], y0, AX.X, ALU.add))
            own.link(nc.vector.tensor_scalar(gs[:, 0, :], gs[:, 0, :], 1.0 / HS, None, ALU.mult))
            nc.vector.tensor_tensor(y0, y0, gs[:, 0, :].unsqueeze(2).to_broadcast([P, NG, HS]),
                                    ALU.subtract).then_inc(yc_done, 1)
            dve.wait_ge(kd_in, 32)
            own.link(nc.vector.tensor_tensor(kd0, kd0, kd1, ALU.add))
            dve.sem_inc(kd_free, 1)
            for p in range(NP_):
                last = nc.vector.scalar_tensor_tensor(out=kd0[:, p, :], in0=s.rT[:, p, :],
                                                      scalar=V["r_k"][:, p:p + 1], in1=kd0[:, p, :],
                                                      op0=ALU.mult, op1=ALU.mult)
            last.then_inc(bprod, 1)
            dve.wait_ge(gsq, 1)
            own.link(nc.vector.tensor_reduce(gs[:, 1, :], y1, AX.X, ALU.add))
            dve.sem_inc(y1_free, 1)
            nc.vector.tensor_scalar(gs[:, 1, :], gs[:, 1, :], 1.0 / HS, GN_EPS, ALU.mult, ALU.add)\
                .then_inc(gvar, 1)
            dve.wait_ge(groot, 1)
            own.link(nc.vector.reciprocal(gs[:, 2, :], gs[:, 1, :]))
            dve.wait_ge(ybz, 2)
            with dve.Fori(0, NCH // 2) as j:
                for i in (0, 1):
                    dve.wait_ge(yn_r, j * 2 + (i + 1))
                    for h in (0, 1):
                        rows = slice(h * HS, (h + 1) * HS)
                        r = gs[rows, 2, ds(j * (2 * NP_) + i * NP_, NP_)].unsqueeze(2)\
                            .to_broadcast([HS, NP_, HS])
                        last = nc.vector.tensor_tensor(ybd[i][rows, :, h * HS:(h + 1) * HS],
                                                       y0[rows, ds(j * (2 * NP_) + i * NP_, NP_), :], r,
                                                       ALU.mult)
                    last.then_inc(yb_r, 1)
            dve.wait_ge(yn_r, NCH + 2)
            for n, (p, c0, w) in enumerate(tiles):
                dve.wait_ge(bon_ps, n + 1)
                c = slice(c0, c0 + w)
                own.link(nc.vector.tensor_tensor(bon[:, p, c], PS[:, (2 + n % 2) * 512:][:, 0:w],
                                                 s.vT[:, p, c], ALU.mult))
                own.link(nc.vector.tensor_tensor(ynT[:, p, c], ynT[:, p, c], bon[:, p, c], ALU.add))
                nc.vector.tensor_tensor(ynT[:, p, c], ynT[:, p, c], PS[:, (4 + n % 2) * 512:][:, 0:w],
                                        ALU.mult).then_inc(rw_r, 1)
            dve.wait_ge(misc_in, 48)
            dve.wait_ge(az, 3)
            for n in range(NT + 3):
                if n < NT:
                    i, g = n % 2, 0 if n < NTS else 1
                    dve.wait_ge(mx, n + 1)
                    dve.wait_ge(x_in[i], 16 * (n // 2 + 1))
                    if n >= 2:
                        dve.wait_ge(acc_w[i], 16 * (n // 2))
                        dve.wait_ge(xn_w[i], 16 * (n // 2))
                    own.link(nc.vector.tensor_tensor(x2[i], mixps[i], g1b[:, g, :], ALU.mult))
                    nc.vector.tensor_tensor(x2[i], x2[i], xt[i], ALU.add).then_inc(x2_r, 1)
                    dve.wait_ge(sq_r, n + 1)
                    nc.vector.tensor_scalar(ms[i], ssq[i], 1.0 / D, RMS_EPS, ALU.mult, ALU.add)\
                        .then_inc(ms_r, 1)
                    dve.wait_ge(rt_r, n + 1)
                    own.link(nc.vector.reciprocal(rstd[i], root[i]))
                    nc.vector.tensor_scalar(xn[i], x2[i], rstd[i], None, ALU.mult).then_inc(xn_r, 1)
                m = n - 1
                if 0 <= m < NT:
                    g = 0 if m < NTS else 1
                    dve.wait_ge(tr, m + 1)
                    for k in range(4, KC):
                        last = nc.vector.tensor_scalar(h2[m % 2][:, k, :], trp[:, k * P:(k + 1) * P],
                                                       s.A2[:, k, g:g + 1], s.B2[:, k, g:g + 1],
                                                       ALU.mult, ALU.add)
                    last.then_inc(h_d, 1)
                m = n - 2
                if 0 <= m < NT:
                    i, o = m % 2, 0 if m < NTS else PB
                    dve.wait_ge(lg_r, m + 1)
                    nc.vector.tensor_reduce(nmx[i], lg, AX.X, ALU.max, negate=True).then_inc(mx_r, 1)
                    dve.wait_ge(ex_r, m + 1)
                    own.link(nc.vector.reciprocal(esum[i], esum[i]))
                    nc.vector.tensor_scalar(aft[i][:, o:o + E], ex[i], esum[i], None, ALU.mult)\
                        .then_inc(af_r, 1)
                m = n - 3
                if 0 <= m < NT:
                    o, t = (0, m) if m < NTS else (PB, m - NTS)
                    dve.wait_ge(at_r, m + 1)
                    nc.vector.tensor_copy(aff[o:o + E, t * P:(t + 1) * P], afp[o:o + E, :]).then_inc(ac_r, 1)
            dve.wait_ge(ac_r, NT)
            for n in range(CAP_S // 8):
                v8 = vals[:, 8 * n:8 * n + 8]
                own.link(nc.vector.max(v8, aff))
                own.link(nc.vector.max_index(idx[:, 8 * n:8 * n + 8], v8, aff))
                own.link(nc.vector.match_replace(aff, v8, aff, -2.0))
            nc.vector.tensor_copy(idxf, idx).then_inc(tab, 1)
            dve.wait_ge(tabt, 1)
            own.link(nc.vector.tensor_copy(s.gateT, PS[:, 0:TB]))
            own.link(nc.vector.tensor_scalar(s.idxF[:, PB:TB], PS[:, TB + PB:2 * TB], float(TS), None,
                                             ALU.add))
            own.link(nc.vector.tensor_copy(s.idxF[:, 0:PB], PS[:, TB:TB + PB]))
            own.link(nc.vector.tensor_copy(s.idxT, s.idxF))



SC = max(STEP_CHUNKS)
PIECE = KC * P
RING = SLOTS * 3 * SC * PIECE
STEP_AT = tuple(sum(STEP_CHUNKS[:i]) for i in range(len(STEP_CHUNKS)))
NSTEP = len(STEP_CHUNKS)
STEP_OF = tuple(st for st in range(NSTEP) for _ in range(STEP_CHUNKS[st]))
SEQ = (("w1", 0), ("w3", 0)) + tuple((w, ch - (w == "w2")) for ch in range(1, NFC)
                                     for w in ("w1", "w3", "w2")) + (("w2", NFC - 1),)
NSEQ = len(SEQ)
AT_SEQ = {piece: i for i, piece in enumerate(SEQ)}
assert NSTEP % SLOTS == 0


def slot_views(s, slot, nch):
    v = [s.M[:, (slot * 3 + i) * SC * PIECE:(slot * 3 + i) * SC * PIECE + nch * PIECE] for i in range(3)]
    return (v[0].rearrange("p (k n) -> p k n", k=KC), v[1].rearrange("p (k n) -> p k n", k=KC),
            v[2].rearrange("p (c n) -> p c n", n=D))


def load_step(sp, s, e, step, w13_free=None, w2_free=None):
    slot, nch, f0 = step % SLOTS, STEP_CHUNKS[step], STEP_AT[step] * P
    v1, v3, v2 = slot_views(s, slot, nch)

    def of(w):
        return w[e] if isinstance(e, int) else w[ds(e, 1)].rearrange("a r n -> (a r) n")

    if w13_free:
        w13_free()
    for dst, name in ((v1, "w1"), (v3, "w3")):
        sp.dma_start(dst, of(s.a[name]).rearrange("(k p) n -> p k n", p=P)[:, :, f0:f0 + nch * P])\
            .then_inc(s.w13_in[slot], 16)
    if w2_free:
        w2_free()
    sp.dma_start(v2, of(s.a["w2"])[f0:f0 + nch * P, :].rearrange("(c p) n -> p c n", p=P))\
        .then_inc(s.w2_in[slot], 16)


def phase_experts(nc, s):
    a, K, PS, M, sem = s.a, s.K, s.PS, s.M, s.sem
    ar = Arena(M, s.n_main, RING)

    NB = 4
    xe = ar.get(KC, CAP)
    xn = ar.get(KC, CAP)
    xg, xgp = ar.get(D), ar.get(D, rows=CAP_P)
    yeT = ar.get(KC, CAP)
    ye, yep = ar.get(D), ar.get(D, rows=CAP_P)
    sg = [ar.get(CAP) for _ in range(NB)]
    hid = [ar.get(CAP) for _ in range(NB)]
    ig, igp, iw, iwp = (s.lora_up[0:r, 2, o:o + 1].bitcast(I32)
                        for r, o in ((P, 0), (CAP_P, 1), (P, 2), (CAP_P, 3)))
    gt, gtp = s.lora_up[:, 2, 4:5], s.lora_up[0:CAP_P, 2, 5:6]
    accps = [PS[:, (m // 3) * 512 + (m % 3) * CAP:(m // 3) * 512 + (m % 3 + 1) * CAP] for m in range(KC)]
    hps = [PS[:, (3 + b) * 512:(3 + b) * 512 + 2 * CAP] for b in range(NB)]
    swap = PS[:, 7 * 512:8 * 512]
    IN = ((40, range(0, 3)), (44, range(3, 6)), (48, range(6, KC)))
    OUT = (NSEQ + 3, NSEQ + 5, NSEQ + 7, NSEQ + 9)
    NIN, NOUT = len(IN), len(OUT)
    TURN = OUT[-1] + 1 - NSEQ

    ixg, gath, turns = sem("gather_index"), sem("gathered"), sem("pool_turns_e")
    used = sem("piece_used")
    swap_ps, swap_free = sem("swap_filled"), sem("swap_free")
    xn_a, xn_d, xe_a, xe_d = (sem("next_by_act"), sem("next_by_dve"), sem("inputs_by_act"),
                              sem("inputs_by_dve"))
    sg_r, h_r = sem("hidden_sigmoid"), sem("hidden_ready")
    y_a, y_d = sem("expert_out_by_act"), sem("expert_out_by_dve")
    gate_r, ye_a, ye_d = sem("gates_staged"), sem("rows_by_act"), sem("rows_by_dve")
    rows_free = sem("row_buffers_free")
    ixw, scat, dvo = sem("scatter_index"), sem("scattered"), sem("dve_own_d")

    def swaps_in(e):
        return e * (NIN + NOUT) + (NIN - (NIN + NOUT))

    def swaps_out(e):
        return e * (NIN + NOUT) + 2 * NIN

    SWAPS_LAST = E * NIN + (E - 1) * NOUT

    def piece(v):
        w, ch = SEQ[v]
        st = STEP_OF[ch]
        c = ch - STEP_AT[st]
        v1, v3, v2 = slot_views(s, st % SLOTS, STEP_CHUNKS[st])
        if w == "w2":
            return v2[:, c, :].rearrange("p (k n) -> p k n", n=P)
        return (v1 if w == "w1" else v3)[:, :, c * P:(c + 1) * P]

    def experts(eng_loop, step, tail):
        for v in range(TURN):
            step(0, v, first=True)
        eng_loop(lambda e: ([step(e, v) for v in range(TURN, NSEQ)],
                            [step(e + 1, v) for v in range(TURN)]))
        for v in range(TURN, NSEQ):
            step(E - 1, v, last=True)
        tail()

    def parts():
        return ((0, slice(0, CAP_S)), (1, slice(CAP_S, CAP)))

    with nc.Block() as block:

        @block.sync
        def _(sp):
            def last_piece(w, step):
                return AT_SEQ[w, STEP_AT[step] + STEP_CHUNKS[step] - 1] + 1

            def reload(e, step, of, prev):
                load_step(sp, s, e, step, lambda: sp.wait_ge(used, of * NSEQ + last_piece("w3", prev)),
                          lambda: sp.wait_ge(used, of * NSEQ + last_piece("w2", prev)))

            with sp.Fori(0, E - 1) as e:
                for step in range(SLOTS, NSTEP):
                    reload(e, step, e, step - SLOTS)
                for step in range(SLOTS):
                    reload(e + 1, step, e, step + NSTEP - SLOTS)
            for step in range(SLOTS, NSTEP):
                reload(E - 1, step, E - 1, step - SLOTS)

        @block.gpsimd
        def _(pool):
            def gather(e):
                nc.gpsimd.tensor_copy(ig, s.idxT[:, ds(e, 1)])
                nc.gpsimd.tensor_copy(igp, s.idxT[0:CAP_P, ds(e + PB, 1)]).then_inc(ixg, 1)
                hold(pool, turns, (ixg, e + 1))
                for dst, ix in ((xg, ig), (xgp, igp)):
                    nc.gpsimd.indirect_dma_start(dst, None, s.xn_d,
                                                 bass.IndirectOffsetOnAxis(ap=ix, axis=0))\
                        .then_inc(gath, 16)

            def scatter(e):
                nc.gpsimd.tensor_copy(iw, s.idxT[:, ds(e, 1)])
                nc.gpsimd.tensor_copy(iwp, s.idxT[0:CAP_P, ds(e + PB, 1)]).then_inc(ixw, 1)
                hold(pool, turns, (ixw, e + 1), (ye_a, e + 2), (ye_d, e + 2))
                for src, ix in ((ye, iw), (yep, iwp)):
                    nc.gpsimd.indirect_dma_start(s.acc_d, bass.IndirectOffsetOnAxis(ap=ix, axis=0),
                                                 src, None, compute_op=ALU.add).then_inc(scat, 16)
                pool.wait_ge(scat, e * 32 + 32)
                pool.sem_inc(rows_free, 1)

            pool.sem_inc(rows_free, 1)
            gather(0)
            with pool.Fori(0, E - 1) as e:
                hold(pool, turns, (xn_a, e * 2 + 2), (xn_d, e + 1))
                gather(e + 1)
                scatter(e)
            scatter(E - 1)

        @block.tensor
        def _(pe):
            def inputs(ks):
                for j, k in enumerate(ks):
                    o = j * CAP
                    nc.tensor.transpose(swap[:, o:o + CAP_S], xg[:, k * P:(k + 1) * P], K["ident"])
                    last = nc.tensor.transpose(swap[:, o + CAP_S:o + CAP], xgp[:, k * P:(k + 1) * P],
                                               K["ident"][0:CAP_P, 0:CAP_P])
                last.then_inc(swap_ps, 1)

            def results(r):
                for j in range(4):
                    m = 4 * (r % 2) + j
                    c = slice(0, CAP_S) if r < 2 else slice(CAP_S, CAP)
                    last = nc.tensor.transpose(swap[0:CAP_S if r < 2 else CAP_P, j * P:(j + 1) * P],
                                               yeT[:, m, c], K["ident"])
                last.then_inc(swap_ps, 1)

            def step(e, v, first=False, last=False):
                w, ch = SEQ[v]
                b = ch % NB
                if v == 0:
                    pe.wait_ge(xe_a, e + 1)
                    pe.wait_ge(xe_d, e + 1)
                if w == "w1":
                    if ch >= NB:
                        pe.wait_ge(h_r, e * NFC + (ch - NB + 1))
                    elif ch < NFC % NB and not first:
                        pe.wait_ge(h_r, e * NFC + (ch - NFC % NB + 1))
                if w == "w2":
                    pe.wait_ge(h_r, e * NFC + (ch + 1))
                    if ch == 0 and not first:
                        pe.wait_ge(y_a, e)
                        pe.wait_ge(y_d, e)
                st = STEP_OF[ch]
                if ch == STEP_AT[st] and w != "w3":
                    slot, turn = st % SLOTS, st // SLOTS
                    one, sm = (32, s.w13_in[slot]) if w == "w1" else (16, s.w2_in[slot])
                    pe.wait_ge(sm, e * (NSTEP // SLOTS * one) + (turn + 1) * one)
                for k in range(KC):
                    if w == "w2":
                        ins = nc.tensor.matmul(accps[k], piece(v)[:, k, :], hid[b],
                                               start=(ch == 0 and k % 3 == 0), stop=(ch == NFC - 1),
                                               skip_group_check=True)
                    else:
                        half = 0 if w == "w1" else 1
                        ins = nc.tensor.matmul(hps[b][:, half * CAP:(half + 1) * CAP],
                                               piece(v)[:, k, :], xe[:, k, :],
                                               start=(k == 0), stop=(k == KC - 1))
                ins.then_inc(used, 1)
                for r, (at, ks) in enumerate(IN):
                    if v == at and not last:
                        if r == 0:
                            pe.wait_ge(gath, e * 32 + 64)
                        pe.wait_ge(swap_free, swaps_in(e + 1) + r)
                        inputs(ks)
                for r, at in enumerate(OUT):
                    if v + NSEQ == at and not first:
                        if r == 0:
                            pe.wait_ge(y_a, e)
                            pe.wait_ge(y_d, e)
                        pe.wait_ge(swap_free, swaps_out(e - 1) + r)
                        results(r)

            def loop(body):
                with pe.Fori(0, E - 1) as e:
                    body(e)

            def tail():
                pe.wait_ge(y_a, E)
                pe.wait_ge(y_d, E)
                for r in range(NOUT):
                    pe.wait_ge(swap_free, SWAPS_LAST + r)
                    results(r)

            pe.wait_ge(gath, 32)
            for r, (_, ks) in enumerate(IN):
                if r:
                    pe.wait_ge(swap_free, r)
                inputs(ks)
            experts(loop, step, tail)

        def tasks_of(table):
            def step(e, v, first=False, last=False):
                for fn in table.get(v, ()):
                    fn(e, last)
                if not first:
                    for fn in table.get(v + NSEQ, ()):
                        fn(e - 1, False)

            def tail():
                for v in range(NSEQ, NSEQ + TURN):
                    for fn in table.get(v, ()):
                        fn(E - 1, True)
            return step, tail

        def at(table, v, fn):
            table.setdefault(v, []).append(fn)

        @block.scalar
        def _(act):
            table = {}

            def inputs(r):
                def fn(e, last):
                    if last:
                        return
                    fill(e + 1, r)
                return fn

            def fill(e, r, first=False):
                act.wait_ge(swap_ps, r + 1 if first else swaps_in(e) + (r + 1))
                if r == 0 and not first:
                    act.wait_ge(xe_a, e)
                    act.wait_ge(xe_d, e)
                for j, k in enumerate(IN[r][1]):
                    for g, c in parts():
                        o = slice(j * CAP + c.start, j * CAP + c.stop)
                        ins = nc.scalar.activation(xn[:, k, c], swap[:, o], ACT.Identity,
                                                   scale=s.A2[:, k, g:g + 1], bias=s.B2[:, k, g:g + 1])
                ins.then_inc(xn_a, 1)
                act.wait_ge(xn_a, r // 2 + 1 if first else e * 2 + (r // 2 + 1))
                act.sem_inc(swap_free, 1)

            def take(e, first=False):
                act.wait_ge(xn_a, e * 2 + 2)
                act.wait_ge(xn_d, e + 1)
                if not first:
                    act.wait_ge(used, e * NSEQ + (AT_SEQ["w3", NFC - 1] + 1 - NSEQ))
                nc.scalar.activation(xe[:, 0:4, :], xn[:, 0:4, :], ACT.Copy).then_inc(xe_a, 1)

            def sigmoid(ch):
                def fn(e, last):
                    act.wait_ge(used, e * NSEQ + (AT_SEQ["w3", ch] + 1))
                    nc.scalar.activation(sg[ch % NB], hps[ch % NB][:, 0:CAP], ACT.Sigmoid).then_inc(sg_r, 1)
                return fn

            def sums_out(e, last):
                act.wait_ge(used, e * NSEQ + NSEQ)
                for m in range(3):
                    for g, c in parts():
                        ins = nc.scalar.activation(yeT[:, m, c], accps[m][:, c], ACT.Copy,
                                                   scale=s.G2[:, m, g:g + 1])
                ins.then_inc(y_a, 1)

            def rows_out(r):
                def fn(e, last):
                    act.wait_ge(swap_ps, SWAPS_LAST + r + 1 if last else swaps_out(e) + (r + 1))
                    if r == 0:
                        act.wait_ge(gate_r, e + 1)
                        act.wait_ge(rows_free, e + 1)
                    ins = nc.scalar.activation(ye[:, r * 512:(r + 1) * 512], swap, ACT.Copy, scale=gt)
                    ins.then_inc(swap_free, 1)
                    if r == 1:
                        act.wait_ge(swap_free, SWAPS_LAST + 2 if last else swaps_out(e) + 2)
                        act.sem_inc(ye_a, 1)
                return fn

            for r in (0, 2):
                at(table, IN[r][0], inputs(r))
            for ch in range(NFC):
                at(table, AT_SEQ["w3", ch], sigmoid(ch))
            at(table, AT_SEQ["w3", NFC - 1], lambda e, last: None if last else take(e + 1))
            at(table, NSEQ - 1, sums_out)
            for r in (0, 1):
                at(table, OUT[r], rows_out(r))

            act.sem_inc(ye_a, 1)
            fill(0, 0, True)
            fill(0, 2, True)
            take(0, True)

            def loop(body):
                with act.Fori(0, E - 1) as e:
                    body(e)

            step, tail = tasks_of(table)
            experts(loop, step, tail)

        @block.vector
        def _(dve):
            own, table = Chain(dve, dvo), {}
            dve.sem_inc(ye_d, 1)

            def fill(e, first=False):
                if first:
                    dve.wait_ge(swap_ps, 2)
                else:
                    dve.wait_ge(swap_ps, swaps_in(e) + 2)
                    dve.wait_ge(xe_a, e)
                    dve.wait_ge(xe_d, e)
                for j, k in enumerate(IN[1][1]):
                    for g, c in parts():
                        o = slice(j * CAP + c.start, j * CAP + c.stop)
                        ins = nc.vector.tensor_scalar(xn[:, k, c], swap[:, o], s.A2[:, k, g:g + 1],
                                                      s.B2[:, k, g:g + 1], ALU.mult, ALU.add)
                ins.then_inc(xn_d, 1)
                dve.wait_ge(xn_d, e + 1)
                dve.sem_inc(swap_free, 1)

            def inputs(e, last):
                if not last:
                    fill(e + 1)

            def take(e, first=False):
                dve.wait_ge(xn_a, e * 2 + 2)
                dve.wait_ge(xn_d, e + 1)
                if not first:
                    dve.wait_ge(used, e * NSEQ + (AT_SEQ["w3", NFC - 1] + 1 - NSEQ))
                nc.vector.tensor_copy(xe[:, 4:KC, :], xn[:, 4:KC, :]).then_inc(xe_d, 1)

            def hidden(ch):
                def fn(e, last):
                    b = ch % NB
                    dve.wait_ge(sg_r, e * NFC + (ch + 1))
                    own.link(nc.vector.tensor_tensor(sg[b], sg[b], hps[b][:, 0:CAP], ALU.mult))
                    nc.vector.tensor_tensor(hid[b], sg[b], hps[b][:, CAP:2 * CAP], ALU.mult)\
                        .then_inc(h_r, 1)
                return fn

            def sums_out(e, last):
                dve.wait_ge(used, e * NSEQ + NSEQ)
                for m in range(3, KC):
                    for g, c in parts():
                        ins = nc.vector.tensor_scalar(yeT[:, m, c], accps[m][:, c],
                                                      s.G2[:, m, g:g + 1], None, ALU.mult)
                ins.then_inc(y_d, 1)

            def gates(e, last):
                dve.wait_ge(ye_a, e + 1)
                dve.wait_ge(ye_d, e + 1)
                nc.vector.tensor_copy(gt, s.gateT[:, ds(e, 1)])
                nc.vector.tensor_copy(gtp, s.gateT[0:CAP_P, ds(e + PB, 1)]).then_inc(gate_r, 1)

            def rows_out(r):
                def fn(e, last):
                    dve.wait_ge(swap_ps, SWAPS_LAST + r + 1 if last else swaps_out(e) + (r + 1))
                    if r == 2:
                        dve.wait_ge(gate_r, e + 1)
                        dve.wait_ge(rows_free, e + 1)
                    nc.vector.tensor_scalar(yep[:, (r - 2) * 512:(r - 1) * 512], swap[0:CAP_P, :], gtp, None,
                                            ALU.mult).then_inc(swap_free, 1)
                    if r == 3:
                        dve.wait_ge(swap_free, SWAPS_LAST + 4 if last else swaps_out(e) + 4)
                        dve.sem_inc(ye_d, 1)
                return fn

            at(table, IN[1][0], inputs)
            for ch in range(NFC):
                at(table, AT_SEQ["w3", ch], hidden(ch))
            at(table, AT_SEQ["w3", NFC - 1], lambda e, last: None if last else take(e + 1))
            at(table, NSEQ - 1, sums_out)
            at(table, NSEQ, gates)
            for r in (2, 3):
                at(table, OUT[r], rows_out(r))

            fill(0, True)
            take(0, True)

            def loop(body):
                looped(dve, own, 0, E - 1, NFC, body)

            step, tail = tasks_of(table)
            experts(loop, step, tail)

def phase_final(nc, s):
    a, M, sem = s.a, s.M, s.sem
    ar = Arena(M, s.n_main)
    gf = ar.get(D)
    xt, yo, junk = [[ar.get(D) for _ in (0, 1)] for _ in range(3)]
    ssq, ms, root, rstd = [[s.st[:, i:i + 1] for i in (o, o + 1)] for o in (0, 2, 4, 8)]
    out_free = [sem(f"result_buffer_free{i}") for i in (0, 1)]
    g_in = sem("final_g_in")
    x_in = [sem(f"row_in{i}") for i in (0, 1)]
    y_out = [sem(f"result_written{i}") for i in (0, 1)]
    sq_r, ms_r, rt_r, rr_r, y_r = (sem("final_squared"), sem("final_mean_square"), sem("final_root"),
                                   sem("final_rstd"), sem("result_ready"))

    with nc.Block() as block:

        @block.sync
        def _(sp):
            sp.dma_start(gf, a["final_g"].to_broadcast([P, D])).then_inc(g_in, 16)
            for i in (0, 1):
                sp.sem_inc(out_free[i], 1)
                sp.dma_start(xt[i], s.acc_d[i * P:(i + 1) * P, :]).then_inc(x_in[i], 16)
            with sp.Fori(0, NT // 2 - 1) as j:
                for i in (0, 1):
                    sp.wait_ge(y_r, j * 2 + (i + 1))
                    sp.dma_start(a["out_y"][ds(j * (2 * P) + i * P, P), :], yo[i]).then_inc(y_out[i], 16)
                    sp.dma_start(xt[i], s.acc_d[ds(j * (2 * P) + (i + 2) * P, P), :])\
                        .then_inc(x_in[i], 16)
                for i in (0, 1):
                    sp.wait_ge(y_out[i], j * 16 + 16)
                    sp.sem_inc(out_free[i], 1)
            for i in (0, 1):
                n = NT - 2 + i
                sp.wait_ge(y_r, n + 1)
                sp.dma_start(a["out_y"][n * P:(n + 1) * P, :], yo[i]).then_inc(y_out[i], 16)
            for i in (0, 1):
                sp.wait_ge(y_out[i], 16 * (NT // 2))

        @block.scalar
        def _(act):
            with act.Fori(0, NT // 2) as j:
                for i in (0, 1):
                    act.wait_ge(x_in[i], j * 16 + 16)
                    nc.scalar.activation(junk[i], xt[i], ACT.Square, accum_out=ssq[i]).then_inc(sq_r, 1)
                for i in (0, 1):
                    act.wait_ge(ms_r, j * 2 + (i + 1))
                    nc.scalar.activation(root[i], ms[i], ACT.Sqrt).then_inc(rt_r, 1)

        @block.vector
        def _(dve):
            dve.wait_ge(g_in, 16)
            with dve.Fori(0, NT // 2) as j:
                for i in (0, 1):
                    dve.wait_ge(sq_r, j * 2 + (i + 1))
                    nc.vector.tensor_scalar(ms[i], ssq[i], 1.0 / D, RMS_EPS, ALU.mult, ALU.add)\
                        .then_inc(ms_r, 1)
                for i in (0, 1):
                    dve.wait_ge(rt_r, j * 2 + (i + 1))
                    nc.vector.reciprocal(rstd[i], root[i]).then_inc(rr_r, 1)
                    dve.wait_ge(rr_r, j * 2 + (i + 1))
                    dve.wait_ge(out_free[i], j + 1)
                    nc.vector.scalar_tensor_tensor(out=yo[i], in0=xt[i], scalar=rstd[i], in1=gf,
                                                   op0=ALU.mult, op1=ALU.mult).then_inc(y_r, 1)


_OUT = (("out_y", (T, D)), ("out_state", (2, NH, HS, HS)))


def kernel(x_prompt, x_sample, state_wkv, c, c_ctx, norm1_g, norm2_g, w_mod, b_mod, w_in, conv_dw, conv_b,
           conv_ln_g, conv_ln_b, rwkv_w0, rwkv_w_up, rwkv_a0, rwkv_a_up, rwkv_g_up, rwkv_k_k, rwkv_k_a,
           rwkv_r_k, rwkv_gn_g, rwkv_gn_b, w_out, router, exp_w1, exp_w3, exp_w2, final_norm_g):
    import numpy as _np
    import concourse.bacc as _bacc
    from concourse import mybir as _mybir
    from concourse.bass_utils import run_bass_kernel_spmd as _run

    def columns(v):
        return _np.asarray(v).reshape(-1, P).T

    taps = _np.asarray(conv_dw)[0].reshape(KW, NP_, P).transpose(2, 1, 0).reshape(P, NP_ * KW)
    bias = _np.concatenate([columns(v) for d in (0, 1) for v in (rwkv_w0[0, d], rwkv_a0[0, d])], 1)
    cond = _np.stack([columns(c[0]), columns(c_ctx)], 2).reshape(P, 16)
    vectors = _np.concatenate([columns(norm1_g[0]), columns(norm2_g[0]), columns(b_mod[0]), taps,
                               columns(conv_b[0]), columns(conv_ln_g[0]), columns(conv_ln_b[0]), bias,
                               columns(rwkv_k_k[0]), columns(rwkv_k_a[0]), columns(rwkv_r_k[0].reshape(-1)),
                               columns(rwkv_gn_g[0]), columns(rwkv_gn_b[0]), cond], 1)
    arrays = {
        "x": _np.concatenate([_np.asarray(x_sample)[0], _np.asarray(x_prompt)[0]], 0),
        "vectors": vectors, "table": _np.concatenate(list(constant_table().values()), 1),
        "w_mod": w_mod[0], "w_in": w_in[0], "w_up": rwkv_w_up[0], "a_up": rwkv_a_up[0],
        "g_up": rwkv_g_up[0], "state": state_wkv[0, 0], "w_out": w_out[0], "router": router[0],
        "w1": exp_w1[0], "w3": exp_w3[0], "w2": exp_w2[0],
        "final_g": _np.asarray(final_norm_g).reshape(1, D),
    }
    nc = _bacc.Bacc("TRN2", target_bir_lowering=False, num_devices=1)
    f32 = _mybir.dt.float32
    data, a = {}, {}
    for name, v in arrays.items():
        data[f"in_{name}"] = _np.ascontiguousarray(v)
        a[name] = nc.dram_tensor(f"in_{name}", data[f"in_{name}"].shape, f32, kind="ExternalInput").ap()
    for name, shape in _OUT:
        a[name] = nc.dram_tensor(name, shape, f32, kind="ExternalOutput").ap()
    build(nc, a)
    r = _run(nc, [data], core_ids=[0]).results[0]
    y, state = r["out_y"], r["out_state"]
    return y[None, TS:], y[None, :TS], state[None, None]
```

```python
import concourse.bass as bass
from concourse import mybir
from contextlib import ExitStack
import numpy as np

P = 128
D = 1024
KC = D // P
TS, TP = 1024, 256
T = TS + TP
NT = T // P
NTS = TS // P
CW = 512
NP_ = CW // P
HS = 64
NH = CW // HS
KW = 31
PAD = (KW - 1) // 2
GRID = 64
WIN = GRID + 2 * PAD
NWIN = T // GRID
C = 64
NCH = T // C
NCS = TS // C
NCP = TP // C
E = 16
FF = 2816
NFC = FF // P
CAP_S = 2 * TS // E
CAP_P = 2 * TP // E
CAP = CAP_S + CAP_P
PB = 32
LEVELS = (2, 4, 8, 16, 32)
C0 = float(np.exp(-0.5))
RMS_EPS, LN_EPS, GN_EPS = 1e-6, 1e-5, 64e-5
STEP_CHUNKS = (4, 4, 4, 4, 3, 3)
SLOTS = 3
COLS3 = ((0, 512), (512, 512), (1024, 256))


def constant_table():
    t = {}
    i = np.arange(P)
    ident = np.eye(P, dtype=np.float32)
    t["ident"] = ident
    same = (i[:, None] // HS == i[None] // HS)
    t["blockones"] = same.astype(np.float32)
    t["fold"] = (i[:, None] % HS == np.arange(HS)[None]).astype(np.float32)
    t["lnmean"] = np.full((P, P), 1.0 / CW, np.float32)
    r, c = i[:, None] % C, i[None] % C
    for d in (0, 1):
        before = (r < c) if d == 0 else (r > c)
        t[f"strict{d}"] = (same & before).astype(np.float32)
        t[f"incl{d}"] = (same & (before | (r == c))).astype(np.float32)
        after = (r > c) if d == 0 else (r < c)
        for b in (1,) + LEVELS:
            off = (r // (2 * b) == c // (2 * b)) & (r // b != c // b)
            m = ident - (same & after & off)
            t[f"lev{d}_{b}"] = m.astype(np.float32)
            col = np.arange(HS)[None]
            rr = i[:, None] % C
            aft = (rr > col) if d == 0 else (rr < col)
            bef = (rr < col) if d == 0 else (rr > col)
            of = (rr // (2 * b) == col // (2 * b)) & (rr // b != col // b)
            mc = (rr == col).astype(np.float32) - (aft & of)
            t[f"levc{d}_{b}"] = mc.astype(np.float32)
            if b == 1:
                t[f"first{d}"] = m.T.astype(np.float32)
                t[f"firstc{d}"] = -(bef & of).astype(np.float32)
                del t[f"lev{d}_1"], t[f"levc{d}_1"]
    reset = np.ones((P, NP_ * C), np.float32)
    reset[:, ::C] = 0
    t["reset"] = reset
    return t


def table_columns(t):
    at, cols = 0, {}
    for n, a in t.items():
        cols[n] = (at, a.shape[1])
        at += a.shape[1]
    return cols, at


VECTORS = (("n1", 8), ("n2", 8), ("bmod", 48), ("dw", NP_ * KW), ("db", 4), ("lng", 4), ("lnb", 4),
           ("bias_wa", 16), ("k_k", 4), ("k_a", 4), ("r_k", 4), ("gng", 4), ("gnb", 4), ("cond", 16))


class Chain:

    def __init__(self, eng, sem):
        self.eng, self.sem, self.n, self.at, self.last = eng, sem, 0, 0, None

    def link(self, ins):
        self.n += 1
        ins.then_inc(self.sem, 1)
        self.eng.wait_ge(self.sem, self.at + self.n)
        self.last = ins
        return ins


class Shared:
    pass


class Arena:

    def __init__(self, main, size, at=0):
        self.main, self.size, self.at = main, size, at

    def get(self, *shape, rows=P):
        n = int(np.prod(shape))
        v = self.main[0:rows, self.at:self.at + n]
        self.at += n
        assert self.at <= self.size, (self.at, self.size)
        if len(shape) == 2:
            v = v.rearrange("p (a b) -> p a b", b=shape[1])
        if len(shape) == 3:
            v = v.rearrange("p (a b c) -> p a b c", b=shape[1], c=shape[2])
        return v


def hold(pool, turns, *waits):
    for sm, value in waits:
        pool.wait_ge(sm, value)
        pool.sem_inc(turns, 1)


F32, I32, U32 = mybir.dt.float32, mybir.dt.int32, mybir.dt.uint32
ALU, ACT, AX = mybir.AluOpType, mybir.ActivationFunctionType, mybir.AxisListType
ds = bass.ds


def build(nc, a, phases=5):
    with ExitStack() as ctx:
        s = Shared()
        s.a = a

        def sem(name):
            return ctx.enter_context(nc.semaphore(name))

        def dram(name, shape):
            return nc.dram_tensor(name, shape, F32, kind="Internal").ap()

        def small(name, shape, dt=F32):
            return ctx.enter_context(nc.sbuf_tensor(name, shape, dt))

        s.sem, s.small = sem, small
        s.g1_d = dram("gate1_rows", (2, D))
        s.conv_d = dram("conv_out", (P, NP_ * T))
        s.y_d = dram("wkv_out", (2, NCH, P, NP_ * HS))
        s.xg_d = dram("gate_lora", (P, T))
        s.gates_d = dram("gates", (2, NCH, P, 2 * NP_ * C))
        s.kd_d = dram("keys_out", (2, P, NP_, T))
        s.xn_d = dram("normed_rows", (T, D))
        s.acc_d = dram("residual_rows", (T, D))

        cols, n_const = table_columns(constant_table())
        s.consts = small("consts", [P, n_const])
        s.K = {n: s.consts[:, o:o + w] for n, (o, w) in cols.items()}
        s.vecs = small("vecs", [P, sum(w for _, w in VECTORS)])
        s.V, at = {}, 0
        for n, w in VECTORS:
            s.V[n] = s.vecs[:, at:at + w]
            at += w
        s.condT = small("condT", [P, KC, 2])
        s.modT = small("modT", [P, 48, 2])
        s.A1, s.A2 = small("A1", [P, KC, 2]), small("A2", [P, KC, 2])
        s.lora_up = small("lora_up", [P, 4, CW])
        s.st = small("row_stats", [P, 12])
        s.taps = small("taps", [P, KW])
        s.B1, s.B2, s.G2 = s.modT[:, 0:8, :], s.modT[:, 24:32, :], s.modT[:, 40:48, :]
        s.gateT, s.idxF = s.lora_up[:, 0, 0:64], s.lora_up[:, 0, 64:128]
        s.idxT = s.lora_up[:, 0, 128:192].bitcast(I32)
        s.w13_in = [sem(f"w1_w3_in{i}") for i in range(SLOTS)]
        s.w2_in = [sem(f"w2_in{i}") for i in range(SLOTS)]
        n_main = (nc.sbuf_usable_end - nc.sbuf_base) // 4 - 64
        s.M = small("main", [P, n_main])
        s.n_main = n_main
        s.PS = ctx.enter_context(nc.psum_tensor("PS", [P, 8 * 512], F32))
        s.ar = Arena(s.M, n_main)
        s.rkv = s.ar.get(3 * NP_, T)
        s.rT, s.kT, s.vT = s.rkv[:, 0:4, :], s.rkv[:, 4:8, :], s.rkv[:, 8:12, :]
        s.loraT = s.ar.get(2, T)
        s.mark = s.ar.at
        for phase in (phase_project, phase_wkv, phase_mix, phase_experts, phase_final)[:phases]:
            own = []

            def phase_sem(name, own=own):
                own.append(nc.alloc_semaphore(name))
                return own[-1]

            s.sem = phase_sem
            phase(nc, s)
            nc.clear_and_free_semaphores(own)
            nc.all_engine_barrier()


def phase_project(nc, s):
    a, K, V, PS, M, sem = s.a, s.K, s.V, s.PS, s.M, s.sem
    ar = Arena(M, s.n_main, s.mark)
    hT = ar.get(KC, T)
    mark = ar.at
    u = ar.get(NP_, NWIN * WIN)
    sq = M[:, mark:mark + NP_ * T].rearrange("p (k n) -> p k n", n=T)
    lrs = M[:, mark + NP_ * T:mark + NP_ * T + T]
    mark = ar.at
    cv = ar.get(NP_, T)
    ws = [ar.get(KC, P) for _ in range(4)]
    late = [M[:, at:at + 4096].rearrange("p (k n) -> p k n", n=512)
            for at in (s.mark, ar.at - 4096)]
    s.kk = M[:, s.mark + 4096:s.mark + 4096 + NP_ * T].rearrange("p (k t) -> p k t", t=T)
    kn = sq
    KT = T // 4
    knps = [PS[:, 6 * 512 + 96:6 * 512 + 96 + KT], PS[:, 7 * 512:7 * 512 + KT]]
    xgT = ar.get(T)
    XG = 2
    xt = [M[:, ar.at - (n + 1) * D:ar.at - n * D] for n in range(NT)]
    assert ar.at - NT * D >= mark
    X_WS = -(-(ar.at - mark - NP_ * T) // D)
    junk = [hT[:, i, 0:D] for i in (0, 1)]
    sums, roots, rstds = ar.get(NT), ar.get(NT), ar.get(NT)
    slab = [M[:, i * 4096:(i + 1) * 4096].rearrange("p (k n) -> p k n", n=512) for i in range(4)]
    rows = ar.get(512, rows=2)
    ge = [s.rkv[:, i, :] for i in (0, 1)]
    modps = PS[:, 6 * 512:6 * 512 + 96].rearrange("p (m j) -> p m j", j=2)
    rowps = PS[0:2, 7 * 512:8 * 512]
    trp = [PS[:, 0:1024], PS[:, 1024:2048]]
    pset = [PS[:, 0:T], PS[:, 3 * 512:3 * 512 + T]]
    w_mod = a["w_mod"].rearrange("(k p) n -> p k n", p=P)
    w_in = a["w_in"].rearrange("(k p) n -> p k n", p=P)
    BODY, FULL = 4, 5
    NPC = 23

    tables, ups, zero = sem("tables_loaded"), sem("up_weights_loaded"), sem("zeros_written")
    x_in = [sem(f"x_in{i}") for i in range(NT // XG)]
    mod_in = [sem(f"w_mod_in{i}") for i in range(4)]
    late_in = [sem(f"w_mod_late_in{i}") for i in range(2)]
    mod_used, late_used = sem("w_mod_used"), sem("w_mod_late_used")
    k_sq, k_ps, k_max, k_root = sem("k_squared"), sem("k_norm_psum"), sem("k_norm"), sem("k_root")
    kk_done = sem("kk_ready")
    row_ps, row_r = sem("mod_rows_psum"), sem("mod_rows")
    cond_sig, cond_ready, mod_ready = sem("cond_sigmoid"), sem("cond_ready"), sem("mod_ready")
    sq_done, ms_done, rs_done = sem("row_squares"), sem("row_mean_square"), sem("row_root")
    rr_done = sem("row_rstd")
    xn_done, tr_done = sem("xn_ready"), sem("x_transposed")
    h_act, h_dve = sem("h_by_act"), sem("h_by_dve")
    win = [sem(f"w_in_in{i}") for i in range(4)]
    pr_done = sem("projected")
    free = [sem(f"psum_set_free{i}") for i in range(2)]
    gate_sig, u_done = sem("gate_sigmoid"), sem("u_ready")
    xg_out = sem("gate_lora_written")
    g1_ready, g1_out = sem("g1_ready"), sem("g1_written")
    dvo, conv_own = sem("dve_own_a"), sem("taps_staged")
    conv_done, mean_ps, cen = sem("conv_summed"), sem("ln_mean_psum"), sem("ln_centered")
    csq, var_ps, var_done, lrs_done = (sem("ln_squared"), sem("ln_var_psum"), sem("ln_var"),
                                       sem("ln_rstd"))
    scaled, aff_done, sil_sig, cout = (sem("ln_scaled"), sem("ln_affine"), sem("silu_sigmoid"),
                                       sem("conv_out_ready"))
    conv_spill = sem("conv_written")

    with nc.Block() as block:

        @block.sync
        def _(sp):
            sp.dma_start(s.vecs[:, :], a["vectors"]).then_inc(tables, 16)
            sp.dma_start(s.consts[:, :], a["table"]).then_inc(tables, 16)
            for i in range(4):
                sp.dma_start(slab[i], w_mod[:, :, i * 512:(i + 1) * 512]).then_inc(mod_in[i], 16)
            for n in range(NT // XG):
                for g in range(XG):
                    t = n * XG + g
                    sp.dma_start(xt[t], a["x"][t * P:(t + 1) * P, :]).then_inc(x_in[n], 16)
            sp.wait_ge(zero, 1)
            for d in (0, 1):
                sp.dma_start(s.lora_up[d * HS:(d + 1) * HS, d, :], a["w_up"][d]).then_inc(ups, 16)
                sp.dma_start(s.lora_up[d * HS:(d + 1) * HS, 2 + d, :], a["a_up"][d]).then_inc(ups, 16)
            sp.wait_ge(tr_done, X_WS)
            for n, ch in enumerate((4, 0, 5, 1, 6, 2, 7, 3)):
                if n >= 4:
                    sp.wait_ge(pr_done, n - 3)
                sp.dma_start(ws[n % 4], w_in[:, :, ch * P:(ch + 1) * P]).then_inc(win[n % 4], 16)
            with sp.Fori(2, FULL) as j:
                for i in range(4):
                    sp.wait_ge(pr_done, j * 4 + (i - 3))
                    sp.dma_start(ws[i], w_in[:, :, ds(j * 512 + i * P, P)]).then_inc(win[i], 16)
            for n in range(4 * FULL, NPC):
                sp.wait_ge(pr_done, n - 3)
                sp.dma_start(ws[n % 4], w_in[:, :, n * P:(n + 1) * P]).then_inc(win[n % 4], 16)
            sp.wait_ge(pr_done, NPC)
            for i in range(2):
                sp.dma_start(late[i], w_mod[:, :, (4 + i) * 512:(5 + i) * 512]).then_inc(late_in[i], 16)
            with sp.Fori(1, 4) as j:
                for i in range(2):
                    sp.wait_ge(late_used, j * 2 + (i - 1))
                    sp.dma_start(late[i], w_mod[:, :, ds(j * 1024 + (4 + i) * 512, 512)])\
                        .then_inc(late_in[i], 16)
            sp.wait_ge(free[0], 13)
            sp.dma_start(s.xg_d, xgT).then_inc(xg_out, 16)
            sp.wait_ge(cout, NP_)
            sp.dma_start(s.conv_d, cv.rearrange("p a b -> p (a b)")).then_inc(conv_spill, 16)
            sp.wait_ge(g1_ready, 1)
            for j in range(2):
                sp.dma_start(s.g1_d[j].rearrange("(k p) -> p k", p=P), s.modT[:, 16:24, j],
                             allow_slow_non_contiguous=True).then_inc(g1_out, 16)
            sp.wait_ge(g1_out, 32)
            sp.wait_ge(conv_spill, 16)
            sp.wait_ge(ups, 64)
            sp.wait_ge(xg_out, 16)

        @block.gpsimd
        def _(pool):
            nc.gpsimd.memset(s.lora_up[:, :, :], 0.0).then_inc(zero, 1)
            nc.gpsimd.memset(u[:, :, :], 0.0).then_inc(zero, 1)

        @block.tensor
        def _(pe):
            for sm in (h_act, h_dve):
                pe.sem_inc(sm, 2)
            for sm in free:
                pe.sem_inc(sm, 1)

            def modulate(weights, n, used):
                for k in range(KC):
                    last = nc.tensor.matmul(rowps, s.condT[:, k, :], weights[:, k, :],
                                            start=(k == 0), stop=(k == KC - 1))
                last.then_inc(row_ps, 1)
                pe.wait_ge(row_r, n + 1)
                for m in range(4):
                    last = nc.tensor.transpose(modps[:, 4 * n + m, :], rows[:, m * P:(m + 1) * P],
                                               K["ident"][0:2, 0:2])
                last.then_inc(used, 1)

            pe.wait_ge(cond_ready, 1)
            for n in range(4):
                pe.wait_ge(mod_in[n], 16)
                modulate(slab[n], n, mod_used)

            for n in range(NT):
                i = n % 2
                pe.wait_ge(xn_done, n + 1)
                pe.wait_ge(h_act, n + 1)
                pe.wait_ge(h_dve, n + 1)
                for k in range(KC):
                    last = nc.tensor.transpose(trp[i][:, k * P:(k + 1) * P], xt[n][:, k * P:(k + 1) * P],
                                               K["ident"])
                last.then_inc(tr_done, 1)
            pe.wait_ge(h_act, NT + 2)
            pe.wait_ge(h_dve, NT + 2)

            def project(j, i):
                pe.wait_ge(win[i], j * 16 + 16)
                pe.wait_ge(free[i % 2], j * 2 + (i // 2 + 1))
                for c0, w in COLS3:
                    for k in range(KC):
                        last = nc.tensor.matmul(pset[i % 2][:, c0:c0 + w], ws[i][:, k, :],
                                                hT[:, k, c0:c0 + w], start=(k == 0), stop=(k == KC - 1))
                last.then_inc(pr_done, 1)

            with pe.Fori(0, FULL) as j:
                for i in range(BODY):
                    project(j, i)
            for i in range(NPC - BODY * FULL):
                project(FULL, i)
                if i == 1:
                    for n in range(4 * NP_):
                        pe.wait_ge(k_sq, n // 4 + 1)
                        if n >= 2:
                            pe.wait_ge(k_max, n - 1)
                        nc.tensor.matmul(knps[n % 2], K["blockones"], kn[:, n // 4, n % 4 * KT:(n % 4 + 1) * KT],
                                         start=True, stop=True).then_inc(k_ps, 1)

            pe.wait_ge(conv_done, NP_)
            pe.wait_ge(free[0], 13)
            pe.wait_ge(free[1], 12)
            for c0, w in COLS3:
                for k in range(NP_):
                    last = nc.tensor.matmul(PS[:, c0:c0 + w], K["lnmean"], cv[:, k, c0:c0 + w],
                                            start=(k == 0), stop=(k == NP_ - 1))
            last.then_inc(mean_ps, 1)

            def modulate_late(n):
                if n == 0:
                    pe.wait_ge(k_max, 4 * NP_)
                pe.wait_ge(late_in[n % 2], 16 * (n // 2 + 1))
                modulate(late[n % 2], 4 + n, late_used)

            for n in range(3):
                modulate_late(n)
            for k in range(NP_):
                pe.wait_ge(csq, k + 1)
                for c0, w in COLS3:
                    last = nc.tensor.matmul(PS[:, 3 * 512 + c0:3 * 512 + c0 + w], K["lnmean"],
                                            sq[:, k, c0:c0 + w], start=(k == 0), stop=(k == NP_ - 1))
            last.then_inc(var_ps, 1)
            for n in range(3, 8):
                modulate_late(n)

        @block.scalar
        def _(act):
            act.wait_ge(tables, 32)
            cond = V["cond"].rearrange("p (k j) -> p k j", j=2)
            nc.scalar.activation(s.condT[:, :, :], cond, ACT.Sigmoid).then_inc(cond_sig, 1)

            def take_rows(n):
                act.wait_ge(row_ps, n + 1)
                nc.scalar.activation(rows, rowps, ACT.Copy).then_inc(row_r, 1)

            def squares(tiles):
                for n in tiles:
                    if n % XG == 0:
                        act.wait_ge(x_in[n // XG], 16 * XG)
                    if n >= 2:
                        act.wait_ge(sq_done, n - 1)
                    nc.scalar.activation(junk[n % 2], xt[n], ACT.Square, accum_out=sums[:, n:n + 1])\
                        .then_inc(sq_done, 1)

            for n in range(3):
                take_rows(n)
            squares(range(4))
            take_rows(3)
            squares(range(4, NT))
            act.wait_ge(ms_done, 1)
            nc.scalar.activation(roots, sums, ACT.Sqrt).then_inc(rs_done, 1)
            act.wait_ge(mod_ready, 1)
            for n in range(NT):
                i, g = n % 2, 0 if n < NTS else 1
                act.wait_ge(tr_done, n + 1)
                for k in range(4):
                    last = nc.scalar.activation(hT[:, k, n * P:(n + 1) * P], trp[i][:, k * P:(k + 1) * P],
                                                ACT.Identity, scale=s.A1[:, k, g:g + 1],
                                                bias=s.B1[:, k, g:g + 1])
                last.then_inc(h_act, 1)

            with act.Fori(0, 4) as j:
                act.wait_ge(pr_done, j * 2 + 1)
                act.wait_ge(u_done, j + 1)
                nc.scalar.activation(ge[0], pset[0], ACT.Sigmoid).then_inc(gate_sig, 1)
                act.wait_ge(gate_sig, j + 1)
                act.sem_inc(free[0], 1)
            act.wait_ge(u_done, 5)
            with act.Fori(0, 6) as j:
                for i in range(2):
                    act.wait_ge(pr_done, j * 2 + (9 + i))
                    nc.scalar.activation(s.rkv[:, ds(j * 2 + i, 1), :].rearrange("p a b -> p (a b)"),
                                         pset[i], ACT.Copy).then_inc(free[i], 1)
            for n, fn in enumerate((ACT.Tanh, ACT.Copy, ACT.Sigmoid)):
                act.wait_ge(pr_done, 21 + n)
                nc.scalar.activation(s.loraT[:, n, :] if n < 2 else xgT, pset[n % 2], fn)\
                    .then_inc(free[n % 2], 1)
                if n == 0:
                    act.wait_ge(conv_done, NP_)
                    act.wait_ge(free[1], 9)
                    for k in range(NP_):
                        nc.scalar.activation(kn[:, k, :], s.kT[:, k, :], ACT.Square,
                                             scale=V["k_k"][:, k:k + 1]).then_inc(k_sq, 1)
                if n == 1:
                    for k in range(NP_):
                        act.wait_ge(k_max, 4 * k + 4)
                        nc.scalar.activation(kn[:, k, :], kn[:, k, :], ACT.Sqrt).then_inc(k_root, 1)
            take_rows(4)
            take_rows(5)
            for k in range(NP_):
                act.wait_ge(cen, k + 1)
                act.wait_ge(kk_done, k + 1)
                nc.scalar.activation(sq[:, k, :], cv[:, k, :], ACT.Square).then_inc(csq, 1)
            take_rows(6)
            act.wait_ge(var_done, 1)
            nc.scalar.activation(lrs, lrs, ACT.Sqrt).then_inc(lrs_done, 1)
            take_rows(7)
            for k in range(NP_):
                act.wait_ge(scaled, k + 1)
                nc.scalar.activation(cv[:, k, :], cv[:, k, :], ACT.Identity, scale=V["lng"][:, k:k + 1],
                                     bias=V["lnb"][:, k:k + 1]).then_inc(aff_done, 1)
                act.wait_ge(aff_done, k + 1)
                nc.scalar.activation(sq[:, k, :], cv[:, k, :], ACT.Sigmoid).then_inc(sil_sig, 1)
                if k == 1:
                    take_rows(8)
            for n in range(9, 12):
                take_rows(n)

        @block.vector
        def _(dve):
            own = Chain(dve, dvo)
            dve.sem_inc(u_done, 1)
            cond = V["cond"].rearrange("p (k j) -> p k j", j=2)
            dve.wait_ge(cond_sig, 1)
            nc.vector.tensor_tensor(s.condT[:, :, :], s.condT[:, :, :], cond, ALU.mult)\
                .then_inc(cond_ready, 1)

            def mod_out(lo, n):
                b = V["bmod"][:, lo:lo + n].unsqueeze(2).to_broadcast([P, n, 2])
                return nc.vector.tensor_tensor(s.modT[:, lo:lo + n, :], modps[:, lo:lo + n, :], b, ALU.add)

            def one_plus_times(out, sc, norm):
                g = norm.unsqueeze(2).to_broadcast([P, KC, 2])
                return nc.vector.scalar_tensor_tensor(out=out[:, :, :], in0=sc, scalar=1.0, in1=g,
                                                      op0=ALU.add, op1=ALU.mult)

            dve.wait_ge(mod_used, 4)
            own.link(mod_out(0, 16))
            one_plus_times(s.A1, s.modT[:, 8:16, :], V["n1"]).then_inc(mod_ready, 1)
            dve.wait_ge(mod_ready, 1)

            dve.wait_ge(sq_done, NT)
            nc.vector.tensor_scalar(sums, sums, 1.0 / D, RMS_EPS, ALU.mult, ALU.add).then_inc(ms_done, 1)
            dve.wait_ge(rs_done, 1)
            nc.vector.reciprocal(rstds, roots).then_inc(rr_done, 1)
            dve.wait_ge(rr_done, 1)
            for n in range(NT + 1):
                if n < NT:
                    nc.vector.tensor_scalar(xt[n], xt[n], rstds[:, n:n + 1], None, ALU.mult)\
                        .then_inc(xn_done, 1)
                m = n - 1
                if m >= 0:
                    i, g = m % 2, 0 if m < NTS else 1
                    dve.wait_ge(tr_done, m + 1)
                    for k in range(4, KC):
                        last = nc.vector.tensor_scalar(hT[:, k, m * P:(m + 1) * P],
                                                       trp[i][:, k * P:(k + 1) * P],
                                                       s.A1[:, k, g:g + 1], s.B1[:, k, g:g + 1],
                                                       ALU.mult, ALU.add)
                    last.then_inc(h_dve, 1)

            dve.wait_ge(zero, 2)
            base, n0 = own.n, 2
            with dve.Fori(0, NP_) as j:
                own.at = j * n0
                dve.wait_ge(gate_sig, j + 1)
                dve.wait_ge(pr_done, j * 2 + 2)
                uc = u[:, ds(j, 1), :].rearrange("p a (w x) -> p (a w) x", x=WIN)
                own.link(nc.vector.tensor_tensor(
                    uc[:, :, PAD:PAD + GRID], ge[0].rearrange("p (w x) -> p w x", x=GRID),
                    pset[1].rearrange("p (w x) -> p w x", x=GRID), ALU.mult))
                dve.sem_inc(free[1], 1)
                w0 = TS // GRID
                nc.vector.tensor_copy(uc[:, w0 + 1:NWIN, 0:PAD], uc[:, w0:NWIN - 1, GRID:GRID + PAD])
                own.link(nc.vector.tensor_copy(uc[:, w0:NWIN - 1, PAD + GRID:WIN],
                                               uc[:, w0 + 1:NWIN, PAD:2 * PAD]))
                dve.sem_inc(u_done, 1)
            assert own.n == base + n0
            own.n, own.at = base + n0 * NP_, 0
            base = own.n
            with dve.Fori(0, NP_) as j:
                own.at = j * KW
                uc = u[:, ds(j, 1), :].rearrange("p a (w x) -> p (a w) x", x=WIN)
                out = cv[:, ds(j, 1), :].rearrange("p a (w x) -> p (a w) x", x=GRID)
                nc.vector.tensor_copy(s.st[:, 6:7], V["db"][:, ds(j, 1)]).then_inc(conv_own, 1)
                taps = s.taps
                nc.vector.tensor_copy(taps[:, :], V["dw"][:, ds(j * KW, KW)]).then_inc(conv_own, 1)
                dve.wait_ge(conv_own, j * 2 + 2)
                for k in range(KW):
                    src = uc[:, :, k:k + GRID]
                    if k == 0:
                        ins = nc.vector.tensor_scalar(out, src, taps[:, 0:1], s.st[:, 6:7],
                                                      ALU.mult, ALU.add)
                    else:
                        ins = nc.vector.scalar_tensor_tensor(out=out, in0=src, scalar=taps[:, k:k + 1],
                                                             in1=out, op0=ALU.mult, op1=ALU.add)
                    own.link(ins)
                dve.sem_inc(conv_done, 1)
            own.n, own.at = base + NP_ * KW, 0
            for n in range(4 * NP_):
                dve.wait_ge(k_ps, n + 1)
                nc.vector.tensor_scalar(kn[:, n // 4, n % 4 * KT:(n % 4 + 1) * KT], knps[n % 2], 1e-24, None,
                                        ALU.max).then_inc(k_max, 1)
            for k in range(NP_):
                dve.wait_ge(k_root, k + 1)
                own.link(nc.vector.reciprocal(kn[:, k, :], kn[:, k, :]))
            dve.wait_ge(pr_done, NPC)
            for k in range(NP_):
                nc.vector.scalar_tensor_tensor(out=s.kk[:, k, :], in0=s.kT[:, k, :],
                                               scalar=V["k_k"][:, k:k + 1], in1=kn[:, k, :],
                                               op0=ALU.mult, op1=ALU.mult).then_inc(kk_done, 1)
            dve.wait_ge(mean_ps, 1)
            for k in range(NP_):
                nc.vector.tensor_tensor(cv[:, k, :], cv[:, k, :], PS[:, 0:T], ALU.subtract)\
                    .then_inc(cen, 1)
            dve.wait_ge(var_ps, 1)
            nc.vector.tensor_scalar(lrs, PS[:, 3 * 512:3 * 512 + T], LN_EPS, None, ALU.add)\
                .then_inc(var_done, 1)
            dve.wait_ge(lrs_done, 1)
            own.link(nc.vector.reciprocal(lrs, lrs))
            for k in range(NP_):
                nc.vector.tensor_tensor(cv[:, k, :], cv[:, k, :], lrs, ALU.mult).then_inc(scaled, 1)
            for k in range(NP_):
                dve.wait_ge(sil_sig, k + 1)
                nc.vector.tensor_tensor(cv[:, k, :], cv[:, k, :], sq[:, k, :], ALU.mult).then_inc(cout, 1)
            dve.wait_ge(late_used, 8)
            own.link(mod_out(16, 32))
            dve.sem_inc(g1_ready, 1)
            own.link(one_plus_times(s.A2, s.modT[:, 32:40, :], V["n2"]))


def looped(eng, own, lo, hi, links, body):
    base = own.n
    with eng.Fori(lo, hi) as i:
        own.at = i * links + (-lo * links)
        body(i)
    assert own.n == base + links, (own.n - base, links)
    own.n, own.at = base + (hi - lo) * links, 0


def phase_wkv(nc, s):
    a, K, V, PS, M, sem = s.a, s.K, s.V, s.PS, s.M, s.sem
    ar = Arena(M, s.n_main, s.mark)
    PC = NP_ * C
    two = (0, 1)

    def pair_of(*shape):
        return [ar.get(*shape) for _ in two]

    wa = pair_of(2, NP_, C)
    cum = pair_of(2, NP_, C)
    inv = pair_of(NP_, C)
    kd = pair_of(NP_, C)
    ba = pair_of(NP_, C)
    bet = pair_of(NP_, C)
    assert ar.at == s.mark + 4096
    kk = ar.get(NP_, T)
    kr = pair_of(NP_, 2 * C)
    key = pair_of(NP_, C)
    at_bd = ar.at
    bds = {n: pair_of(NP_, P) for n in ("AT", "M", "P", "Q", "Z", "NT", "NI", "keyt", "bett",
                                        "kap", "rho", "bet", "key", "val")}
    N, Z = pair_of(NP_, C), pair_of(NP_, C)
    praw = pair_of(NP_, C)
    wc = [ar.get(NP_) for _ in two]
    Vt, X, U, S = pair_of(NP_, HS), pair_of(NP_, HS), pair_of(NP_, HS), pair_of(NP_, HS)
    Yo = X
    S_next = ar.get(NP_, HS)
    S_keep = ar.get(NP_, HS)
    fin = bds["P"][0]
    st_rows = M[0:HS, at_bd:at_bd + 2 * NH * HS].rearrange("p (d n) -> p d n", d=2)
    GT, at_g = 4 * C, at_bd + 4 * NP_ * P
    NTURN = T // GT
    gates = [M[:, at_g + d * 8 * GT:at_g + (d + 1) * 8 * GT].rearrange("p (c a t) -> p c a t", a=8, t=C)
             for d in two]
    BA, BB, BC, BD = [[PS[:, (4 * d + b) * 512:(4 * d + b + 1) * 512] for d in two] for b in range(4)]

    def both(name):
        return [sem(f"{name}{d}") for d in two]

    dvo = sem("dve_own_b")
    zeroed, turns = sem("bd_zeroed"), sem("pool_turns")
    st_loaded, st_ps, st_set = sem("state_loaded"), sem("state_transposed"), sem("state_set")
    lo_ps, lo_free = sem("lora_psum"), both("lora_bank_free")
    g_ready, g_free, g_out, wa_in = both("gates_ready"), both("gates_free"), both("gates_out"), both("gates_in")
    at_r, praw_r = both("at_ready"), both("p_raw")
    inv_e = both("inv_ready")
    cr, er, kdr = both("sums_ready"), both("exps_ready"), both("kd_ready")
    krr, bkr = both("kap_rho_ready"), both("bet_key_ready")
    vbd, kbd, rbd, bbd, kyb = (both("v_bd_ready"), both("kap_bd_ready"), both("rho_bd_ready"),
                               both("bet_bd_ready"), both("key_bd_ready"))
    v_ps, g1_ps, g2_ps, kt_ps, bt_ps = (both("v_psum"), both("gram_bet_psum"), both("gram_key_psum"),
                                        both("keyt_psum"), both("bett_psum"))
    p_r, kt_r, bt_r = both("p_ready"), both("keyt_ready"), both("bett_ready")
    inv_r, mpq = both("inverse_started"), both("masked_grams")
    y_ps, z_r, n_ps, n_r = both("level_y_psum"), both("level_z"), both("level_n_psum"), both("level_n")
    x_ps, x_r, u_ps, u_r = both("x_psum"), both("x_ready"), both("u_psum"), both("u_ready")
    o_r, o_sp = both("y_ready"), both("y_written")
    kd_sp, o_free, kd_free = both("kd_written"), both("y_buffer_free"), both("kd_buffer_free")
    done, st_r = both("round_psum_done"), both("state_ready")
    out_ps, out_r, out_w = sem("final_psum"), sem("final_ready"), sem("final_written")

    def cols(i, d, n=C):
        return ds(i * C, n) if d == 0 else ds(i * (-C) + (NCH - 1) * C, n)

    def q4(ap):
        return ap.rearrange("p (a b) -> p a b", a=NP_)

    def bd4(ap):
        return ap.rearrange("p a (h t) -> p a h t", h=2)

    def over_h(ap):
        return ap.unsqueeze(2).to_broadcast([P, NP_, 2, C])

    def mask_bd(m):
        return m.rearrange("p (h t) -> p h t", h=2).unsqueeze(1).to_broadcast([P, NP_, 2, C])

    def mask_c(m):
        return m.unsqueeze(1).to_broadcast([P, NP_, C])

    with nc.Block() as block:

        @block.sync
        def _(sp):
            for d in two:
                sp.dma_start(st_rows[:, d, :].rearrange("v (h k) -> v h k", h=NH),
                             a["state"][d].rearrange("h v k -> v h k")).then_inc(st_loaded, 16)
                sp.sem_inc(o_free[d], 1)
                sp.sem_inc(kd_free[d], 1)

            def gates_in(i):
                for d in two:
                    chunk = i if d == 0 else i * (-1) + (NCH - 1)
                    sp.dma_start(wa[d].rearrange("p q a t -> p (q a t)"),
                                 s.gates_d[d][ds(chunk, 1)].rearrange("a p n -> (a p) n"))\
                        .then_inc(wa_in[d], 16)

            def keys_out(i, ahead=True):
                for d in two:
                    sp.wait_ge(kdr[d], i + 1)
                if ahead:
                    gates_in(i + 1)
                for d in two:
                    sp.dma_start(s.kd_d[d][:, :, cols(i, d)], kd[d]).then_inc(kd_sp[d], 16)
                for d in two:
                    sp.wait_ge(kd_sp[d], i * 16 + 16)
                    sp.sem_inc(kd_free[d], 1)

            def y_out(i):
                for d in two:
                    chunk = i if d == 0 else i * (-1) + (NCH - 1)
                    sp.wait_ge(o_r[d], i + 1)
                    sp.dma_start(s.y_d[d][ds(chunk, 1)].rearrange("a p n -> (a p) n"),
                                 Yo[d].rearrange("p a b -> p (a b)")).then_inc(o_sp[d], 16)
                for d in two:
                    sp.wait_ge(o_sp[d], i * 16 + 16)
                    sp.sem_inc(o_free[d], 1)

            for d in two:
                sp.sem_inc(g_free[d], 1)

            def gates_to_dram(t):
                for d in two:
                    chunks = ds(t * 4, 4) if d == 0 else ds(t * (-4) + (NCH - 4), 4)
                    sp.wait_ge(g_ready[d], t * 2 + 2)
                    sp.dma_start(s.gates_d[d][chunks].rearrange("c p n -> p c n"),
                                 gates[d].rearrange("p c a t -> p c (a t)")).then_inc(g_out[d], 16)
                for d in two:
                    sp.wait_ge(g_out[d], t * 16 + 16)
                    sp.sem_inc(g_free[d], 1)

            gates_to_dram(0)
            gates_in(0)
            with sp.Fori(1, NTURN) as t:
                gates_to_dram(t)
            keys_out(0)
            with sp.Fori(0, NCH - 2) as i:
                keys_out(i + 1)
                y_out(i)
            keys_out(NCH - 1, False)
            y_out(NCH - 2)
            y_out(NCH - 1)
            sp.wait_ge(out_r, 1)
            for d in two:
                for q in range(2):
                    for j in range(2):
                        h0 = 2 * (2 * q + j)
                        src = fin[j * HS:(j + 1) * HS, d * 2 + q, :].rearrange("v (h k) -> v h k", h=2)
                        sp.dma_start(a["out_state"][d, h0:h0 + 2].rearrange("h v k -> v h k"), src)\
                            .then_inc(out_w, 16)
            sp.wait_ge(out_w, 16 * 8)

        @block.gpsimd
        def _(pool):
            for n in ("kap", "rho", "bet", "key", "val"):
                for d in two:
                    last = nc.gpsimd.memset(bds[n][d], 0.0)
            last.then_inc(zeroed, 1)
            pool.wait_ge(zeroed, 1)

            def spread(dst, src):
                nc.gpsimd.tensor_copy(dst[0:HS, :, 0:C], src[0:HS])
                return nc.gpsimd.tensor_copy(dst[HS:P, :, C:P], src[HS:P])

            with pool.Fori(0, NCH) as i:
                for d in two:
                    hold(pool, turns, (v_ps[d], i + 1))
                    spread(bds["val"][d], s.vT[:, :, cols(i, d)]).then_inc(vbd[d], 1)
                for d in two:
                    hold(pool, turns, (bkr[d], i + 1), (kt_ps[d], i + 1))
                    spread(bds["key"][d], key[d]).then_inc(kyb[d], 1)
                for d in two:
                    hold(pool, turns, (done[d], i + 1))
                    spread(bds["rho"][d], kr[d][:, :, C:2 * C]).then_inc(rbd[d], 1)

        @block.tensor
        def _(pe):
            for d in two:
                pe.sem_inc(done[d], 1)
                pe.sem_inc(v_ps[d], 1)
                pe.sem_inc(kt_ps[d], 1)
            pe.wait_ge(st_loaded, 32)
            for d in two:
                for p in range(NP_):
                    last = nc.tensor.transpose(BA[0][:, (d * NP_ + p) * HS:(d * NP_ + p + 1) * HS],
                                               st_rows[:, d, p * P:(p + 1) * P], K["ident"][0:HS, 0:HS])
            last.then_inc(st_ps, 1)
            for q in two:
                pe.sem_inc(lo_free[q], 1)
            with pe.Fori(0, NTURN) as t:
                for d in two:
                    tokens = ds(t * GT, GT) if d == 0 else ds(t * (-GT) + (T - GT), GT)
                    for q in two:
                        pe.wait_ge(lo_free[q], t * 2 + (d + 1))
                        for p in range(NP_):
                            last = nc.tensor.matmul((BC, BD)[q][p // 2][:, p % 2 * GT:(p % 2 + 1) * GT],
                                                    s.lora_up[:, 2 * q + d, p * P:(p + 1) * P],
                                                    s.loraT[:, q, tokens], start=True, stop=True)
                        last.then_inc(lo_ps, 1)
            for q in two:
                pe.wait_ge(lo_free[q], 2 * NTURN + 1)
            pe.wait_ge(st_set, 1)

            def each(out, lhsT, rhs, w, acc=None):
                for p in range(NP_):
                    terms = [(lhsT, rhs)] + (acc or [])
                    for n, (l, r) in enumerate(terms):
                        last = nc.tensor.matmul(out[:, p * w:(p + 1) * w], l[:, p, :], r[:, p, :],
                                                start=(n == 0), stop=(n == len(terms) - 1))
                return last

            def rows(d, name, done_sem):
                for p in range(NP_):
                    last = nc.tensor.transpose(BA[d][:, p * P:(p + 1) * P], bds[name][d][:, p, :],
                                               K["ident"])
                last.then_inc(done_sem[d], 1)

            def solve(i):
                for d in two:
                    pe.wait_ge(n_r[d], i * 5 + 5)
                    pe.wait_ge(x_r[d], i + 1)
                    each(BC[d], bds["NI"][d], X[d], HS).then_inc(u_ps[d], 1)

            def results(i):
                for d in two:
                    b = {n: v[d] for n, v in bds.items()}
                    pe.wait_ge(kt_r[d], i + 1)
                    pe.wait_ge(u_r[d], i + 1)
                    pe.wait_ge(rbd[d], i + 1)
                    pe.wait_ge(p_r[d], i + 1)
                    each(BA[d], b["rho"], S[d], HS, [(b["P"], U[d]), (b["Q"], Vt[d])])
                    each(BA[d][:, 256:512], b["keyt"], Vt[d], HS, [(b["bett"], U[d])]).then_inc(done[d], 1)

            def body(i, prev=True, ahead=True):
                for d in two:
                    pe.wait_ge(bbd[d], i + 1)
                    pe.wait_ge(krr[d], i + 1)
                    each(BB[d], bds["bet"][d], kr[d], 2 * C).then_inc(g1_ps[d], 1)
                if prev:
                    solve(i - 1)
                    results(i - 1)
                for lv in range(len(LEVELS)):
                    for d in two:
                        b = {n: v[d] for n, v in bds.items()}
                        if lv == 0:
                            pe.wait_ge(inv_r[d], i + 1)
                            pe.wait_ge(praw_r[d], i + 1)
                        else:
                            pe.wait_ge(n_r[d], i * 5 + lv)
                        each(BB[d], b["AT"], N[d], C).then_inc(y_ps[d], 1)
                    if lv == 4:
                        for d in two:
                            pe.wait_ge(mpq[d], i + 1)
                            rows(d, "key", kt_ps)
                        for d in two:
                            b = {n: v[d] for n, v in bds.items()}
                            pe.wait_ge(kbd[d], i + 1)
                            if prev:
                                pe.wait_ge(st_r[d], i)
                            each(BC[d], b["kap"], S[d], HS, [(b["M"], Vt[d])]).then_inc(x_ps[d], 1)
                    for d in two:
                        b = {n: v[d] for n, v in bds.items()}
                        if lv == 0 and prev:
                            pe.wait_ge(u_r[d], i)
                        if lv == 0:
                            pe.wait_ge(vbd[d], i + 1)
                            for p in range(NP_):
                                last = nc.tensor.matmul(BC[d][:, 256 + p * HS:256 + (p + 1) * HS],
                                                        b["val"][:, p, :], K["fold"], start=True, stop=True)
                            last.then_inc(v_ps[d], 1)
                        pe.wait_ge(z_r[d], i * 5 + (lv + 1))
                        if lv < len(LEVELS) - 1:
                            each(BC[d], b["NT"], Z[d], C)
                        each(BD[d], b["Z"], b["NT"], P).then_inc(n_ps[d], 1)
                    if lv == 1:
                        for d in two:
                            if prev:
                                pe.wait_ge(o_r[d], i)
                                pe.wait_ge(st_r[d], i)
                            rows(d, "bet", bt_ps)
                    if lv == 2:
                        for d in two:
                            pe.wait_ge(bt_r[d], i + 1)
                            pe.wait_ge(kyb[d], i + 1)
                            each(BA[d], bds["key"][d], kr[d], 2 * C).then_inc(g2_ps[d], 1)

            body(0, prev=False)
            with pe.Fori(1, NCH - 1) as i:
                body(i)
            body(NCH - 1, ahead=False)
            solve(NCH - 1)
            results(NCH - 1)
            for d in two:
                pe.wait_ge(st_r[d], NCH)
                pe.wait_ge(o_r[d], NCH)
            for d, src in enumerate((S[0], S_keep)):
                for q in range(2):
                    last = nc.tensor.transpose(BA[0][:, (d * 2 + q) * P:(d * 2 + q + 1) * P],
                                               src[:, 2 * q:2 * q + 2, :].rearrange("p a b -> p (a b)"),
                                               K["ident"])
            last.then_inc(out_ps, 1)

        @block.scalar
        def _(act):
            def spread(dst, src):
                nc.scalar.activation(dst[0:HS, :, 0:C], src[0:HS], ACT.Copy)
                return nc.scalar.activation(dst[HS:P, :, C:P], src[HS:P], ACT.Copy)

            act.wait_ge(zeroed, 1)

            def exps(i):
                for d in two:
                    act.wait_ge(cr[d], i + 1)
                    nc.scalar.activation(inv[d], cum[d][:, 1], ACT.Exp, scale=C0).then_inc(inv_e[d], 1)
                for d in two:
                    act.wait_ge(inv_e[d], i + 1)
                    nc.scalar.activation(cum[d], cum[d], ACT.Exp, scale=-C0).then_inc(er[d], 1)

            def spread_bet(i):
                for d in two:
                    act.wait_ge(bkr[d], i + 1)
                    spread(bds["bet"][d], bet[d]).then_inc(bbd[d], 1)

            def spread_kap(i):
                for d in two:
                    act.wait_ge(krr[d], i + 1)
                    spread(bds["kap"][d], kr[d][:, :, 0:C]).then_inc(kbd[d], 1)

            def take_u(i):
                for d in two:
                    act.wait_ge(u_ps[d], i + 1)
                    nc.scalar.activation(U[d], q4(BC[d][:, 0:PC]), ACT.Copy, scale=-1.0).then_inc(u_r[d], 1)

            def take_y(i):
                for d in two:
                    act.wait_ge(done[d], i + 2)
                    nc.scalar.activation(Yo[d], q4(BA[d][:, 0:PC]), ACT.Copy).then_inc(o_r[d], 1)

            def body(i, prev=True, ahead=True):
                if prev:
                    take_u(i - 1)
                for d in two:
                    act.wait_ge(at_r[d], i + 1)
                    nc.scalar.activation(praw[d], q4(BB[d])[:, :, C:2 * C], ACT.Copy).then_inc(praw_r[d], 1)
                if prev:
                    take_y(i - 1)
                for lv in range(len(LEVELS)):
                    if lv == 2:
                        for d in two:
                            act.wait_ge(bt_ps[d], i + 1)
                            nc.scalar.activation(bds["bett"][d], q4(BA[d]), ACT.Copy).then_inc(bt_r[d], 1)
                    if lv == 4:
                        for d in two:
                            act.wait_ge(kt_ps[d], i + 2)
                            nc.scalar.activation(bds["keyt"][d], q4(BA[d]), ACT.Copy).then_inc(kt_r[d], 1)
                        for d in two:
                            act.wait_ge(x_ps[d], i + 1)
                            act.wait_ge(o_free[d], i + 1)
                            nc.scalar.activation(X[d], q4(BC[d][:, 0:PC]), ACT.Copy).then_inc(x_r[d], 1)
                        if ahead:
                            spread_bet(i + 1)
                            spread_kap(i + 1)
                    for d in two:
                        act.wait_ge(n_ps[d], i * 5 + (lv + 1))
                        if lv < len(LEVELS) - 1:
                            nc.scalar.activation(N[d], q4(BC[d][:, 0:PC]), ACT.Copy)
                        if lv == 0:
                            nc.scalar.activation(Vt[d], q4(BC[d][:, PC:2 * PC]), ACT.Copy)
                        nc.scalar.activation(bds["NT" if lv < len(LEVELS) - 1 else "NI"][d], q4(BD[d]),
                                             ACT.Copy).then_inc(n_r[d], 1)
                    if lv == 2 and ahead:
                        exps(i + 1)

            def sigmoids(t):
                for d in two:
                    act.wait_ge(g_free[d], t + 1)
                    for q in two:
                        act.wait_ge(lo_ps, t * 4 + (2 * d + q + 1))
                        for p in range(NP_):
                            src = (BC, BD)[q][p // 2][:, p % 2 * GT:(p % 2 + 1) * GT]
                            a_ = q * NP_ + p
                            last = nc.scalar.activation(gates[d][:, :, a_, :],
                                                        src.rearrange("p (c t) -> p c t", t=C), ACT.Sigmoid,
                                                        bias=V["bias_wa"][:, 8 * d + a_:8 * d + a_ + 1])
                        last.then_inc(g_ready[d], 1)
                        act.wait_ge(g_ready[d], t * 2 + (q + 1))
                        act.sem_inc(lo_free[q], 1)

            with act.Fori(0, 2) as t:
                sigmoids(t)
            exps(0)
            with act.Fori(2, NTURN) as t:
                sigmoids(t)
            spread_bet(0)
            spread_kap(0)
            body(0, prev=False)
            with act.Fori(1, NCH - 1) as i:
                body(i)
            body(NCH - 1, ahead=False)
            take_u(NCH - 1)
            take_y(NCH - 1)
            act.wait_ge(out_ps, 1)
            nc.scalar.activation(fin, BA[0].rearrange("p (a b) -> p a b", b=P), ACT.Copy).then_inc(out_r, 1)

        @block.vector
        def _(dve):
            own = Chain(dve, dvo)
            dve.wait_ge(st_ps, 1)
            st = BA[0].rearrange("p (d a b) -> p d a b", d=2, a=NP_)
            nc.vector.memset(S[1], 0.0)
            nc.vector.tensor_copy(S[0], st[:, 0])
            own.link(nc.vector.tensor_copy(S_next, st[:, 1]))
            dve.sem_inc(st_set, 1)

            def sums(i):
                for d in two:
                    dve.wait_ge(wa_in[d], i * 16 + 16)
                    sg = wa[d][:, 0]
                    first = cum[d][:, 1] if d == 0 else ba[d]
                    own.link(nc.vector.tensor_tensor_scan(first.rearrange("p a t -> p (a t)"), K["reset"],
                                                          sg.rearrange("p a t -> p (a t)"), 0.0,
                                                          ALU.mult, ALU.add))
                    if d == 0:
                        nc.vector.tensor_tensor(cum[d][:, 0], cum[d][:, 1], sg, ALU.subtract)\
                            .then_inc(cr[d], 1)
                    else:
                        total = first[:, :, C - 1:C].to_broadcast([P, NP_, C])
                        own.link(nc.vector.tensor_tensor(cum[d][:, 0], total, first, ALU.subtract))
                        nc.vector.tensor_tensor(cum[d][:, 1], cum[d][:, 0], sg, ALU.add).then_inc(cr[d], 1)

            def keys(i):
                k_a = V["k_a"].unsqueeze(2).to_broadcast([P, NP_, C])
                for d in two:
                    ga = wa[d][:, 1]
                    own.link(nc.vector.tensor_tensor(ba[d], kk[:, :, cols(i, d)], ga, ALU.mult))
                    dve.wait_ge(kd_free[d], i + 1)
                    own.link(nc.vector.scalar_tensor_tensor(out=kd[d], in0=ga, scalar=1.0, in1=k_a,
                                                            op0=ALU.subtract, op1=ALU.mult))
                    nc.vector.scalar_tensor_tensor(out=kd[d], in0=kd[d], scalar=1.0,
                                                   in1=s.kT[:, :, cols(i, d)], op0=ALU.add, op1=ALU.mult)\
                        .then_inc(kdr[d], 1)

            def decayed(i, first=False):
                for d in two:
                    if not first:
                        dve.wait_ge(rbd[d], i)
                        dve.wait_ge(g2_ps[d], i)
                    dve.wait_ge(er[d], i + 1)
                    nc.vector.tensor_tensor(kr[d][:, :, 0:C], cum[d][:, 0], kk[:, :, cols(i, d)], ALU.mult)
                    nc.vector.tensor_tensor(kr[d][:, :, C:2 * C], cum[d][:, 1], s.rT[:, :, cols(i, d)],
                                            ALU.mult).then_inc(krr[d], 1)
                    nc.vector.tensor_tensor(bet[d], inv[d], ba[d], ALU.mult)
                    dve.wait_ge(kdr[d], i + 1)
                    nc.vector.tensor_tensor(key[d], inv[d], kd[d], ALU.mult).then_inc(bkr[d], 1)

            def keep_decay(i, prev=True):
                for d in two:
                    end = C - 1 if d == 0 else 0
                    if prev:
                        dve.wait_ge(st_r[d], i)
                    last = nc.vector.tensor_copy(wc[d], cum[d][:, 1, :, end])
                own.link(last)

            def state(i, switch=None):
                for d in two:
                    dve.wait_ge(done[d], i + 2)
                    dve.wait_ge(o_r[d], i + 1)
                    if switch == "prompt" and d == 0:
                        nc.vector.memset(S[0], 0.0).then_inc(st_r[0], 1)
                        continue
                    own.link(nc.vector.tensor_tensor(S[d], S[d], q4(BA[d][:, 256:512]), ALU.add))
                    out = nc.vector.tensor_tensor(S[d], S[d], wc[d].unsqueeze(2).to_broadcast([P, NP_, HS]),
                                                  ALU.mult)
                    if switch == "sample" and d == 1:
                        own.link(out)
                        own.link(nc.vector.tensor_copy(S_keep, S[1]))
                        out = nc.vector.tensor_copy(S[1], S_next)
                    out.then_inc(st_r[d], 1)

            def body(i, prev=True, ahead=True, switch=None):
                for d in two:
                    b = {n: v[d] for n, v in bds.items()}
                    dve.wait_ge(g1_ps[d], i + 1)
                    nc.vector.tensor_tensor(Z[d], q4(BB[d])[:, :, 0:C], mask_c(K[f"firstc{d}"]), ALU.mult)
                    own.link(nc.vector.tensor_tensor(bd4(b["AT"]), over_h(q4(BB[d])[:, :, 0:C]),
                                                     mask_bd(K[f"strict{d}"]), ALU.mult))
                    nc.vector.tensor_tensor(b["AT"], b["AT"],
                                            K["ident"].unsqueeze(1).to_broadcast([P, NP_, P]), ALU.add)\
                        .then_inc(at_r[d], 1)
                    dve.wait_ge(at_r[d], i + 1)
                    nc.vector.tensor_tensor(b["NT"], b["AT"],
                                            K[f"first{d}"].unsqueeze(1).to_broadcast([P, NP_, P]), ALU.mult)
                    own.link(nc.vector.tensor_tensor(Z[d], Z[d], mask_c(K["fold"]), ALU.add))
                    nc.vector.transpose(N[d].rearrange("p a t -> p (a t)"),
                                        Z[d].rearrange("p a t -> p (a t)")).then_inc(inv_r[d], 1)
                for lv, size in enumerate(LEVELS):
                    for d in two:
                        dve.wait_ge(y_ps[d], i * 5 + (lv + 1))
                        y = q4(BB[d][:, 0:PC])
                        if lv < len(LEVELS) - 1:
                            nc.vector.tensor_tensor(Z[d], y, mask_c(K[f"levc{d}_{size}"]), ALU.mult)
                        nc.vector.tensor_tensor(bd4(bds["Z"][d]), over_h(y), mask_bd(K[f"lev{d}_{size}"]),
                                                ALU.mult).then_inc(z_r[d], 1)
                    if lv == 0:
                        if prev:
                            state(i - 1, switch)
                        keep_decay(i, prev)
                    if lv == 1 and ahead:
                        sums(i + 1)
                    if lv == 2:
                        for d in two:
                            nc.vector.tensor_tensor(bd4(bds["P"][d]), over_h(praw[d]),
                                                    mask_bd(K[f"incl{d}"]), ALU.mult).then_inc(p_r[d], 1)
                        if ahead:
                            keys(i + 1)
                    if lv == 3:
                        for d in two:
                            b, g2 = {n: v[d] for n, v in bds.items()}, q4(BA[d])
                            dve.wait_ge(g2_ps[d], i + 1)
                            nc.vector.tensor_tensor(bd4(b["M"]), over_h(g2[:, :, 0:C]),
                                                    mask_bd(K[f"strict{d}"]), ALU.mult)
                            nc.vector.tensor_tensor(bd4(b["Q"]), over_h(g2[:, :, C:2 * C]),
                                                    mask_bd(K[f"incl{d}"]), ALU.mult).then_inc(mpq[d], 1)
                        if ahead:
                            decayed(i + 1)

            LINKS = 14
            sums(0)
            keys(0)
            decayed(0, True)
            for d in two:
                dve.wait_ge(g_free[d], NTURN + 1)
            body(0, prev=False)
            looped(dve, own, 1, NCP, LINKS, body)
            body(NCP, switch="sample")
            looped(dve, own, NCP + 1, NCS, LINKS, body)
            body(NCS, switch="prompt")
            looped(dve, own, NCS + 1, NCH - 1, LINKS, body)
            body(NCH - 1, ahead=False)
            state(NCH - 1)
def phase_mix(nc, s):
    a, K, V, PS, M, sem = s.a, s.K, s.V, s.PS, s.M, s.sem
    ar = Arena(M, s.n_main, s.mark)
    NG = NCH * NP_
    ybd = [ar.get(NP_, P) for _ in (0, 1)]
    at_y0 = ar.at
    y0 = ar.get(NG, HS)
    at_k0 = ar.at
    kd0 = ar.get(NP_, T)
    at_y1 = ar.at
    y1 = ar.get(NG, HS)
    kd1 = ar.get(NP_, T)
    cvT = ar.get(NP_, T)
    xgT, g_up = ar.get(T), ar.get(CW)
    gs = ar.get(3, NG)
    ynT = s.kT
    bon = s.rT
    w_o = M[:, at_y1:at_y1 + KC * D].rearrange("p (k n) -> p k n", n=D)
    t0 = at_y1 + KC * D
    assert t0 >= RING
    TB = 64
    aff = M[0:TB, t0:t0 + TS]
    vals = M[0:TB, t0 + TS:t0 + TS + P]
    idx = M[0:TB, t0 + TS + P:t0 + TS + 2 * P].bitcast(U32)
    idxf = M[0:TB, t0 + TS + 2 * P:t0 + TS + 3 * P]
    aft = [M[:, t0 + TS + (3 + i) * P:t0 + TS + (4 + i) * P] for i in (0, 1)]
    g1b = M[:, at_y0:at_y0 + 2 * D].rearrange("p (j n) -> p j n", n=D)
    xt = [M[:, at_y0 + (2 + i) * D:at_y0 + (3 + i) * D] for i in (0, 1)]
    junk = [M[:, at_y0 + 4 * D:at_y0 + 5 * D], M[:, at_k0 + 4 * D:at_k0 + 5 * D]]
    x2 = [M[:, at_k0 + i * D:at_k0 + (i + 1) * D] for i in (0, 1)]
    xn = [M[:, at_k0 + (2 + i) * D:at_k0 + (3 + i) * D] for i in (0, 1)]
    h2 = [s.rkv[:, 0:4, :].rearrange("p a b -> p (a b)")[:, i * D:(i + 1) * D]
          .rearrange("p (k t) -> p k t", t=P) for i in (0, 1)]
    rt = s.vT.rearrange("p a b -> p (a b)")[:, 0:KC * E].rearrange("p (k e) -> p k e", e=E)
    ex = [s.vT[:, 1, i * E:(i + 1) * E] for i in (0, 1)]
    mixps = [PS[:, 0:D], PS[:, D:2 * D]]
    trp = PS[:, 4 * 512:4 * 512 + D]
    lg, afp = PS[:, 6 * 512:6 * 512 + E], PS[:, 7 * 512:7 * 512 + P]
    ssq = [s.st[:, i:i + 1] for i in (0, 1)]
    ms = [s.st[:, i:i + 1] for i in (2, 3)]
    root = [s.st[:, i:i + 1] for i in (4, 5)]
    rstd = [s.st[:, i:i + 1] for i in (8, 9)]
    nmx = [s.st[:, i:i + 1] for i in (6, 7)]
    esum = [s.st[:, i:i + 1] for i in (10, 11)]
    tiles = [(p, c0, w) for p in range(NP_) for c0, w in COLS3]

    y_in, kd_in, c_in, wo_in, misc_in = (sem("y_in"), sem("kd_in"), sem("conv_in"), sem("w_out_in"),
                                         sem("gate1_router_in"))
    g_in = sem("gate_lora_in")
    gsq, gvar, groot, y1_free = sem("gn_squared"), sem("gn_var"), sem("gn_root"), sem("y1_free")
    yc_done, kd_free = sem("gn_centered"), sem("kd1_free")
    ybz, yb_r, yn_ps, yn_r = sem("ybd_zeroed"), sem("ybd_ready"), sem("yn_psum"), sem("yn_ready")
    bprod, bon_ps, rw_r = sem("bonus_product"), sem("bonus_gate_psum"), sem("rwkv_out_ready")
    x_in = [sem(f"x_again{i}") for i in (0, 1)]
    acc_w = [sem(f"residual_written{i}") for i in (0, 1)]
    xn_w = [sem(f"normed_written{i}") for i in (0, 1)]
    mx, x2_r, sq_r, ms_r, rt_r, xn_r = (sem("mix_psum"), sem("x2_ready"), sem("x2_squared"),
                                        sem("x2_mean_square"), sem("x2_root"), sem("x2_normed"))
    tr, h_a, h_d, lg_r, mx_r, ex_r, af_r, at_r, ac_r = (
        sem("x2_transposed"), sem("h2_by_act"), sem("h2_by_dve"), sem("logits"), sem("logit_max"),
        sem("exp_logits"), sem("affinity_rows"), sem("affinity_psum"), sem("affinity_ready"))
    az, dvo, tab, tabt = sem("affinity_zeroed"), sem("dve_own_c"), sem("lists_ready"), sem("lists_psum")

    with nc.Block() as block:

        @block.sync
        def _(sp):
            for d, dst in enumerate((y0, y1)):
                sp.dma_start(dst.rearrange("p (c a) b -> p c (a b)", a=NP_),
                             s.y_d[d].rearrange("c p n -> p c n")).then_inc(y_in, 16)
            for d, dst in enumerate((kd0, kd1)):
                sp.dma_start(dst, s.kd_d[d]).then_inc(kd_in, 16)
            sp.dma_start(cvT.rearrange("p a b -> p (a b)"), s.conv_d).then_inc(c_in, 16)
            sp.dma_start(xgT, s.xg_d).then_inc(g_in, 16)
            sp.dma_start(g_up, a["g_up"]).then_inc(g_in, 16)
            sp.wait_ge(y1_free, 1)
            sp.wait_ge(kd_free, 1)
            sp.dma_start(w_o, a["w_out"].rearrange("(k p) n -> p k n", p=P)).then_inc(wo_in, 16)
            sp.wait_ge(rw_r, len(tiles))
            for j in range(2):
                sp.dma_start(g1b[:, j, :], s.g1_d[j:j + 1, :].to_broadcast([P, D])).then_inc(misc_in, 16)
            sp.dma_start(rt, a["router"].rearrange("(k p) e -> p k e", p=P)).then_inc(misc_in, 16)
            for n in range(NT + 1):
                if n < NT:
                    if n >= 2:
                        sp.wait_ge(x2_r, n - 1)
                    sp.dma_start(xt[n % 2], a["x"][n * P:(n + 1) * P, :]).then_inc(x_in[n % 2], 16)
                if n >= 1:
                    m = n - 1
                    sp.wait_ge(x2_r, m + 1)
                    sp.dma_start(s.acc_d[m * P:(m + 1) * P, :], x2[m % 2]).then_inc(acc_w[m % 2], 16)
                    sp.wait_ge(xn_r, m + 1)
                    sp.dma_start(s.xn_d[m * P:(m + 1) * P, :], xn[m % 2]).then_inc(xn_w[m % 2], 16)
            for i in (0, 1):
                sp.wait_ge(acc_w[i], 16 * NT // 2)
                sp.wait_ge(xn_w[i], 16 * NT // 2)
            sp.wait_ge(lg_r, NT)
            sp.wait_ge(ex_r, NT)
            sp.wait_ge(af_r, NT)
            for n in range(SLOTS):
                load_step(sp, s, 0, n)

        @block.gpsimd
        def _(pool):
            for i in (0, 1):
                nc.gpsimd.memset(ybd[i], 0.0).then_inc(ybz, 1)
            pool.wait_ge(y1_free, 1)
            pool.wait_ge(kd_free, 1)
            for i in (0, 1):
                nc.gpsimd.memset(aft[i], 0.0).then_inc(az, 1)
            nc.gpsimd.memset(M[0:TB, t0:t0 + TS + 3 * P], -1.0).then_inc(az, 1)

        @block.tensor
        def _(pe):
            for sm in (yn_r,):
                pe.sem_inc(sm, 2)
            with pe.Fori(0, NCH // 2) as j:
                for i in (0, 1):
                    pe.wait_ge(yb_r, j * 2 + (i + 1))
                    pe.wait_ge(yn_r, j * 2 + (i + 1))
                    for p in range(NP_):
                        last = nc.tensor.matmul(PS[:, i * 512 + p * C:i * 512 + (p + 1) * C],
                                                ybd[i][:, p, :], K["fold"], start=True, stop=True)
                    last.then_inc(yn_ps, 1)
            pe.wait_ge(bprod, 1)
            pe.wait_ge(g_in, 32)
            for n, (p, c0, w) in enumerate(tiles):
                if n >= 2:
                    pe.wait_ge(rw_r, n - 1)
                nc.tensor.matmul(PS[:, (2 + n % 2) * 512:(2 + n % 2) * 512 + w], K["blockones"],
                                 kd0[:, p, c0:c0 + w], start=True, stop=True)
                nc.tensor.matmul(PS[:, (4 + n % 2) * 512:(4 + n % 2) * 512 + w],
                                 g_up[:, p * P:(p + 1) * P], xgT[:, c0:c0 + w],
                                 start=True, stop=True).then_inc(bon_ps, 1)
            pe.wait_ge(rw_r, len(tiles))
            pe.wait_ge(yn_r, NCH + 2)
            pe.wait_ge(wo_in, 16)
            pe.wait_ge(c_in, 16)
            pe.wait_ge(misc_in, 48)
            for n in range(NT + 3):
                if n < NT:
                    if n >= 2:
                        pe.wait_ge(x2_r, n - 1)
                    for half in (0, 1):
                        for k in range(KC):
                            src = cvT if k < NP_ else ynT
                            last = nc.tensor.matmul(mixps[n % 2][:, half * 512:(half + 1) * 512],
                                                    src[:, k % NP_, n * P:(n + 1) * P],
                                                    w_o[:, k, half * 512:(half + 1) * 512],
                                                    start=(k == 0), stop=(k == KC - 1))
                    last.then_inc(mx, 1)
                m = n - 1
                if 0 <= m < NT:
                    pe.wait_ge(xn_r, m + 1)
                    if m >= 1:
                        pe.wait_ge(h_a, m)
                        pe.wait_ge(h_d, m)
                    for k in range(KC):
                        last = nc.tensor.transpose(trp[:, k * P:(k + 1) * P],
                                                   xn[m % 2][:, k * P:(k + 1) * P], K["ident"])
                    last.then_inc(tr, 1)
                m = n - 2
                if 0 <= m < NT:
                    pe.wait_ge(h_a, m + 1)
                    pe.wait_ge(h_d, m + 1)
                    if m >= 1:
                        pe.wait_ge(ex_r, m)
                        pe.wait_ge(mx_r, m)
                    for k in range(KC):
                        last = nc.tensor.matmul(lg, h2[m % 2][:, k, :], rt[:, k, :],
                                                start=(k == 0), stop=(k == KC - 1))
                    last.then_inc(lg_r, 1)
                m = n - 3
                if 0 <= m < NT:
                    pe.wait_ge(af_r, m + 1)
                    if m >= 1:
                        pe.wait_ge(ac_r, m)
                    nc.tensor.transpose(afp, aft[m % 2], K["ident"]).then_inc(at_r, 1)
            pe.wait_ge(tab, 1)
            nc.tensor.transpose(PS[:, 0:TB], vals, K["ident"][0:TB, 0:TB])
            nc.tensor.transpose(PS[:, TB:2 * TB], idxf, K["ident"][0:TB, 0:TB]).then_inc(tabt, 1)

        @block.scalar
        def _(act):
            act.wait_ge(yc_done, 1)
            nc.scalar.activation(y1, y0, ACT.Square).then_inc(gsq, 1)
            act.wait_ge(gvar, 1)
            nc.scalar.activation(gs[:, 1, :], gs[:, 1, :], ACT.Sqrt).then_inc(groot, 1)
            with act.Fori(0, NCH // 2) as j:
                for i in (0, 1):
                    act.wait_ge(yn_ps, j * 2 + (i + 1))
                    for p in range(NP_):
                        last = nc.scalar.activation(ynT[:, p, ds(j * (2 * C) + i * C, C)],
                                                    PS[:, i * 512 + p * C:i * 512 + (p + 1) * C],
                                                    ACT.Identity, scale=V["gng"][:, p:p + 1],
                                                    bias=V["gnb"][:, p:p + 1])
                    last.then_inc(yn_r, 1)
            for n in range(NT + 2):
                if n < NT:
                    i = n % 2
                    act.wait_ge(x2_r, n + 1)
                    nc.scalar.activation(junk[i], x2[i], ACT.Square, accum_out=ssq[i]).then_inc(sq_r, 1)
                    act.wait_ge(ms_r, n + 1)
                    nc.scalar.activation(root[i], ms[i], ACT.Sqrt).then_inc(rt_r, 1)
                m = n - 1
                if 0 <= m < NT:
                    g = 0 if m < NTS else 1
                    act.wait_ge(tr, m + 1)
                    for k in range(4):
                        last = nc.scalar.activation(h2[m % 2][:, k, :], trp[:, k * P:(k + 1) * P],
                                                    ACT.Identity, scale=s.A2[:, k, g:g + 1],
                                                    bias=s.B2[:, k, g:g + 1])
                    last.then_inc(h_a, 1)
                m = n - 2
                if 0 <= m < NT:
                    act.wait_ge(mx_r, m + 1)
                    nc.scalar.activation(ex[m % 2], lg, ACT.Exp, bias=nmx[m % 2],
                                         accum_out=esum[m % 2]).then_inc(ex_r, 1)

        @block.vector
        def _(dve):
            own = Chain(dve, dvo)
            dve.wait_ge(y_in, 32)
            own.link(nc.vector.tensor_tensor(y0, y0, y1, ALU.add))
            own.link(nc.vector.tensor_reduce(gs[:, 0, :], y0, AX.X, ALU.add))
            own.link(nc.vector.tensor_scalar(gs[:, 0, :], gs[:, 0, :], 1.0 / HS, None, ALU.mult))
            nc.vector.tensor_tensor(y0, y0, gs[:, 0, :].unsqueeze(2).to_broadcast([P, NG, HS]),
                                    ALU.subtract).then_inc(yc_done, 1)
            dve.wait_ge(kd_in, 32)
            own.link(nc.vector.tensor_tensor(kd0, kd0, kd1, ALU.add))
            dve.sem_inc(kd_free, 1)
            for p in range(NP_):
                last = nc.vector.scalar_tensor_tensor(out=kd0[:, p, :], in0=s.rT[:, p, :],
                                                      scalar=V["r_k"][:, p:p + 1], in1=kd0[:, p, :],
                                                      op0=ALU.mult, op1=ALU.mult)
            last.then_inc(bprod, 1)
            dve.wait_ge(gsq, 1)
            own.link(nc.vector.tensor_reduce(gs[:, 1, :], y1, AX.X, ALU.add))
            dve.sem_inc(y1_free, 1)
            nc.vector.tensor_scalar(gs[:, 1, :], gs[:, 1, :], 1.0 / HS, GN_EPS, ALU.mult, ALU.add)\
                .then_inc(gvar, 1)
            dve.wait_ge(groot, 1)
            own.link(nc.vector.reciprocal(gs[:, 2, :], gs[:, 1, :]))
            dve.wait_ge(ybz, 2)
            with dve.Fori(0, NCH // 2) as j:
                for i in (0, 1):
                    dve.wait_ge(yn_r, j * 2 + (i + 1))
                    for h in (0, 1):
                        rows = slice(h * HS, (h + 1) * HS)
                        r = gs[rows, 2, ds(j * (2 * NP_) + i * NP_, NP_)].unsqueeze(2)\
                            .to_broadcast([HS, NP_, HS])
                        last = nc.vector.tensor_tensor(ybd[i][rows, :, h * HS:(h + 1) * HS],
                                                       y0[rows, ds(j * (2 * NP_) + i * NP_, NP_), :], r,
                                                       ALU.mult)
                    last.then_inc(yb_r, 1)
            dve.wait_ge(yn_r, NCH + 2)
            for n, (p, c0, w) in enumerate(tiles):
                dve.wait_ge(bon_ps, n + 1)
                c = slice(c0, c0 + w)
                own.link(nc.vector.tensor_tensor(bon[:, p, c], PS[:, (2 + n % 2) * 512:][:, 0:w],
                                                 s.vT[:, p, c], ALU.mult))
                own.link(nc.vector.tensor_tensor(ynT[:, p, c], ynT[:, p, c], bon[:, p, c], ALU.add))
                nc.vector.tensor_tensor(ynT[:, p, c], ynT[:, p, c], PS[:, (4 + n % 2) * 512:][:, 0:w],
                                        ALU.mult).then_inc(rw_r, 1)
            dve.wait_ge(misc_in, 48)
            dve.wait_ge(az, 3)
            for n in range(NT + 3):
                if n < NT:
                    i, g = n % 2, 0 if n < NTS else 1
                    dve.wait_ge(mx, n + 1)
                    dve.wait_ge(x_in[i], 16 * (n // 2 + 1))
                    if n >= 2:
                        dve.wait_ge(acc_w[i], 16 * (n // 2))
                        dve.wait_ge(xn_w[i], 16 * (n // 2))
                    own.link(nc.vector.tensor_tensor(x2[i], mixps[i], g1b[:, g, :], ALU.mult))
                    nc.vector.tensor_tensor(x2[i], x2[i], xt[i], ALU.add).then_inc(x2_r, 1)
                    dve.wait_ge(sq_r, n + 1)
                    nc.vector.tensor_scalar(ms[i], ssq[i], 1.0 / D, RMS_EPS, ALU.mult, ALU.add)\
                        .then_inc(ms_r, 1)
                    dve.wait_ge(rt_r, n + 1)
                    own.link(nc.vector.reciprocal(rstd[i], root[i]))
                    nc.vector.tensor_scalar(xn[i], x2[i], rstd[i], None, ALU.mult).then_inc(xn_r, 1)
                m = n - 1
                if 0 <= m < NT:
                    g = 0 if m < NTS else 1
                    dve.wait_ge(tr, m + 1)
                    for k in range(4, KC):
                        last = nc.vector.tensor_scalar(h2[m % 2][:, k, :], trp[:, k * P:(k + 1) * P],
                                                       s.A2[:, k, g:g + 1], s.B2[:, k, g:g + 1],
                                                       ALU.mult, ALU.add)
                    last.then_inc(h_d, 1)
                m = n - 2
                if 0 <= m < NT:
                    i, o = m % 2, 0 if m < NTS else PB
                    dve.wait_ge(lg_r, m + 1)
                    nc.vector.tensor_reduce(nmx[i], lg, AX.X, ALU.max, negate=True).then_inc(mx_r, 1)
                    dve.wait_ge(ex_r, m + 1)
                    own.link(nc.vector.reciprocal(esum[i], esum[i]))
                    nc.vector.tensor_scalar(aft[i][:, o:o + E], ex[i], esum[i], None, ALU.mult)\
                        .then_inc(af_r, 1)
                m = n - 3
                if 0 <= m < NT:
                    o, t = (0, m) if m < NTS else (PB, m - NTS)
                    dve.wait_ge(at_r, m + 1)
                    nc.vector.tensor_copy(aff[o:o + E, t * P:(t + 1) * P], afp[o:o + E, :]).then_inc(ac_r, 1)
            dve.wait_ge(ac_r, NT)
            for n in range(CAP_S // 8):
                v8 = vals[:, 8 * n:8 * n + 8]
                own.link(nc.vector.max(v8, aff))
                own.link(nc.vector.max_index(idx[:, 8 * n:8 * n + 8], v8, aff))
                own.link(nc.vector.match_replace(aff, v8, aff, -2.0))
            nc.vector.tensor_copy(idxf, idx).then_inc(tab, 1)
            dve.wait_ge(tabt, 1)
            own.link(nc.vector.tensor_copy(s.gateT, PS[:, 0:TB]))
            own.link(nc.vector.tensor_scalar(s.idxF[:, PB:TB], PS[:, TB + PB:2 * TB], float(TS), None,
                                             ALU.add))
            own.link(nc.vector.tensor_copy(s.idxF[:, 0:PB], PS[:, TB:TB + PB]))
            own.link(nc.vector.tensor_copy(s.idxT, s.idxF))



SC = max(STEP_CHUNKS)
PIECE = KC * P
RING = SLOTS * 3 * SC * PIECE
STEP_AT = tuple(sum(STEP_CHUNKS[:i]) for i in range(len(STEP_CHUNKS)))
NSTEP = len(STEP_CHUNKS)
STEP_OF = tuple(st for st in range(NSTEP) for _ in range(STEP_CHUNKS[st]))
SEQ = (("w1", 0), ("w3", 0)) + tuple((w, ch - (w == "w2")) for ch in range(1, NFC)
                                     for w in ("w1", "w3", "w2")) + (("w2", NFC - 1),)
NSEQ = len(SEQ)
AT_SEQ = {piece: i for i, piece in enumerate(SEQ)}
assert NSTEP % SLOTS == 0


def slot_views(s, slot, nch):
    v = [s.M[:, (slot * 3 + i) * SC * PIECE:(slot * 3 + i) * SC * PIECE + nch * PIECE] for i in range(3)]
    return (v[0].rearrange("p (k n) -> p k n", k=KC), v[1].rearrange("p (k n) -> p k n", k=KC),
            v[2].rearrange("p (c n) -> p c n", n=D))


def load_step(sp, s, e, step, w13_free=None, w2_free=None):
    slot, nch, f0 = step % SLOTS, STEP_CHUNKS[step], STEP_AT[step] * P
    v1, v3, v2 = slot_views(s, slot, nch)

    def of(w):
        return w[e] if isinstance(e, int) else w[ds(e, 1)].rearrange("a r n -> (a r) n")

    if w13_free:
        w13_free()
    for dst, name in ((v1, "w1"), (v3, "w3")):
        sp.dma_start(dst, of(s.a[name]).rearrange("(k p) n -> p k n", p=P)[:, :, f0:f0 + nch * P])\
            .then_inc(s.w13_in[slot], 16)
    if w2_free:
        w2_free()
    sp.dma_start(v2, of(s.a["w2"])[f0:f0 + nch * P, :].rearrange("(c p) n -> p c n", p=P))\
        .then_inc(s.w2_in[slot], 16)


def phase_experts(nc, s):
    a, K, PS, M, sem = s.a, s.K, s.PS, s.M, s.sem
    ar = Arena(M, s.n_main, RING)

    NB = 4
    xe = ar.get(KC, CAP)
    xn = ar.get(KC, CAP)
    xg, xgp = ar.get(D), ar.get(D, rows=CAP_P)
    yeT = ar.get(KC, CAP)
    ye, yep = ar.get(D), ar.get(D, rows=CAP_P)
    sg = [ar.get(CAP) for _ in range(NB)]
    hid = [ar.get(CAP) for _ in range(NB)]
    ig, igp, iw, iwp = (s.lora_up[0:r, 2, o:o + 1].bitcast(I32)
                        for r, o in ((P, 0), (CAP_P, 1), (P, 2), (CAP_P, 3)))
    gt, gtp = s.lora_up[:, 2, 4:5], s.lora_up[0:CAP_P, 2, 5:6]
    accps = [PS[:, (m // 3) * 512 + (m % 3) * CAP:(m // 3) * 512 + (m % 3 + 1) * CAP] for m in range(KC)]
    hps = [PS[:, (3 + b) * 512:(3 + b) * 512 + 2 * CAP] for b in range(NB)]
    swap = PS[:, 7 * 512:8 * 512]
    IN = ((40, range(0, 3)), (44, range(3, 6)), (48, range(6, KC)))
    OUT = (NSEQ + 3, NSEQ + 5, NSEQ + 7, NSEQ + 9)
    NIN, NOUT = len(IN), len(OUT)
    TURN = OUT[-1] + 1 - NSEQ

    ixg, gath, turns = sem("gather_index"), sem("gathered"), sem("pool_turns_e")
    used = sem("piece_used")
    swap_ps, swap_free = sem("swap_filled"), sem("swap_free")
    xn_a, xn_d, xe_a, xe_d = (sem("next_by_act"), sem("next_by_dve"), sem("inputs_by_act"),
                              sem("inputs_by_dve"))
    sg_r, h_r = sem("hidden_sigmoid"), sem("hidden_ready")
    y_a, y_d = sem("expert_out_by_act"), sem("expert_out_by_dve")
    gate_r, ye_a, ye_d = sem("gates_staged"), sem("rows_by_act"), sem("rows_by_dve")
    rows_free = sem("row_buffers_free")
    ixw, scat, dvo = sem("scatter_index"), sem("scattered"), sem("dve_own_d")

    def swaps_in(e):
        return e * (NIN + NOUT) + (NIN - (NIN + NOUT))

    def swaps_out(e):
        return e * (NIN + NOUT) + 2 * NIN

    SWAPS_LAST = E * NIN + (E - 1) * NOUT

    def piece(v):
        w, ch = SEQ[v]
        st = STEP_OF[ch]
        c = ch - STEP_AT[st]
        v1, v3, v2 = slot_views(s, st % SLOTS, STEP_CHUNKS[st])
        if w == "w2":
            return v2[:, c, :].rearrange("p (k n) -> p k n", n=P)
        return (v1 if w == "w1" else v3)[:, :, c * P:(c + 1) * P]

    def experts(eng_loop, step, tail):
        for v in range(TURN):
            step(0, v, first=True)
        eng_loop(lambda e: ([step(e, v) for v in range(TURN, NSEQ)],
                            [step(e + 1, v) for v in range(TURN)]))
        for v in range(TURN, NSEQ):
            step(E - 1, v, last=True)
        tail()

    def parts():
        return ((0, slice(0, CAP_S)), (1, slice(CAP_S, CAP)))

    with nc.Block() as block:

        @block.sync
        def _(sp):
            def last_piece(w, step):
                return AT_SEQ[w, STEP_AT[step] + STEP_CHUNKS[step] - 1] + 1

            def reload(e, step, of, prev):
                load_step(sp, s, e, step, lambda: sp.wait_ge(used, of * NSEQ + last_piece("w3", prev)),
                          lambda: sp.wait_ge(used, of * NSEQ + last_piece("w2", prev)))

            with sp.Fori(0, E - 1) as e:
                for step in range(SLOTS, NSTEP):
                    reload(e, step, e, step - SLOTS)
                for step in range(SLOTS):
                    reload(e + 1, step, e, step + NSTEP - SLOTS)
            for step in range(SLOTS, NSTEP):
                reload(E - 1, step, E - 1, step - SLOTS)

        @block.gpsimd
        def _(pool):
            def gather(e):
                nc.gpsimd.tensor_copy(ig, s.idxT[:, ds(e, 1)])
                nc.gpsimd.tensor_copy(igp, s.idxT[0:CAP_P, ds(e + PB, 1)]).then_inc(ixg, 1)
                hold(pool, turns, (ixg, e + 1))
                for dst, ix in ((xg, ig), (xgp, igp)):
                    nc.gpsimd.indirect_dma_start(dst, None, s.xn_d,
                                                 bass.IndirectOffsetOnAxis(ap=ix, axis=0))\
                        .then_inc(gath, 16)

            def scatter(e):
                nc.gpsimd.tensor_copy(iw, s.idxT[:, ds(e, 1)])
                nc.gpsimd.tensor_copy(iwp, s.idxT[0:CAP_P, ds(e + PB, 1)]).then_inc(ixw, 1)
                hold(pool, turns, (ixw, e + 1), (ye_a, e + 2), (ye_d, e + 2))
                for src, ix in ((ye, iw), (yep, iwp)):
                    nc.gpsimd.indirect_dma_start(s.acc_d, bass.IndirectOffsetOnAxis(ap=ix, axis=0),
                                                 src, None, compute_op=ALU.add).then_inc(scat, 16)
                pool.wait_ge(scat, e * 32 + 32)
                pool.sem_inc(rows_free, 1)

            pool.sem_inc(rows_free, 1)
            gather(0)
            with pool.Fori(0, E - 1) as e:
                hold(pool, turns, (xn_a, e * 2 + 2), (xn_d, e + 1))
                gather(e + 1)
                scatter(e)
            scatter(E - 1)

        @block.tensor
        def _(pe):
            def inputs(ks):
                for j, k in enumerate(ks):
                    o = j * CAP
                    nc.tensor.transpose(swap[:, o:o + CAP_S], xg[:, k * P:(k + 1) * P], K["ident"])
                    last = nc.tensor.transpose(swap[:, o + CAP_S:o + CAP], xgp[:, k * P:(k + 1) * P],
                                               K["ident"][0:CAP_P, 0:CAP_P])
                last.then_inc(swap_ps, 1)

            def results(r):
                for j in range(4):
                    m = 4 * (r % 2) + j
                    c = slice(0, CAP_S) if r < 2 else slice(CAP_S, CAP)
                    last = nc.tensor.transpose(swap[0:CAP_S if r < 2 else CAP_P, j * P:(j + 1) * P],
                                               yeT[:, m, c], K["ident"])
                last.then_inc(swap_ps, 1)

            def step(e, v, first=False, last=False):
                w, ch = SEQ[v]
                b = ch % NB
                if v == 0:
                    pe.wait_ge(xe_a, e + 1)
                    pe.wait_ge(xe_d, e + 1)
                if w == "w1":
                    if ch >= NB:
                        pe.wait_ge(h_r, e * NFC + (ch - NB + 1))
                    elif ch < NFC % NB and not first:
                        pe.wait_ge(h_r, e * NFC + (ch - NFC % NB + 1))
                if w == "w2":
                    pe.wait_ge(h_r, e * NFC + (ch + 1))
                    if ch == 0 and not first:
                        pe.wait_ge(y_a, e)
                        pe.wait_ge(y_d, e)
                st = STEP_OF[ch]
                if ch == STEP_AT[st] and w != "w3":
                    slot, turn = st % SLOTS, st // SLOTS
                    one, sm = (32, s.w13_in[slot]) if w == "w1" else (16, s.w2_in[slot])
                    pe.wait_ge(sm, e * (NSTEP // SLOTS * one) + (turn + 1) * one)
                for k in range(KC):
                    if w == "w2":
                        ins = nc.tensor.matmul(accps[k], piece(v)[:, k, :], hid[b],
                                               start=(ch == 0 and k % 3 == 0), stop=(ch == NFC - 1),
                                               skip_group_check=True)
                    else:
                        half = 0 if w == "w1" else 1
                        ins = nc.tensor.matmul(hps[b][:, half * CAP:(half + 1) * CAP],
                                               piece(v)[:, k, :], xe[:, k, :],
                                               start=(k == 0), stop=(k == KC - 1))
                ins.then_inc(used, 1)
                for r, (at, ks) in enumerate(IN):
                    if v == at and not last:
                        if r == 0:
                            pe.wait_ge(gath, e * 32 + 64)
                        pe.wait_ge(swap_free, swaps_in(e + 1) + r)
                        inputs(ks)
                for r, at in enumerate(OUT):
                    if v + NSEQ == at and not first:
                        if r == 0:
                            pe.wait_ge(y_a, e)
                            pe.wait_ge(y_d, e)
                        pe.wait_ge(swap_free, swaps_out(e - 1) + r)
                        results(r)

            def loop(body):
                with pe.Fori(0, E - 1) as e:
                    body(e)

            def tail():
                pe.wait_ge(y_a, E)
                pe.wait_ge(y_d, E)
                for r in range(NOUT):
                    pe.wait_ge(swap_free, SWAPS_LAST + r)
                    results(r)

            pe.wait_ge(gath, 32)
            for r, (_, ks) in enumerate(IN):
                if r:
                    pe.wait_ge(swap_free, r)
                inputs(ks)
            experts(loop, step, tail)

        def tasks_of(table):
            def step(e, v, first=False, last=False):
                for fn in table.get(v, ()):
                    fn(e, last)
                if not first:
                    for fn in table.get(v + NSEQ, ()):
                        fn(e - 1, False)

            def tail():
                for v in range(NSEQ, NSEQ + TURN):
                    for fn in table.get(v, ()):
                        fn(E - 1, True)
            return step, tail

        def at(table, v, fn):
            table.setdefault(v, []).append(fn)

        @block.scalar
        def _(act):
            table = {}

            def inputs(r):
                def fn(e, last):
                    if last:
                        return
                    fill(e + 1, r)
                return fn

            def fill(e, r, first=False):
                act.wait_ge(swap_ps, r + 1 if first else swaps_in(e) + (r + 1))
                if r == 0 and not first:
                    act.wait_ge(xe_a, e)
                    act.wait_ge(xe_d, e)
                for j, k in enumerate(IN[r][1]):
                    for g, c in parts():
                        o = slice(j * CAP + c.start, j * CAP + c.stop)
                        ins = nc.scalar.activation(xn[:, k, c], swap[:, o], ACT.Identity,
                                                   scale=s.A2[:, k, g:g + 1], bias=s.B2[:, k, g:g + 1])
                ins.then_inc(xn_a, 1)
                act.wait_ge(xn_a, r // 2 + 1 if first else e * 2 + (r // 2 + 1))
                act.sem_inc(swap_free, 1)

            def take(e, first=False):
                act.wait_ge(xn_a, e * 2 + 2)
                act.wait_ge(xn_d, e + 1)
                if not first:
                    act.wait_ge(used, e * NSEQ + (AT_SEQ["w3", NFC - 1] + 1 - NSEQ))
                nc.scalar.activation(xe[:, 0:4, :], xn[:, 0:4, :], ACT.Copy).then_inc(xe_a, 1)

            def sigmoid(ch):
                def fn(e, last):
                    act.wait_ge(used, e * NSEQ + (AT_SEQ["w3", ch] + 1))
                    nc.scalar.activation(sg[ch % NB], hps[ch % NB][:, 0:CAP], ACT.Sigmoid).then_inc(sg_r, 1)
                return fn

            def sums_out(e, last):
                act.wait_ge(used, e * NSEQ + NSEQ)
                for m in range(3):
                    for g, c in parts():
                        ins = nc.scalar.activation(yeT[:, m, c], accps[m][:, c], ACT.Copy,
                                                   scale=s.G2[:, m, g:g + 1])
                ins.then_inc(y_a, 1)

            def rows_out(r):
                def fn(e, last):
                    act.wait_ge(swap_ps, SWAPS_LAST + r + 1 if last else swaps_out(e) + (r + 1))
                    if r == 0:
                        act.wait_ge(gate_r, e + 1)
                        act.wait_ge(rows_free, e + 1)
                    ins = nc.scalar.activation(ye[:, r * 512:(r + 1) * 512], swap, ACT.Copy, scale=gt)
                    ins.then_inc(swap_free, 1)
                    if r == 1:
                        act.wait_ge(swap_free, SWAPS_LAST + 2 if last else swaps_out(e) + 2)
                        act.sem_inc(ye_a, 1)
                return fn

            for r in (0, 2):
                at(table, IN[r][0], inputs(r))
            for ch in range(NFC):
                at(table, AT_SEQ["w3", ch], sigmoid(ch))
            at(table, AT_SEQ["w3", NFC - 1], lambda e, last: None if last else take(e + 1))
            at(table, NSEQ - 1, sums_out)
            for r in (0, 1):
                at(table, OUT[r], rows_out(r))

            act.sem_inc(ye_a, 1)
            fill(0, 0, True)
            fill(0, 2, True)
            take(0, True)

            def loop(body):
                with act.Fori(0, E - 1) as e:
                    body(e)

            step, tail = tasks_of(table)
            experts(loop, step, tail)

        @block.vector
        def _(dve):
            own, table = Chain(dve, dvo), {}
            dve.sem_inc(ye_d, 1)

            def fill(e, first=False):
                if first:
                    dve.wait_ge(swap_ps, 2)
                else:
                    dve.wait_ge(swap_ps, swaps_in(e) + 2)
                    dve.wait_ge(xe_a, e)
                    dve.wait_ge(xe_d, e)
                for j, k in enumerate(IN[1][1]):
                    for g, c in parts():
                        o = slice(j * CAP + c.start, j * CAP + c.stop)
                        ins = nc.vector.tensor_scalar(xn[:, k, c], swap[:, o], s.A2[:, k, g:g + 1],
                                                      s.B2[:, k, g:g + 1], ALU.mult, ALU.add)
                ins.then_inc(xn_d, 1)
                dve.wait_ge(xn_d, e + 1)
                dve.sem_inc(swap_free, 1)

            def inputs(e, last):
                if not last:
                    fill(e + 1)

            def take(e, first=False):
                dve.wait_ge(xn_a, e * 2 + 2)
                dve.wait_ge(xn_d, e + 1)
                if not first:
                    dve.wait_ge(used, e * NSEQ + (AT_SEQ["w3", NFC - 1] + 1 - NSEQ))
                nc.vector.tensor_copy(xe[:, 4:KC, :], xn[:, 4:KC, :]).then_inc(xe_d, 1)

            def hidden(ch):
                def fn(e, last):
                    b = ch % NB
                    dve.wait_ge(sg_r, e * NFC + (ch + 1))
                    own.link(nc.vector.tensor_tensor(sg[b], sg[b], hps[b][:, 0:CAP], ALU.mult))
                    nc.vector.tensor_tensor(hid[b], sg[b], hps[b][:, CAP:2 * CAP], ALU.mult)\
                        .then_inc(h_r, 1)
                return fn

            def sums_out(e, last):
                dve.wait_ge(used, e * NSEQ + NSEQ)
                for m in range(3, KC):
                    for g, c in parts():
                        ins = nc.vector.tensor_scalar(yeT[:, m, c], accps[m][:, c],
                                                      s.G2[:, m, g:g + 1], None, ALU.mult)
                ins.then_inc(y_d, 1)

            def gates(e, last):
                dve.wait_ge(ye_a, e + 1)
                dve.wait_ge(ye_d, e + 1)
                nc.vector.tensor_copy(gt, s.gateT[:, ds(e, 1)])
                nc.vector.tensor_copy(gtp, s.gateT[0:CAP_P, ds(e + PB, 1)]).then_inc(gate_r, 1)

            def rows_out(r):
                def fn(e, last):
                    dve.wait_ge(swap_ps, SWAPS_LAST + r + 1 if last else swaps_out(e) + (r + 1))
                    if r == 2:
                        dve.wait_ge(gate_r, e + 1)
                        dve.wait_ge(rows_free, e + 1)
                    nc.vector.tensor_scalar(yep[:, (r - 2) * 512:(r - 1) * 512], swap[0:CAP_P, :], gtp, None,
                                            ALU.mult).then_inc(swap_free, 1)
                    if r == 3:
                        dve.wait_ge(swap_free, SWAPS_LAST + 4 if last else swaps_out(e) + 4)
                        dve.sem_inc(ye_d, 1)
                return fn

            at(table, IN[1][0], inputs)
            for ch in range(NFC):
                at(table, AT_SEQ["w3", ch], hidden(ch))
            at(table, AT_SEQ["w3", NFC - 1], lambda e, last: None if last else take(e + 1))
            at(table, NSEQ - 1, sums_out)
            at(table, NSEQ, gates)
            for r in (2, 3):
                at(table, OUT[r], rows_out(r))

            fill(0, True)
            take(0, True)

            def loop(body):
                looped(dve, own, 0, E - 1, NFC, body)

            step, tail = tasks_of(table)
            experts(loop, step, tail)



def phase_final(nc, s):
    a, M, sem = s.a, s.M, s.sem
    ar = Arena(M, s.n_main)
    gf = ar.get(D)
    G = 2
    NG = NT // G
    xt = [ar.get(G, D) for _ in range(NG)]
    yo = [ar.get(G, D) for _ in range(NG)]
    junk = [ar.get(D) for _ in (0, 1)]
    ssq, root, rstd = ar.get(NT), ar.get(NT), ar.get(NT)
    g_in = sem("final_g_in")
    x_in = [sem(f"rows_in{n}") for n in range(NG)]
    y_out = [sem(f"result_written{n}") for n in range(NG)]
    sq_r, ms_r, rt_r, rr_r, y_r = (sem("final_squared"), sem("final_mean_square"), sem("final_root"),
                                   sem("final_rstd"), sem("result_ready"))

    def tiles(dram, n):
        return dram[n * G * P:(n + 1) * G * P, :].rearrange("(g p) d -> p g d", p=P)

    with nc.Block() as block:

        @block.sync
        def _(sp):
            for n in range(NG):
                sp.dma_start(xt[n], tiles(s.acc_d, n)).then_inc(x_in[n], 16)
            sp.dma_start(gf, a["final_g"].to_broadcast([P, D])).then_inc(g_in, 16)
            for n in range(NG):
                sp.wait_ge(y_r, (n + 1) * G)
                sp.dma_start(tiles(a["out_y"], n), yo[n]).then_inc(y_out[n], 16)
            for n in range(NG):
                sp.wait_ge(y_out[n], 16)

        @block.scalar
        def _(act):
            for n in range(NT):
                if n % G == 0:
                    act.wait_ge(x_in[n // G], 16)
                if n >= 2:
                    act.wait_ge(sq_r, n - 1)
                nc.scalar.activation(junk[n % 2], xt[n // G][:, n % G, :], ACT.Square,
                                     accum_out=ssq[:, n:n + 1]).then_inc(sq_r, 1)
            act.wait_ge(ms_r, 1)
            nc.scalar.activation(root, ssq, ACT.Sqrt).then_inc(rt_r, 1)

        @block.vector
        def _(dve):
            dve.wait_ge(sq_r, NT)
            nc.vector.tensor_scalar(ssq, ssq, 1.0 / D, RMS_EPS, ALU.mult, ALU.add).then_inc(ms_r, 1)
            dve.wait_ge(rt_r, 1)
            nc.vector.reciprocal(rstd, root).then_inc(rr_r, 1)
            dve.wait_ge(rr_r, 1)
            dve.wait_ge(g_in, 16)
            for n in range(NT):
                nc.vector.scalar_tensor_tensor(out=yo[n // G][:, n % G, :], in0=xt[n // G][:, n % G, :],
                                               scalar=rstd[:, n:n + 1], in1=gf,
                                               op0=ALU.mult, op1=ALU.mult).then_inc(y_r, 1)


_OUT = (("out_y", (T, D)), ("out_state", (2, NH, HS, HS)))


def kernel(x_prompt, x_sample, state_wkv, c, c_ctx, norm1_g, norm2_g, w_mod, b_mod, w_in, conv_dw, conv_b,
           conv_ln_g, conv_ln_b, rwkv_w0, rwkv_w_up, rwkv_a0, rwkv_a_up, rwkv_g_up, rwkv_k_k, rwkv_k_a,
           rwkv_r_k, rwkv_gn_g, rwkv_gn_b, w_out, router, exp_w1, exp_w3, exp_w2, final_norm_g):
    import numpy as _np
    import concourse.bacc as _bacc
    from concourse import mybir as _mybir
    from concourse.bass_utils import run_bass_kernel_spmd as _run

    def columns(v):
        return _np.asarray(v).reshape(-1, P).T

    taps = _np.asarray(conv_dw)[0].reshape(KW, NP_, P).transpose(2, 1, 0).reshape(P, NP_ * KW)
    bias = _np.concatenate([columns(v) for d in (0, 1) for v in (rwkv_w0[0, d], rwkv_a0[0, d])], 1)
    cond = _np.stack([columns(c[0]), columns(c_ctx)], 2).reshape(P, 16)
    vectors = _np.concatenate([columns(norm1_g[0]), columns(norm2_g[0]), columns(b_mod[0]), taps,
                               columns(conv_b[0]), columns(conv_ln_g[0]), columns(conv_ln_b[0]), bias,
                               columns(rwkv_k_k[0]), columns(rwkv_k_a[0]), columns(rwkv_r_k[0].reshape(-1)),
                               columns(rwkv_gn_g[0]), columns(rwkv_gn_b[0]), cond], 1)
    arrays = {
        "x": _np.concatenate([_np.asarray(x_sample)[0], _np.asarray(x_prompt)[0]], 0),
        "vectors": vectors, "table": _np.concatenate(list(constant_table().values()), 1),
        "w_mod": w_mod[0], "w_in": w_in[0], "w_up": rwkv_w_up[0], "a_up": rwkv_a_up[0],
        "g_up": rwkv_g_up[0], "state": state_wkv[0, 0], "w_out": w_out[0], "router": router[0],
        "w1": exp_w1[0], "w3": exp_w3[0], "w2": exp_w2[0],
        "final_g": _np.asarray(final_norm_g).reshape(1, D),
    }
    nc = _bacc.Bacc("TRN2", target_bir_lowering=False, num_devices=1)
    f32 = _mybir.dt.float32
    data, a = {}, {}
    for name, v in arrays.items():
        data[f"in_{name}"] = _np.ascontiguousarray(v)
        a[name] = nc.dram_tensor(f"in_{name}", data[f"in_{name}"].shape, f32, kind="ExternalInput").ap()
    for name, shape in _OUT:
        a[name] = nc.dram_tensor(name, shape, f32, kind="ExternalOutput").ap()
    build(nc, a)
    r = _run(nc, [data], core_ids=[0]).results[0]
    y, state = r["out_y"], r["out_state"]
    return y[None, TS:], y[None, :TS], state[None, None]
```
